# Optimizing a Trainium2 kernel written in Bass

```python
import jax, jax.numpy as jnp
from jax import lax
import numpy as np

D_MODEL = 1024
BATCH = 1
SEQ = 256
DEPTH = 2

N_HEADS = 8
N_KV_HEADS = 2
HEAD_DIM = 64
ATTN_WIDTH = N_HEADS * HEAD_DIM
KV_WIDTH = N_KV_HEADS * HEAD_DIM
WINDOW = 128
ROT_DIM = HEAD_DIM // 4
ROPE_THETA = 500000.0
HGRN_HEADS = 4
HGRN_HEAD_DIM = 128
HGRN_WIDTH = HGRN_HEADS * HGRN_HEAD_DIM
CHUNK = 64
NORM_EPS = 1e-6
MASK_VALUE = -1e30
SPLITS = (ATTN_WIDTH, KV_WIDTH, KV_WIDTH, ATTN_WIDTH,
          HGRN_WIDTH, HGRN_WIDTH, HGRN_WIDTH, HGRN_WIDTH,
          D_MODEL, D_MODEL)
IN_WIDTH = 2 * ATTN_WIDTH + 2 * KV_WIDTH + 4 * HGRN_WIDTH + 2 * D_MODEL


def rms_norm(x, w):
    xf = x.astype(jnp.float32)
    y = xf * lax.rsqrt(jnp.mean(xf * xf, axis=-1, keepdims=True) + NORM_EPS)
    return (y * w.astype(jnp.float32)).astype(x.dtype)

def partial_rope(x, positions):
    half = ROT_DIM // 2
    inv_freq = jnp.power(ROPE_THETA, -jnp.arange(half, dtype=jnp.float32) * (2.0 / ROT_DIM))
    ang = positions.astype(jnp.float32)[..., None] * inv_freq
    cos = jnp.cos(ang)[:, :, None, :]
    sin = jnp.sin(ang)[:, :, None, :]
    xr = x[..., :ROT_DIM].astype(jnp.float32)
    x1, x2 = xr[..., :half], xr[..., half:]
    rot = jnp.concatenate([x1 * cos - x2 * sin, x2 * cos + x1 * sin], axis=-1)
    return jnp.concatenate([rot.astype(x.dtype), x[..., ROT_DIM:]], axis=-1)

def sliding_window_attention(q, k, v, sinks):
    B, T = q.shape[0], q.shape[1]
    nb = T // WINDOW
    G = N_HEADS // N_KV_HEADS
    qb = q.astype(jnp.float32).reshape(B, nb, WINDOW, N_KV_HEADS, G, HEAD_DIM) * (HEAD_DIM ** -0.5)

    def band(a):
        a = a.astype(jnp.float32).reshape(B, nb, WINDOW, N_KV_HEADS, HEAD_DIM)
        prev = jnp.pad(a[:, :-1], ((0, 0), (1, 0), (0, 0), (0, 0), (0, 0)))
        return jnp.concatenate([prev, a], axis=2)

    kb, vb = band(k), band(v)
    blk = jnp.arange(nb)[:, None]
    qpos = blk * WINDOW + jnp.arange(WINDOW)[None, :]
    kpos = (blk - 1) * WINDOW + jnp.arange(2 * WINDOW)[None, :]
    delta = qpos[:, :, None] - kpos[:, None, :]
    mask = (delta >= 0) & (delta < WINDOW) & (kpos[:, None, :] >= 0)
    s = jnp.einsum('bnqhgd,bnkhd->bhgnqk', qb, kb)
    s = jnp.where(mask, s, MASK_VALUE)
    sink = sinks.astype(jnp.float32).reshape(N_KV_HEADS, G)[None, :, :, None, None, None]
    m = jnp.maximum(jnp.max(s, axis=-1, keepdims=True), sink)
    p = jnp.exp(s - m)
    p = p / (jnp.sum(p, axis=-1, keepdims=True) + jnp.exp(sink - m))
    o = jnp.einsum('bhgnqk,bnkhd->bnqhgd', p, vb)
    return o.reshape(B, T, ATTN_WIDTH)

def hgrn2_recurrence(q, k, v, logf):
    B, T, H, Dk = q.shape
    Dv = v.shape[-1]
    n = T // CHUNK

    def chunks(a):
        return a.reshape(B, n, CHUNK, H, a.shape[-1]).transpose(1, 0, 3, 2, 4)

    causal = jnp.tril(jnp.ones((CHUNK, CHUNK), dtype=bool))[:, :, None]

    def step(S, blk):
        qc, kc, vc, gc = blk
        G = jnp.cumsum(gc, axis=-2)
        diff = G[:, :, :, None, :] - G[:, :, None, :, :]
        decay = jnp.exp(jnp.where(causal, diff, MASK_VALUE))
        scores = jnp.einsum('bhtd,bhsd,bhtsd->bhts', qc, kc, decay)
        o = (jnp.einsum('bhts,bhsv->bhtv', scores, vc)
             + jnp.einsum('bhtd,bhdv->bhtv', qc * jnp.exp(G), S))
        G_end = G[:, :, -1:, :]
        S = (S * jnp.exp(G_end)[:, :, 0, :, None]
             + jnp.einsum('bhsd,bhsv->bhdv', kc * jnp.exp(G_end - G), vc))
        return S, o

    S0 = jnp.zeros((B, H, Dk, Dv), jnp.float32)
    _, o = lax.scan(step, S0, (chunks(q), chunks(k), chunks(v), chunks(logf)))
    return o.transpose(1, 0, 3, 2, 4).reshape(B, T, H, Dv)

def first_inputs(seed: int = 0) -> dict:
    key = jax.random.key(seed)
    ks = jax.random.split(key, 12)
    f32 = jnp.float32
    x = jax.random.normal(ks[0], (BATCH, SEQ, D_MODEL), f32)
    offsets = jax.random.randint(ks[1], (BATCH, 1), 0, 1024, dtype=jnp.int32)
    positions = (jnp.arange(SEQ, dtype=jnp.int32)[None, :] + offsets).astype(jnp.int32)
    norm_w = 1.0 + 0.02 * jax.random.normal(ks[2], (DEPTH, D_MODEL), f32)
    w_in = jax.random.normal(ks[3], (DEPTH, D_MODEL, IN_WIDTH), f32) * D_MODEL ** -0.5
    attn_sinks = 0.5 * jax.random.normal(ks[4], (DEPTH, N_HEADS), f32)
    hgrn_norm_w = 1.0 + 0.02 * jax.random.normal(ks[5], (DEPTH, HGRN_HEAD_DIM), f32)
    w_up_attn = jax.random.normal(ks[6], (DEPTH, ATTN_WIDTH, D_MODEL), f32) * ATTN_WIDTH ** -0.5
    w_up_hgrn = jax.random.normal(ks[7], (DEPTH, HGRN_WIDTH, D_MODEL), f32) * HGRN_WIDTH ** -0.5
    w_out = jax.random.normal(ks[8], (DEPTH, D_MODEL, D_MODEL), f32) * D_MODEL ** -0.5
    lb_logits = 0.1 * jax.random.normal(ks[9], (DEPTH, HGRN_WIDTH), f32)
    final_norm_w = 1.0 + 0.02 * jax.random.normal(ks[10], (D_MODEL,), f32)
    return {'x': x, 'positions': positions, 'norm_w': norm_w, 'w_in': w_in,
            'attn_sinks': attn_sinks, 'hgrn_norm_w': hgrn_norm_w, 'w_up_attn': w_up_attn,
            'w_up_hgrn': w_up_hgrn, 'w_out': w_out, 'lb_logits': lb_logits,
            'final_norm_w': final_norm_w}

def first_block(x, positions, norm_w, w_in, attn_sinks, hgrn_norm_w, w_up_attn, w_up_hgrn,
              w_out, lb_logits, final_norm_w):
    B, T, _ = x.shape
    split_points = [int(s) for s in np.cumsum(SPLITS)[:-1]]
    lb_soft = jax.nn.softmax(lb_logits.astype(jnp.float32), axis=0)
    lb_all = jnp.cumsum(lb_soft, axis=0) - lb_soft[0]

    for layer in range(DEPTH):
        h = rms_norm(x, norm_w[layer])
        proj = h @ w_in[layer]
        (q, k, v, z_attn, q_h, f_h, i_h, g_h, gate_attn, gate_hgrn) = jnp.split(proj, split_points, axis=-1)

        q = partial_rope(q.reshape(B, T, N_HEADS, HEAD_DIM), positions)
        k = partial_rope(k.reshape(B, T, N_KV_HEADS, HEAD_DIM), positions)
        v = v.reshape(B, T, N_KV_HEADS, HEAD_DIM)
        a = sliding_window_attention(q, k, v, attn_sinks[layer]).astype(x.dtype) * jax.nn.silu(z_attn)

        lb = lb_all[layer]
        fx = f_h.astype(jnp.float32)
        logf = jnp.log(lb + (1.0 - lb) * jax.nn.sigmoid(fx))
        kin = (1.0 - lb) * jax.nn.sigmoid(-fx)
        qin = jax.nn.silu(q_h.astype(jnp.float32))
        heads = lambda t: t.reshape(B, T, HGRN_HEADS, HGRN_HEAD_DIM)
        o = hgrn2_recurrence(heads(qin), heads(kin), heads(i_h.astype(jnp.float32)), heads(logf))
        o = o * lax.rsqrt(jnp.mean(o * o, axis=-1, keepdims=True) + NORM_EPS) * hgrn_norm_w[layer].astype(jnp.float32)
        b = o.reshape(B, T, HGRN_WIDTH).astype(x.dtype) * jax.nn.silu(g_h)

        merged = (jax.nn.sigmoid(gate_attn) * (a @ w_up_attn[layer])
                  + jax.nn.sigmoid(gate_hgrn) * (b @ w_up_hgrn[layer]))
        x = x + merged @ w_out[layer]

    return rms_norm(x, final_norm_w)


DEPTH_2 = 1

N_ATT_HEADS = 8
ATT_WIDTH = N_ATT_HEADS * HEAD_DIM
Q_BLOCK = 128
CONV_WIDTH = 512
CONV_K = 3
N_GROUPS = 4
EXPERTS_PER_GROUP = 4
N_EXPERTS = N_GROUPS * EXPERTS_PER_GROUP
TOP_K_IN_GROUP = 2
D_EXPERT = 256
PLE_DIM = 256
EPS = 1e-6
NEG_INF = -1e30

PROJ_SIZES = (ATT_WIDTH, ATT_WIDTH, ATT_WIDTH, N_ATT_HEADS,
              CONV_WIDTH, CONV_WIDTH, CONV_WIDTH, D_MODEL, D_MODEL)
PROJ_WIDTH = 3 * ATT_WIDTH + N_ATT_HEADS + 3 * CONV_WIDTH + 2 * D_MODEL


def rms_norm_2(x, g):
    xf = x.astype(jnp.float32)
    y = xf * lax.rsqrt(jnp.mean(xf * xf, axis=-1, keepdims=True) + EPS)
    return (y * g.astype(jnp.float32)).astype(x.dtype)

def split_offsets():
    offs, acc = [], 0
    for s in PROJ_SIZES[:-1]:
        acc += s
        offs.append(acc)
    return offs

def forgetting_attention(q, k, v, log_f):
    b, s, h, d = q.shape
    n_blocks = s // Q_BLOCK
    c = jnp.cumsum(log_f, axis=1).transpose(0, 2, 1)
    qh = q.transpose(0, 2, 1, 3)
    kh = k.transpose(0, 2, 1, 3)
    vh = v.transpose(0, 2, 1, 3)
    q_blocks = jnp.moveaxis(qh.reshape(b, h, n_blocks, Q_BLOCK, d), 2, 0)
    c_blocks = jnp.moveaxis(c.reshape(b, h, n_blocks, Q_BLOCK), 2, 0)
    key_pos = jnp.arange(s)
    scale = HEAD_DIM ** -0.5

    def one_block(args):
        qb, cqb, blk = args
        q_pos = blk * Q_BLOCK + jnp.arange(Q_BLOCK)
        logits = jnp.einsum('bhqd,bhkd->bhqk', qb, kh).astype(jnp.float32) * scale
        logits = logits + (cqb[..., :, None] - c[..., None, :])
        causal = key_pos[None, :] <= q_pos[:, None]
        logits = jnp.where(causal, logits, NEG_INF)
        probs = jax.nn.softmax(logits, axis=-1)
        return jnp.einsum('bhqk,bhkd->bhqd', probs.astype(vh.dtype), vh)

    out = lax.map(one_block, (q_blocks, c_blocks, jnp.arange(n_blocks)))
    out = out.transpose(1, 0, 3, 2, 4).reshape(b, s, h * d)
    return out

def causal_short_conv(u, w):
    s = u.shape[1]
    u_pad = jnp.pad(u, ((0, 0), (CONV_K - 1, 0), (0, 0)))
    y = w[0] * u_pad[:, 0:s]
    for j in range(1, CONV_K):
        y = y + w[j] * u_pad[:, j:j + s]
    return y

def hierarchical_moe(h, w_rg, b_rg, w_re, b_re, w_gate, w_up, w_down):
    b, s, d = h.shape
    ht = h.reshape(b * s, d)
    g_logits = (ht @ w_rg + b_rg).astype(jnp.float32)
    g_prob = jax.nn.softmax(g_logits, axis=-1)
    g_val, g_idx = lax.top_k(g_prob, 1)
    e_logits = (ht @ w_re + b_re).astype(jnp.float32)
    e_logits = e_logits.reshape(-1, N_GROUPS, EXPERTS_PER_GROUP)
    e_in = jnp.take_along_axis(e_logits, g_idx[:, :, None], axis=1)[:, 0]
    e_prob = jax.nn.softmax(e_in, axis=-1)
    e_val, e_idx = lax.top_k(e_prob, TOP_K_IN_GROUP)
    e_val = e_val / jnp.sum(e_val, axis=-1, keepdims=True)
    gate = g_val * e_val
    global_idx = g_idx * EXPERTS_PER_GROUP + e_idx
    combine = jnp.sum(jax.nn.one_hot(global_idx, N_EXPERTS, dtype=jnp.float32)
                      * gate[..., None], axis=1)
    a = jnp.einsum('td,edf->tef', ht, w_gate)
    u = jnp.einsum('td,edf->tef', ht, w_up)
    hid = jax.nn.silu(a) * u * combine[..., None].astype(ht.dtype)
    out = jnp.einsum('tef,efd->td', hid, w_down)
    return out.reshape(b, s, d)

def second_inputs(seed: int = 0) -> dict:
    key = jax.random.key(seed)
    ks = jax.random.split(key, 24)
    L, D = DEPTH_2, D_MODEL
    f32 = jnp.float32

    def nrm(k, shape, scale):
        return jax.random.normal(k, shape, f32) * scale

    def gain(k, shape):
        return 1.0 + 0.05 * jax.random.normal(k, shape, f32)

    return {
        "x": nrm(ks[0], (BATCH, SEQ, D), 1.0),
        "p": nrm(ks[1], (DEPTH_2, BATCH, SEQ, PLE_DIM), 1.0),
        "attn_norm_g": gain(ks[2], (L, D)),
        "w_in": nrm(ks[3], (L, D, PROJ_WIDTH), D ** -0.5),
        "b_f": 1.0 + 3.0 * jax.random.uniform(ks[4], (L, N_ATT_HEADS), f32),
        "q_norm_g": gain(ks[5], (L, HEAD_DIM)),
        "k_norm_g": gain(ks[6], (L, HEAD_DIM)),
        "conv_w": nrm(ks[7], (L, CONV_K, CONV_WIDTH), CONV_K ** -0.5),
        "w_out_att": nrm(ks[8], (L, ATT_WIDTH, D), ATT_WIDTH ** -0.5),
        "w_out_conv": nrm(ks[9], (L, CONV_WIDTH, D), CONV_WIDTH ** -0.5),
        "w_o": nrm(ks[10], (L, D, D), D ** -0.5),
        "ffn_norm_g": gain(ks[11], (L, D)),
        "w_rg": nrm(ks[12], (L, D, N_GROUPS), D ** -0.5),
        "b_rg": nrm(ks[13], (L, N_GROUPS), 0.01),
        "w_re": nrm(ks[14], (L, D, N_EXPERTS), D ** -0.5),
        "b_re": nrm(ks[15], (L, N_EXPERTS), 0.01),
        "w_gate": nrm(ks[16], (L, N_EXPERTS, D, D_EXPERT), D ** -0.5),
        "w_up": nrm(ks[17], (L, N_EXPERTS, D, D_EXPERT), D ** -0.5),
        "w_down": nrm(ks[18], (L, N_EXPERTS, D_EXPERT, D), D_EXPERT ** -0.5),
        "ple_norm_g": gain(ks[19], (L, D)),
        "w_pg": nrm(ks[20], (L, D, D), D ** -0.5),
        "w_ple": nrm(ks[21], (L, PLE_DIM, D), PLE_DIM ** -0.5),
    }

def second_block(x, p, attn_norm_g, w_in, b_f, q_norm_g, k_norm_g, conv_w, w_out_att,
              w_out_conv, w_o, ffn_norm_g, w_rg, b_rg, w_re, b_re, w_gate, w_up, w_down,
              ple_norm_g, w_pg, w_ple):
    b, s, _ = x.shape
    offs = split_offsets()
    for i in range(DEPTH_2):
        h = rms_norm_2(x, attn_norm_g[i])
        proj = h @ w_in[i]
        q, k, v, f_logit, cb, cc, cu, ga, gb = jnp.split(proj, offs, axis=-1)

        q = rms_norm_2(q.reshape(b, s, N_ATT_HEADS, HEAD_DIM), q_norm_g[i])
        k = rms_norm_2(k.reshape(b, s, N_ATT_HEADS, HEAD_DIM), k_norm_g[i])
        v = v.reshape(b, s, N_ATT_HEADS, HEAD_DIM)
        log_f = jax.nn.log_sigmoid(f_logit.astype(jnp.float32) + b_f[i].astype(jnp.float32))
        y_att = forgetting_attention(q, k, v, log_f)

        y_conv = cb * causal_short_conv(cc * cu, conv_w[i])

        merged = (jax.nn.sigmoid(ga) * (y_att @ w_out_att[i])
                  + jax.nn.sigmoid(gb) * (y_conv @ w_out_conv[i]))
        x = x + merged @ w_o[i]

        h2 = rms_norm_2(x, ffn_norm_g[i])
        x = x + hierarchical_moe(h2, w_rg[i], b_rg[i], w_re[i], b_re[i],
                                 w_gate[i], w_up[i], w_down[i])

        h3 = rms_norm_2(x, ple_norm_g[i])
        x = x + jax.nn.sigmoid(h3 @ w_pg[i]) * (p[i] @ w_ple[i])
    return x


def setup_inputs(seed=0):
    out = dict(first_inputs(seed))
    for name, value in second_inputs(seed + 1).items():
        if name != "x":
            out[name + "_2"] = value
    return out


def reference(
    x, positions, norm_w, w_in, attn_sinks, hgrn_norm_w, w_up_attn, w_up_hgrn, w_out, lb_logits,
    final_norm_w, p_2, attn_norm_g_2, w_in_2, b_f_2, q_norm_g_2, k_norm_g_2, conv_w_2,
    w_out_att_2, w_out_conv_2, w_o_2, ffn_norm_g_2, w_rg_2, b_rg_2, w_re_2, b_re_2, w_gate_2,
    w_up_2, w_down_2, ple_norm_g_2, w_pg_2, w_ple_2,
):
    x = first_block(
        x, positions, norm_w, w_in, attn_sinks, hgrn_norm_w, w_up_attn, w_up_hgrn, w_out,
        lb_logits, final_norm_w,
    )
    return second_block(
        x, p_2, attn_norm_g_2, w_in_2, b_f_2, q_norm_g_2, k_norm_g_2, conv_w_2, w_out_att_2,
        w_out_conv_2, w_o_2, ffn_norm_g_2, w_rg_2, b_rg_2, w_re_2, b_re_2, w_gate_2, w_up_2,
        w_down_2, ple_norm_g_2, w_pg_2, w_ple_2,
    )


_drawn_inputs = setup_inputs


def setup_inputs(seed=0):
    import zlib

    import numpy as np

    out = dict(_drawn_inputs(seed))
    spreads = {}
    factors = {'attn_sinks': 8.0,
     'lb_logits': 6.515,
     'q_norm_g_2': 3.968,
     'k_norm_g_2': 4.785,
     'b_rg_2': 3.176,
     'b_re_2': 21.435,
     'ple_norm_g_2': 6.364}
    for name, (base, spread) in spreads.items():
        noise = np.random.default_rng([zlib.crc32(name.encode()), seed]).standard_normal(out[name].shape)
        drawn = base * np.exp(spread * noise) if base else spread * noise
        out[name] = __import__('jax').numpy.asarray(drawn.astype(out[name].dtype))
    for name, factor in factors.items():
        out[name] = (out[name] * factor).astype(out[name].dtype)
    return out
```

```python
from contextlib import ExitStack

import numpy as np
import concourse.bass as bass
from concourse import mybir

F32 = mybir.dt.float32
F32R = mybir.dt.float32r
I32 = mybir.dt.int32
U8 = mybir.dt.uint8
ALU = mybir.AluOpType
ACT = mybir.ActivationFunctionType
AX = mybir.AxisListType.X

P = 128
TT = 2
D = 1024
KT = D // P
W = 512
RING = 3
EPS = 1e-6
MASKED = -1e30
WINDOW_LEVELS = [1, 2, 4, 8, 16, 32, 64, 128]
LEVELS = 7
GATE_FLOOR = -43.0

B1_COLS = dict(fh=1792, qh=1280, vh=2304, q=0, kv=512, z=768, g=2816, ga0=3328, ga1=3840, gb0=4352, gb1=4864)


def group_tiles(matrix, col, width, row_tiles):
    return [(matrix, k, 4, col, width) for k in range(0, row_tiles, 4)]


B1_TILES = []
for _name, _col in B1_COLS.items():
    B1_TILES += group_tiles("w_in", _col, 256 if _name == "kv" else W, KT)
for _m in ("w_up_attn", "w_up_hgrn"):
    B1_TILES += group_tiles(_m, 0, W, 4) + group_tiles(_m, W, W, 4)
B1_TILES += group_tiles("w_out", 0, W, KT) + group_tiles("w_out", W, W, KT)
NT1 = len(B1_TILES)
assert NT1 % RING == 0

B2_COLS = dict(q=0, k=512, v=1024, cc=2056, cu=2568, cb=1544, ga0=3080, ga1=3592, gb0=4104, gb1=4616)
B2_TILES = []
for _name, _col in B2_COLS.items():
    B2_TILES += group_tiles("w_in_2", _col, W, KT)
for _m in ("w_out_conv_2", "w_out_att_2"):
    B2_TILES += group_tiles(_m, 0, W, 4) + group_tiles(_m, W, W, 4)
B2_TILES += group_tiles("w_o_2", 0, W, KT) + group_tiles("w_o_2", W, W, KT)
NT2 = len(B2_TILES)
T2 = 2 * NT1
TM = T2 + NT2
EXPERTS = 16
NTM = 3 * EXPERTS
TP = TM + NTM

JOBS1 = ["N0", "N1", "F", "QH", "L0", "L1", "L2", "L3", "L4", "QT", "KT", "L5", "S0", "L6", "S1",
         "L7", "P0", "L8", "V0", "S2", "P1", "OH", "V1", "P2", "V2", "BT", "AT", "M0", "M1"]
JOBS2 = ["N0", "N1", "FL", "CT", "QT", "KT", "S0", "S1", "P0", "V0", "S2", "P1", "V1", "P2", "V2", "UT", "CB",
         "AT", "PT", "M0", "M1", "R0", "R1", "RL"]
GROUPS1 = list(B1_COLS) + ["a0", "a1", "b0", "b1", "o0", "o1"]
GROUPS2 = list(B2_COLS) + ["b0", "b1", "a0", "a1", "o0", "o1"]


class Turns:

    def __init__(self, names, base):
        self.names = names
        self.base = base
        self.per = [(len(names) + 1) // 2, len(names) // 2]

    def turn(self, name, layer=0):
        i = self.names.index(name)
        return i % 2, layer * self.per[i % 2] + self.base[i % 2] + i // 2 + 1


def last_tiles(names, tiles, first):
    at, out = first, {}
    for name in names:
        at += 1 if name[0] in "ab" and name[1:] in ("0", "1") else 2
        out[name] = at - 1
    assert at == first + len(tiles)
    return out


AUX1 = Turns(JOBS1, [0, 0])
AUX2 = Turns(JOBS2, [2 * n for n in AUX1.per])
MM1 = Turns(GROUPS1, [0, 0])
MM2 = Turns(GROUPS2, [2 * n for n in MM1.per])
LAST1 = last_tiles(GROUPS1, B1_TILES, 0)
LAST2 = last_tiles(GROUPS2, B2_TILES, T2)
AUXM = [AUX2.base[p] + AUX2.per[p] for p in range(2)]
MMM = [MM2.base[p] + MM2.per[p] for p in range(2)]
AUXP = [AUXM[0] + EXPERTS, AUXM[1] + EXPERTS]

COLS = ["norm_w", "lb", "hgrn", "attn_norm", "ffn_norm", "ple_norm", "conv", "q_gain", "k_gain"]
COL_COUNT = dict(norm_w=2 * KT, lb=2 * 4, hgrn=2, attn_norm=KT, ffn_norm=KT, ple_norm=KT, conv=3 * 4, q_gain=1, k_gain=1)
COL_AT, _n = {}, 0
for _c in COLS:
    COL_AT[_c] = _n
    _n += COL_COUNT[_c]
N_COLS = _n
LAYER_COLS = KT + 4 + 4 + 1 + 8

EARLY = 2


def build(nc, A, out):
    ctx = ExitStack()
    with ctx:
        def sb(name, shape, dt=F32):
            return ctx.enter_context(nc.sbuf_tensor("sb_" + name, shape, dt))

        def sem(name):
            return ctx.enter_context(nc.semaphore(name))

        raw = sb("raw", [P, RING, 2048])
        w_hi = sb("w_hi", [P, RING, 2048], F32R)
        w_lo = sb("w_lo", [P, RING, 2048], F32R)
        x = sb("x", [P, TT, D])
        xm = sb("xm", [P, TT * D])
        xm3 = xm[:, :].rearrange("p (t d) -> p t d", t=TT)
        hT_hi = sb("hT_hi", [P, KT, TT * P], F32R)
        hT_lo = sb("hT_lo", [P, KT, TT * P], F32R)
        aT_hi = sb("aT_hi", [P, 4, TT * P], F32R)
        aT_lo = sb("aT_lo", [P, 4, TT * P], F32R)
        bT_hi = sb("bT_hi", [P, 4, TT * P], F32R)
        bT_lo = sb("bT_lo", [P, 4, TT * P], F32R)
        ga = sb("ga", [P, TT, D])
        gb = sb("gb", [P, TT, D])
        z = sb("z", [P, TT, W])
        g = sb("g", [P, TT, W])
        qk = sb("qk", [P, TT, 10, 64])
        a_tok = sb("a_tok", [P, TT, W])
        v_sb = sb("v_sb", [P, TT, P])
        vh = sb("vh", [P, TT, W])
        qTh = sb("qTh", [P, 1024])
        kTh = sb("kTh", [P, 1024])
        pre = sb("pre", [P, 1024])
        acc = sb("acc", [P, 1024])
        sc128 = sb("sc128", [P, 512])
        qTp = sb("qTp", [P, 1024])
        kT = sb("kT", [P, 256])
        s_ring = sb("s_ring", [P, 2, 1024])
        pT = sb("pT", [P, 1024])
        ident = sb("ident", [P, P])
        amask = sb("amask", [P, 4, P])
        lmask = sb("lmask", [P, LEVELS + 1, P], U8)
        segment = sb("segment", [P, 256])
        cols = sb("cols", [P, N_COLS])
        colrows = s_ring[0:N_COLS, 0, 0:P]
        lcols_all = sb("lcols_all", [P, 2, LAYER_COLS])
        lcols = sb("lcols", [P, LAYER_COLS])
        rope = sb("rope", [P, 2, TT, 8])
        rope_t = sb("rope_t", [P, 6, TT, 8])
        pos_i = sb("pos_i", [P, TT], I32)
        st = sb("st", [P, 64])
        hst = sb("hst", [P, 32])
        ast = sb("ast", [P, 5, 16])
        rt = sb("rt", [P, 4, TT, 10, 8])
        wf = sb("wf", [P, KT, 8])
        wr = sb("wr", [P, KT, 20])
        wf_hi = sb("wf_hi", [P, KT, 8], F32R)
        wf_lo = sb("wf_lo", [P, KT, 8], F32R)
        wr_hi = sb("wr_hi", [P, KT, 20], F32R)
        wr_lo = sb("wr_lo", [P, KT, 20], F32R)
        bias = sb("bias", [P, 28])
        lf = sb("lf", [P, 3, TT, 8])
        cT = sb("cT", [P, 256])
        lfw = sb("lfw", [P, TT, P])
        combine = sb("combine", [P, TT, EXPERTS])
        cnow = sb("cnow", [P, TT, 2])
        one = sb("one", [P, 4])

        E = [xm[:, 0:1024], xm[:, 1024:2048]]
        logf = s_ring[:, 0, :]
        fT = s_ring[:, 1, :]
        b_tok = qTh
        moe = pT[:, 0:12 * TT * 20].rearrange("p (a t n) -> p a t n", a=12, t=TT)
        iota_t = vh[:, 0, 0:P].bitcast(I32)
        iota_s = vh[:, 0, P:2 * P].bitcast(I32)
        blk = [vh[:, 1, i * P:(i + 1) * P].bitcast(I32) for i in range(4)]
        fw = gb[:, 0, :]
        selneg = acc[:, :]
        tri = sc128[:, 0:256]
        uT = xm[:, 0:4 * 258].rearrange("p (c t) -> p c t", c=4)
        kT2 = pre
        k2 = kTh
        p_tok = g[:, :, 0:256]
        pl = gb
        sil = z[:, :, :].rearrange("p t (e n) -> p e t n", e=2)
        hid = g[:, :, :].rearrange("p t (e n) -> p e t n", e=2)

        mm = [ctx.enter_context(nc.psum_tensor(f"mm{i}", [P, 1024], F32)) for i in range(2)]
        aux = [ctx.enter_context(nc.psum_tensor(f"aux{i}", [P, 1024], F32)) for i in range(2)]

        raw_loaded = [sem(f"raw_loaded{i}") for i in range(RING)]
        hi_split, lo_split, tile_done = sem("hi_split"), sem("lo_split"), sem("tile_done")
        mm_free = [sem(f"mm_free{i}") for i in range(2)]
        aux_ready = [sem(f"aux_ready{i}") for i in range(2)]
        aux_free = [sem(f"aux_free{i}") for i in range(2)]
        in_x, in_rows, in_small, in_fw, in_p = (sem(n) for n in ("in_x", "in_rows", "in_small", "in_fw", "in_p"))
        x_ready, std_ready, src_ready = sem("x_ready"), sem("std_ready"), sem("src_ready")
        hT_hi_ready, hT_lo_ready = sem("hT_hi_ready"), sem("hT_lo_ready")
        names = ("ident_ready", "iota_ready", "amask_ready", "cols_ready", "setup_pe", "lb_in", "lb_exp",
                 "rope_in", "rope_sin", "layer_cols",
                 "ftok_ready", "qhtok_ready", "fT_ready", "sig_ready", "log_ready", "kTh_ready", "qTh_ready",
                 "vh_ready", "D_ready", "E_ready", "W_ready", "acc_ready", "sc128_ready",
                 "qk_ready", "v_ready", "qT_ready", "kT_ready", "S_ready", "p_ready", "sinkexp_in",
                 "sinkexp_ready", "pT_ready", "z_ready", "g_ready", "gate_ready", "osq_ready", "oss_ready",
                 "ostd_ready", "b_ready", "bT_hi_ready", "bT_lo_ready", "a_ready", "aT_hi_ready", "aT_lo_ready",
                 "wf_hi_ready", "wf_lo_ready", "lf_in", "lf_exp", "lf_ready", "cT_ready", "qsq_ready", "qss_ready",
                 "qstd_ready", "q2_ready", "cc_ready", "u_ready", "cb_ready", "uT_ready", "y_ready", "gain_ready",
                 "pT_lo_ready", "logit_ready", "prob_ready", "sil_ready", "eT_hi_ready",
                 "pl_ready", "pg_ready", "final_ready", "out_done", "selneg_ready", "tri_ready", "lmask_ready", "mask_chain", "level_seen", "load_begun",
                 "dve_chain", "act_chain", "pool_chain")
        S = {n: sem(n) for n in names}

        block = ctx.enter_context(nc.Block())

        def tile_width(tile):
            return tile[2] * tile[4]

        def slot(t):
            return t % RING

        @block.sync
        def _(sp):
            def load(t, halves, sofar):
                sp.wait_ge(hi_split, sofar + 1)
                sp.wait_ge(lo_split, sofar + 1)
                sp.sem_inc(S["load_begun"], 1)
                for dst, src in halves:
                    sp.dma_start(dst, src).then_inc(raw_loaded[slot(t)], 32 // len(halves))

            def halves(t, tile, layer=None):
                matrix, k0, nk, col, width = tile
                w = A[matrix] if layer is None else A[matrix][layer]
                src = w[k0 * P:(k0 + nk) * P, col:col + width].rearrange("(k p) n -> p k n", p=P)
                dst = raw[:, slot(t), 0:nk * width].rearrange("p (k n) -> p k n", n=width)
                return [(dst[:, 0:nk // 2], src[:, 0:nk // 2]), (dst[:, nk // 2:nk], src[:, nk // 2:nk])]

            def expert_halves(t, e, part):
                if part == "down":
                    src = A["w_down_2"][e].rearrange("(k p) n -> p k n", p=P)
                    dst = raw[:, slot(t), :].rearrange("p (k n) -> p k n", n=D)
                    return [(dst[:, k], src[:, k]) for k in range(2)]
                dst = raw[:, slot(t), :].rearrange("p (k n) -> p k n", n=W)
                return [(dst[:, :, 256 * i:256 * i + 256],
                         A[m][e][part * W:(part + 1) * W, :].rearrange("(k p) n -> p k n", p=P))
                        for i, m in enumerate(("w_gate_2", "w_up_2"))]

            sp.dma_start(x[:], A["x"].rearrange("(t p) d -> p t d", p=P)).then_inc(in_x, 16)
            rows = [("norm_w", A["norm_w"].rearrange("l (k c) -> (l k) c", c=P)),
                    ("lb", A["lb_logits"].rearrange("l (k c) -> (l k) c", c=P)),
                    ("hgrn", A["hgrn_norm_w"]),
                    ("attn_norm", A["attn_norm_g_2"].rearrange("(k c) -> k c", c=P)),
                    ("ffn_norm", A["ffn_norm_g_2"].rearrange("(k c) -> k c", c=P)),
                    ("ple_norm", A["ple_norm_g_2"].rearrange("(k c) -> k c", c=P)),
                    ("conv", A["conv_w_2"].rearrange("j (k c) -> (j k) c", c=P))]
            for name, src in rows:
                a = COL_AT[name]
                sp.dma_start(colrows[a:a + COL_COUNT[name], :], src).then_inc(in_rows, 16)
            for name, src in (("q_gain", A["q_norm_g_2"].unsqueeze(0)), ("k_gain", A["k_norm_g_2"].unsqueeze(0))):
                a = COL_AT[name]
                for half in range(2):
                    sp.dma_start(colrows[a:a + 1, 64 * half:64 * half + 64], src).then_inc(in_rows, 16)
            with sp.Fori(0, 2) as layer:
                for i in range(NT1):
                    load(i, halves(i, B1_TILES[i], layer), layer * NT1 + i)
            for i in range(NT2):
                load(T2 + i, halves(T2 + i, B2_TILES[i]), T2 + i)
                if i == 0:
                    sp.wait_ge(src_ready, 4)
                    sp.dma_start(fw, A["final_norm_w"].partition_broadcast(P)).then_inc(in_fw, 16)
                if i == 21:
                    sp.wait_ge(S["uT_ready"], 1)
                    sp.dma_start(p_tok, A["p_2"].rearrange("(t p) n -> p t n", p=P)).then_inc(in_p, 16)
            for i, (e, part) in enumerate(((0, 0), (0, 1), (1, 0), (1, 1), (0, "down"))):
                load(TM + i, expert_halves(TM + i, e, part), TM + i)
            with sp.Fori(0, (EXPERTS - 2) // 2) as it:
                for j in range(2):
                    for i, (de, part) in enumerate(((2, 0), (2, 1), (1, "down"))):
                        n = 5 + 3 * j + i
                        load(TM + n, expert_halves(TM + n, it * 2 + (j + de), part), it * 6 + (TM + n))
            load(TP - 1, expert_halves(TP - 1, EXPERTS - 1, "down"), TP - 1)
            src = A["w_ple_2"].rearrange("(k p) n -> p k n", p=P)
            dst = raw[:, slot(TP), :].rearrange("p (k n) -> p k n", n=D)
            load(TP, [(dst[:, k], src[:, k]) for k in range(2)], TP)
            for i, tile in enumerate(group_tiles("w_pg_2", 0, W, KT) + group_tiles("w_pg_2", W, W, KT)):
                load(TP + 1 + i, halves(TP + 1 + i, tile), TP + 1 + i)
            for half in range(2):
                sp.wait_ge(S["final_ready"], half + 1)
                c = slice(half * W, half * W + W)
                sp.dma_start(out.rearrange("(t p) d -> p t d", p=P)[:, :, c], x[:, :, c]).then_inc(S["out_done"], 16)
            sp.wait_ge(S["out_done"], 32)

        @block.gpsimd
        def _(pool):
            pool.sem_inc(lo_split, RING)
            pool.memset(ident[:], 0.0).then_inc(S["pool_chain"], 1)
            pool.wait_ge(S["pool_chain"], 1)
            pool.affine_select(out=ident[:], in_=ident[:], compare_op=ALU.not_equal, fill=1.0, base=0,
                               pattern=[[-1, P]], channel_multiplier=1).then_inc(S["ident_ready"], 1)

            pool.iota(iota_t, pattern=[[1, P]], base=0, channel_multiplier=0).then_inc(S["iota_ready"], 1)
            pool.iota(iota_s, pattern=[[0, P]], base=0, channel_multiplier=1).then_inc(S["iota_ready"], 1)
            for b in range(4):
                i = pool.memset(amask[:, b, :], 0.0)
            i.then_inc(S["pool_chain"], 1)
            pool.wait_ge(S["pool_chain"], 2)
            pool.affine_select(out=amask[:, 0, :], in_=amask[:, 0, :], compare_op=ALU.is_gt, fill=MASKED, base=0,
                               pattern=[[1, P]], channel_multiplier=-1)
            for b in (1, 3):
                i = pool.affine_select(out=amask[:, b, :], in_=amask[:, b, :], compare_op=ALU.is_ge, fill=MASKED,
                                       base=0, pattern=[[-1, P]], channel_multiplier=1)
            i.then_inc(S["amask_ready"], 1)

            def lo(t, width, sofar, loads):
                pool.wait_ge(raw_loaded[slot(t)], loads)
                pool.wait_ge(hi_split, sofar + (RING + 1))
                pool.tensor_tensor(w_lo[:, slot(t), 0:width], raw[:, slot(t), 0:width],
                                   w_hi[:, slot(t), 0:width].bitcast(F32), ALU.subtract).then_inc(lo_split, 1)

            with pool.Fori(0, 2) as layer:
                for i in range(NT1):
                    lo(i, tile_width(B1_TILES[i]), layer * NT1 + i, layer * (32 * NT1 // RING) + 32 * (i // RING + 1))
            for t in range(T2, T2 + NT2):
                lo(t, 2048, t, 32 * (t // RING + 1))
                if t == T2:
                    pool.wait_ge(S["b_ready"], 2)
                    pool.memset(selneg, 0.0).then_inc(S["pool_chain"], 1)
                    pool.memset(tri, 1.0).then_inc(S["pool_chain"], 1)
                    pool.wait_ge(S["pool_chain"], 4)
                    sel3 = selneg.rearrange("h (g c) -> h g c", g=8)
                    pool.affine_select(out=sel3, in_=sel3, compare_op=ALU.not_equal, fill=-1.0, base=0,
                                       pattern=[[-1, 8], [0, P]], channel_multiplier=1).then_inc(S["pool_chain"], 1)
                    pool.wait_ge(S["pool_chain"], 5)
                    pool.affine_select(out=sel3, in_=sel3, compare_op=ALU.not_equal, fill=-1.0, base=-64,
                                       pattern=[[-1, 8], [0, P]], channel_multiplier=1).then_inc(S["selneg_ready"], 1)
                    pool.affine_select(out=tri[:, 0:P], in_=tri[:, 0:P], compare_op=ALU.is_ge, fill=0.0, base=0,
                                       pattern=[[1, P]], channel_multiplier=-1).then_inc(S["tri_ready"], 1)
            for t in range(TM, TM + 5):
                lo(t, 2048, t, 32 * (t // RING + 1))
            with pool.Fori(0, (EXPERTS - 2) // 2) as it:
                for n in range(TM + 5, TM + 11):
                    lo(n, 2048, it * 6 + n, it * 64 + 32 * (n // RING + 1))
            for t in range(TP - 1, TP + 5):
                lo(t, 2048, t, 32 * (t // RING + 1))

        @block.tensor
        def _(pe):
            pe.sem_inc(tile_done, RING)
            for p in range(2):
                pe.sem_inc(mm_free[p], 1)
                pe.sem_inc(aux_free[p], 1)

            def products(dst, lhs, k, tt, rhs, start, stop):
                a_hi = lhs[0][:, k, tt * P:(tt + 1) * P]
                a_lo = lhs[1][:, k, tt * P:(tt + 1) * P]
                pe.matmul(dst, a_hi, rhs[0], start=start, stop=False, skip_group_check=True)
                pe.matmul(dst, a_hi, rhs[1], start=False, stop=False, skip_group_check=True)
                return pe.matmul(dst, a_lo, rhs[0], start=False, stop=stop, skip_group_check=True)

            def tile_parts(t, n, width=2048):
                return [w[:, slot(t), 0:width].rearrange("p (k n) -> p k n", n=n) for w in (w_hi, w_lo)]

            def use_tile(t, sofar, body, n, width=2048):
                pe.wait_ge(hi_split, sofar + (RING + 1))
                pe.wait_ge(lo_split, sofar + (RING + 1))
                body(tile_parts(t, n, width)).then_inc(tile_done, 1)

            def group(tiles, first, sofar, lhs, turn, lhs_wait=None, lhs_ktile0=0, between=None):
                pair, value = turn
                n_tiles = len(tiles)
                for j, tile in enumerate(tiles):
                    nk, n = tile[2], tile[4]
                    if j == 0:
                        pe.wait_ge(mm_free[pair], value)

                    def body(parts):
                        for k in range(nk):
                            if lhs_wait is not None:
                                lhs_wait(j * 4 + k)
                            for tt in range(TT):
                                last = products(mm[pair][:, tt * W:tt * W + n], lhs, j * 4 + k, tt,
                                                [q[:, k, :] for q in parts], j == 0 and k == 0,
                                                j == n_tiles - 1 and k == nk - 1)
                        return last
                    use_tile(first + j, sofar + j, body, n, nk * n)
                    if between is not None:
                        between(j)

            def begin(turn):
                pair, value = turn
                pe.wait_ge(aux_free[pair], value)
                return aux[pair]

            def end(turn, last):
                last.then_inc(aux_ready[turn[0]], 1)

            def transposes(turn, blocks):
                ps = begin(turn)
                for i, b in enumerate(blocks):
                    last = pe.transpose(ps[:, i * P:(i + 1) * P], b, ident[:])
                end(turn, last)

            def norm_transposes(turns, use):
                pe.wait_ge(src_ready, use + 1)
                for h, turn in enumerate(turns):
                    transposes(turn, [xm3[:, tt, k * P:(k + 1) * P] for k in range(4 * h, 4 * h + 4) for tt in range(TT)])

            hT, aT, bT = (hT_hi, hT_lo), (aT_hi, aT_lo), (bT_hi, bT_lo)

            def hT_part(use):
                def wait(k):
                    pe.wait_ge(hT_hi_ready, use * KT + (k + 1))
                    pe.wait_ge(hT_lo_ready, use * KT + (k + 1))
                return wait

            def score_unit(turn, u, qpart, kpart, bias2):
                ps = begin(turn)
                heads = range(8) if u == 0 else range(4 * (u - 1), 4 * u)
                keys = P if u == 0 else 2 * P
                for i, h in enumerate(heads):
                    dst = ps[:, i * keys:(i + 1) * keys]
                    qtt = 0 if u == 0 else 1
                    last = pe.matmul(dst, qpart(h, qtt), kpart(h, keys), start=True, stop=not bias2)
                    if bias2:
                        r = slice(64 * (h // 4), 64 * (h // 4) + 64)
                        last = pe.matmul(dst, selneg[r, h * P:(h + 1) * P], cT[r, 0:keys], start=False, stop=True)
                end(turn, last)

            def p_transposes(turn, u, n):
                pe.wait_ge(S["p_ready"], n * 3 + (u + 1))
                transposes(turn, [s_ring[:, u % 2, i * P:(i + 1) * P] for i in range(8)])

            def pv(turn, u, n, vpart):
                pe.wait_ge(S["pT_ready"], n * 3 + (u + 1))
                ps = begin(turn)
                if u == 0:
                    for h in range(8):
                        last = pe.matmul(ps[:, h * 64:h * 64 + 64], pT[:, h * P:(h + 1) * P], vpart(h, 0),
                                         start=True, stop=True)
                else:
                    for i in range(4):
                        for kt in range(2):
                            last = pe.matmul(ps[:, i * 64:i * 64 + 64], pT[:, (2 * i + kt) * P:(2 * i + kt + 1) * P],
                                             vpart(4 * (u - 1) + i, kt), start=kt == 0, stop=kt == 1)
                end(turn, last)

            pe.wait_ge(S["ident_ready"], 1)
            pe.wait_ge(in_rows, 16 * 11)
            pe.transpose(mm[1][:, 0:N_COLS], colrows, ident[0:N_COLS, 0:N_COLS]).then_inc(S["setup_pe"], 1)
            pe.wait_ge(S["cols_ready"], 1)

            with pe.Fori(0, 2) as L:
                def job(name):
                    return AUX1.turn(name, L)

                norm_transposes([job("N0"), job("N1")], L * 2)

                def level(j):
                    name = f"L{j}"
                    if j == 0:
                        pe.wait_ge(S["kTh_ready"], L + 1)
                        pe.wait_ge(S["qTh_ready"], L + 1)
                    else:
                        pe.wait_ge(S["W_ready"], L * 8 + j)
                    ps = begin(job(name))
                    e = E[(j - 1) % 2]
                    if j == 8:
                        for h in range(4):
                            last = pe.matmul(ps[:, h * P:(h + 1) * P], e[:, h * 256:h * 256 + P],
                                             e[:, h * 256 + P:h * 256 + 256], start=True, stop=True)
                    else:
                        a, b = (kTh, qTh) if j == 0 else (e, e)
                        for i in range(8):
                            last = pe.matmul(ps[:, i * P:(i + 1) * P], a[:, i * P:(i + 1) * P], b[:, i * P:(i + 1) * P],
                                             start=True, stop=True)
                    end(job(name), last)

                def hgrn_out():
                    pe.wait_ge(S["acc_ready"], L + 1)
                    pe.wait_ge(S["sc128_ready"], L + 1)
                    pe.wait_ge(S["vh_ready"], L + 1)
                    ps = begin(job("OH"))
                    for h in range(4):
                        v0, v1 = (vh[:, tt, h * P:(h + 1) * P] for tt in range(2))
                        pe.matmul(ps[:, h * P:(h + 1) * P], acc[:, 2 * h * P:(2 * h + 1) * P], v0, start=True, stop=True)
                        dst = ps[:, W + h * P:W + (h + 1) * P]
                        pe.matmul(dst, acc[:, (2 * h + 1) * P:(2 * h + 2) * P], v1, start=True, stop=False)
                        last = pe.matmul(dst, sc128[:, h * P:(h + 1) * P], v0, start=False, stop=True)
                    end(job("OH"), last)

                def f_transposes():
                    pe.wait_ge(S["ftok_ready"], L + 1)
                    transposes(job("F"), [E[0][:, tt * W + h * P:tt * W + (h + 1) * P] for h in range(4) for tt in range(TT)])

                def qh_transposes():
                    pe.wait_ge(S["qhtok_ready"], L + 1)
                    transposes(job("QH"), [E[1][:, tt * W + h * P:tt * W + (h + 1) * P] for h in range(4) for tt in range(TT)])

                def q_transposes():
                    pe.wait_ge(S["qk_ready"], L + 1)
                    transposes(job("QT"), [qk[:, tt, 2 * j:2 * j + 2, :].rearrange("p a b -> p (a b)")
                                           for j in range(4) for tt in range(TT)])

                def k_transposes():
                    transposes(job("KT"), [qk[:, tt, 8:10, :].rearrange("p a b -> p (a b)") for tt in range(TT)])

                def scores(u):
                    if u == 0:
                        pe.wait_ge(S["qT_ready"], L + 1)
                        pe.wait_ge(S["kT_ready"], L + 1)
                    score_unit(job(f"S{u}"), u,
                               lambda h, tt: qTp[64 * (h // 4):64 * (h // 4) + 64, (h % 4) * 256 + tt * P:(h % 4) * 256 + (tt + 1) * P],
                               lambda h, keys: kT[64 * (h // 4):64 * (h // 4) + 64, 0:keys], False)

                def pvs(u):
                    if u == 0:
                        pe.wait_ge(S["v_ready"], L + 1)
                    pv(job(f"V{u}"), u, L, lambda h, kt: v_sb[:, kt, 64 * (h // 4):64 * (h // 4) + 64])

                def b_transposes():
                    pe.wait_ge(S["b_ready"], L + 1)
                    transposes(job("BT"), [b_tok[:, tt * W + c * P:tt * W + (c + 1) * P] for c in range(4) for tt in range(TT)])

                def a_transposes():
                    pe.wait_ge(S["a_ready"], L + 1)
                    transposes(job("AT"), [a_tok[:, tt, c * P:(c + 1) * P] for c in range(4) for tt in range(TT)])

                after = {2: [f_transposes], 4: [qh_transposes], 6: [lambda: level(0)], 7: [lambda: level(1)],
                         8: [lambda: level(2)], 9: [lambda: level(3)],
                         10: [lambda: level(4)], 11: [q_transposes, k_transposes, lambda: level(5)],
                         12: [lambda: scores(0), lambda: level(6)], 13: [lambda: scores(1), lambda: level(7)],
                         14: [lambda: p_transposes(job("P0"), 0, L), lambda: level(8)],
                         15: [lambda: pvs(0), lambda: scores(2)],
                         16: [lambda: p_transposes(job("P1"), 1, L), hgrn_out],
                         17: [lambda: pvs(1)], 18: [lambda: p_transposes(job("P2"), 2, L)],
                         19: [lambda: pvs(2), b_transposes], 20: [a_transposes]}

                def between_from(first):
                    def between(j):
                        for f in after.get(first + j, ()):
                            f()
                    return between

                t = 0
                for i, name in enumerate(GROUPS1[:11]):
                    group(B1_TILES[t:t + 2], t, L * NT1 + t, hT, MM1.turn(name, L),
                          lhs_wait=hT_part(L * 2) if i == 0 else None, between=between_from(t))
                    t += 2
                for i, name in enumerate(("a0", "a1", "b0", "b1")):
                    if i == 0:
                        pe.wait_ge(S["aT_hi_ready"], L + 1)
                        pe.wait_ge(S["aT_lo_ready"], L + 1)
                    if i == 2:
                        pe.wait_ge(S["bT_hi_ready"], L + 1)
                        pe.wait_ge(S["bT_lo_ready"], L + 1)
                    group(B1_TILES[t:t + 1], t, L * NT1 + t, aT if i < 2 else bT, MM1.turn(name, L))
                    t += 1
                norm_transposes([job("M0"), job("M1")], L * 2 + 1)
                for i, name in enumerate(("o0", "o1")):
                    group(B1_TILES[t:t + 2], t, L * NT1 + t, hT, MM1.turn(name, L),
                          lhs_wait=hT_part(L * 2 + 1) if i == 0 else None)
                    t += 2

            def job(name):
                return AUX2.turn(name)

            norm_transposes([job("N0"), job("N1")], 4)

            def small(turn, parts, n, wait=None):
                ps = begin(turn)
                for tt in range(TT):
                    for k in range(KT):
                        last = products(ps[:, tt * W:tt * W + n], hT, k, tt, [q[:, k, :] for q in parts], k == 0, k == KT - 1)
                end(turn, last)

            def forget_logits():
                pe.wait_ge(S["wf_hi_ready"], 1)
                pe.wait_ge(S["wf_lo_ready"], 1)
                small(job("FL"), (wf_hi, wf_lo), 8)

            def forget_sums():
                pe.wait_ge(S["lf_ready"], 1)
                pe.wait_ge(S["tri_ready"], 1)
                ps = begin(job("CT"))
                pe.matmul(ps[:, 0:256], lfw[:, 0, :], tri, start=True, stop=False, skip_group_check=True)
                last = pe.matmul(ps[:, P:256], lfw[:, 1, :], tri[:, 0:P], start=False, stop=True, skip_group_check=True)
                end(job("CT"), last)

            def q2_transposes():
                pe.wait_ge(S["q2_ready"], 1)
                transposes(job("QT"), [a_tok[:, tt, c * P:(c + 1) * P] for c in range(4) for tt in range(TT)])

            def k2_transposes():
                pe.wait_ge(S["q2_ready"], 2)
                transposes(job("KT"), [k2[:, tt * W + c * P:tt * W + (c + 1) * P] for c in range(4) for tt in range(TT)])

            def scores2(u):
                if u == 0:
                    pe.wait_ge(S["qT_ready"], 3)
                    pe.wait_ge(S["kT_ready"], 3)
                    pe.wait_ge(S["cT_ready"], 1)
                    pe.wait_ge(S["selneg_ready"], 1)
                score_unit(job(f"S{u}"), u,
                           lambda h, tt: qTp[64 * (h // 4):64 * (h // 4) + 64, (h % 4) * 256 + tt * P:(h % 4) * 256 + (tt + 1) * P],
                           lambda h, keys: kT2[64 * (h // 4):64 * (h // 4) + 64, (h % 4) * 256:(h % 4) * 256 + keys], True)

            def pvs2(u):
                if u == 0:
                    pe.wait_ge(S["vh_ready"], 3)
                pv(job(f"V{u}"), u, 2, lambda h, kt: vh[:, kt, h * 64:h * 64 + 64])

            def u_transposes():
                pe.wait_ge(S["u_ready"], 1)
                transposes(job("UT"), [g[:, tt, c * P:(c + 1) * P] for c in range(4) for tt in range(TT)])

            def cb_transposes():
                pe.wait_ge(S["cb_ready"], 1)
                transposes(job("CB"), [z[:, tt, c * P:(c + 1) * P] for c in range(4) for tt in range(TT)])

            def a2_transposes():
                pe.wait_ge(S["a_ready"], 3)
                transposes(job("AT"), [a_tok[:, tt, c * P:(c + 1) * P] for c in range(4) for tt in range(TT)])

            def p2_transposes():
                pe.wait_ge(in_p, 16)
                transposes(job("PT"), [p_tok[:, tt, c * P:(c + 1) * P] for c in range(2) for tt in range(TT)])

            after = {0: [forget_logits], 2: [forget_sums], 3: [q2_transposes], 5: [k2_transposes],
                     6: [lambda: scores2(0)], 7: [lambda: scores2(1)], 8: [lambda: p_transposes(job("P0"), 0, 2)],
                     9: [lambda: pvs2(0), lambda: scores2(2)], 10: [lambda: p_transposes(job("P1"), 1, 2)],
                     11: [lambda: pvs2(1)], 12: [lambda: p_transposes(job("P2"), 2, 2)],
                     13: [lambda: pvs2(2)], 14: [u_transposes], 15: [cb_transposes], 17: [a2_transposes]}

            def between_from(first):
                def between(j):
                    for f in after.get(first + j, ()):
                        f()
                return between

            t = 0
            for i, name in enumerate(GROUPS2[:10]):
                group(B2_TILES[t:t + 2], T2 + t, T2 + t, hT, MM2.turn(name), lhs_wait=hT_part(4) if i == 0 else None,
                      between=between_from(t))
                t += 2
            for i, name in enumerate(("b0", "b1", "a0", "a1")):
                if i == 0:
                    pe.wait_ge(S["bT_hi_ready"], 3)
                    pe.wait_ge(S["bT_lo_ready"], 3)
                if i == 2:
                    pe.wait_ge(S["aT_hi_ready"], 3)
                    pe.wait_ge(S["aT_lo_ready"], 3)
                group(B2_TILES[t:t + 1], T2 + t, T2 + t, bT if i < 2 else aT, MM2.turn(name))
                t += 1
            p2_transposes()
            norm_transposes([job("M0"), job("M1")], 5)
            for i, name in enumerate(("o0", "o1")):
                group(B2_TILES[t:t + 2], T2 + t, T2 + t, hT, MM2.turn(name), lhs_wait=hT_part(5) if i == 0 else None)
                t += 2

            norm_transposes([job("R0"), job("R1")], 6)
            hT_part(6)(KT - 1)
            pe.wait_ge(S["wf_hi_ready"], 2)
            pe.wait_ge(S["wf_lo_ready"], 2)
            small(job("RL"), (wr_hi, wr_lo), 20)

            def gate_up(t, sofar, part, turn):
                if part == 0:
                    pe.wait_ge(aux_free[0], turn)

                def body(parts):
                    for k in range(4):
                        for tt in range(TT):
                            last = products(aux[0][:, tt * W:(tt + 1) * W], hT, 4 * part + k, tt,
                                            [q[:, k, :] for q in parts], part == 0 and k == 0, part == 1 and k == 3)
                    return last
                use_tile(t, sofar, body, W)

            def expert_transposes(parity, turn, hidden_turn):
                pe.wait_ge(aux_free[0], hidden_turn + 1)
                pe.wait_ge(aux_free[1], turn)
                for i, (c, tt) in enumerate((c, tt) for c in range(2) for tt in range(TT)):
                    last = pe.transpose(aux[1][:, i * P:(i + 1) * P], hid[:, parity, tt, c * P:(c + 1) * P], ident[:])
                last.then_inc(aux_ready[1], 1)

            def down(t, sofar, parity, turn, first=False, final=False):
                pe.wait_ge(aux_free[1], turn + 1)
                lhs = bT if parity else aT

                def body(parts):
                    for k in range(2):
                        for tt in range(TT):
                            for c in range(2):
                                last = products(mm[tt][:, c * W:(c + 1) * W], lhs, k, tt,
                                                [q[:, k, c * W:(c + 1) * W] for q in parts],
                                                first and k == 0, final and k == 1)
                    return last
                use_tile(t, sofar, body, D)

            gate_up(TM, TM, 0, AUXM[0] + 1)
            gate_up(TM + 1, TM + 1, 1, None)
            gate_up(TM + 2, TM + 2, 0, AUXM[0] + 2)
            expert_transposes(0, AUXM[1] + 1, AUXM[0] + 1)
            gate_up(TM + 3, TM + 3, 1, None)
            for tt in range(TT):
                pe.wait_ge(mm_free[tt], MMM[tt] + 1)
            down(TM + 4, TM + 4, 0, AUXM[1] + 1, first=True)
            with pe.Fori(0, (EXPERTS - 2) // 2) as it:
                for j in range(2):
                    n = TM + 5 + 3 * j
                    e = 2 + j
                    gate_up(n, it * 6 + n, 0, it * 2 + (AUXM[0] + e + 1))
                    expert_transposes((e - 1) % 2, it * 2 + (AUXM[1] + e), it * 2 + (AUXM[0] + e))
                    gate_up(n + 1, it * 6 + (n + 1), 1, None)
                    down(n + 2, it * 6 + (n + 2), (e - 1) % 2, it * 2 + (AUXM[1] + e))
            expert_transposes(1, AUXM[1] + EXPERTS, AUXM[0] + EXPERTS)
            down(TP - 1, TP - 1, 1, AUXM[1] + EXPERTS, final=True)

            for p in range(2):
                pe.wait_ge(aux_free[p], AUXP[p] + 1)
            pe.wait_ge(S["pT_lo_ready"], 1)

            def ple(parts):
                for c in range(2):
                    for k in range(2):
                        for tt in range(TT):
                            last = products(aux[c][:, tt * W:(tt + 1) * W], aT, 2 + k, tt,
                                            [q[:, k, c * W:(c + 1) * W] for q in parts], k == 0, k == 1)
                return last
            use_tile(TP, TP, ple, D)
            norm_transposes([(0, AUXP[0] + 2), (1, AUXP[1] + 2)], 7)
            for c in range(2):
                group(group_tiles("w_pg_2", c * W, W, KT), TP + 1 + 2 * c, TP + 1 + 2 * c, hT, (c, MMM[c] + 2),
                      lhs_wait=hT_part(7) if c == 0 else None)

        @block.scalar
        def _(act):
            act.sem_inc(hi_split, RING)
            act.dma_start(pos_i[:].unsqueeze(2), A["positions"].rearrange("(t p one) -> p t one", p=P, one=1), allow_slow_non_contiguous=True).then_inc(in_small, 16)
            for layer in range(2):
                act.dma_start(lcols_all[:, layer, LAYER_COLS - 8:], A["attn_sinks"][layer].partition_broadcast(P)
                              ).then_inc(in_small, 16)
            for a, n, src in ((0, 8, A["b_f_2"]), (8, 4, A["b_rg_2"]), (12, 16, A["b_re_2"])):
                act.dma_start(bias[:, a:a + n], src.partition_broadcast(P)).then_inc(in_small, 16)
            act.dma_start(wf[:], A["w_in_2"][:, 1536:1544].rearrange("(k p) n -> p k n", p=P)).then_inc(in_small, 16)
            act.dma_start(wr[:, :, 0:4], A["w_rg_2"].rearrange("(k p) n -> p k n", p=P)).then_inc(in_small, 16)
            act.dma_start(wr[:, :, 4:20], A["w_re_2"].rearrange("(k p) n -> p k n", p=P)).then_inc(in_small, 16)
            chain = [0]

            def link(ins):
                chain[0] += 1
                ins.then_inc(S["act_chain"], 1)
                act.wait_ge(S["act_chain"], chain[0])

            def release(ins, free, value, event):
                ins.then_inc(free, 1)
                act.wait_ge(free, value + 1)
                act.sem_inc(event, 1)

            def hi(t, width, sofar, loads):
                act.wait_ge(raw_loaded[slot(t)], loads)
                act.wait_ge(tile_done, sofar + 1)
                act.activation(w_hi[:, slot(t), 0:width], raw[:, slot(t), 0:width], ACT.Copy).then_inc(hi_split, 1)

            def row_norm(v, need_x):
                need_x()
                for tt in range(TT):
                    ins = act.activation(xm3[:, tt, :], x[:, tt, :], ACT.Square, accum_out=st[:, tt:tt + 1])
                    link(ins)
                act.activation(st[:, 2:4], st[:, 0:2], ACT.Sqrt, bias=one[:, 0:1], scale=1.0 / D).then_inc(std_ready, 1)

            def split_T(turns, colfn, use):
                for h, (pair, value) in enumerate(turns):
                    act.wait_ge(aux_ready[pair], value)
                    for k in range(4):
                        src = aux[pair][:, k * 256:(k + 1) * 256]
                        dst = hT_hi[:, 4 * h + k, :]
                        if colfn is None:
                            ins = act.activation(dst, src, ACT.Copy)
                        else:
                            ins = act.activation(dst, src, ACT.Copy, scale=colfn(4 * h + k))
                        ins.then_inc(hT_hi_ready, 1)

            def exps(u, n, n_heads):
                act.wait_ge(S["S_ready"], n * 3 + (u + 1))
                w = 1024 // n_heads
                for i in range(n_heads):
                    src = s_ring[:, u % 2, i * w:(i + 1) * w]
                    ins = act.activation(src, src, ACT.Exp, bias=ast[:, 1, a_at(u) + i:a_at(u) + i + 1],
                                         accum_out=ast[:, 2, a_at(u) + i:a_at(u) + i + 1])
                ins.then_inc(S["p_ready"], 1)

            def copy_out(dst, turn, width, event, func=ACT.Copy, **kw):
                pair, value = turn
                act.wait_ge(aux_ready[pair], value)
                ins = act.activation(dst, aux[pair][:, 0:width], func, **kw)
                release(ins, aux_free[pair], value, event)

            hi(0, 2048, 0, 32)
            act.wait_ge(S["lb_in"], 1)
            act.activation(hst[:, 0:8], hst[:, 8:16], ACT.Exp).then_inc(S["lb_exp"], 1)
            act.wait_ge(S["rope_in"], 1)
            act.activation(rope[:, :, :, :].rearrange("p a b c -> p (a b c)"),
                           rope_t[:, 4:6, :, :].rearrange("p a b c -> p (a b c)"), ACT.Sin).then_inc(S["rope_sin"], 1)
            hi(1, 2048, 1, 32)

            with act.Fori(0, 2) as L:
                def per(i):
                    return L * (32 * NT1 // RING) + 32 * (i // RING + 1)

                def layer_hi(i):
                    if i < NT1:
                        hi(i, tile_width(B1_TILES[i]), L * NT1 + i, per(i))

                chain[0] = 0
                row_norm(L, lambda: act.wait_ge(x_ready, L + 1))
                layer_hi(2)
                act.wait_ge(S["layer_cols"], L + 1)
                split_T([AUX1.turn("N0", L), AUX1.turn("N1", L)], lambda k: lcols[:, k:k + 1], L * 2)

                def sigmoids():
                    act.wait_ge(S["fT_ready"], L + 1)
                    link(act.activation(E[0], fT, ACT.Sigmoid))
                    act.activation(kTh[:], fT, ACT.Sigmoid, scale=-1.0).then_inc(S["sig_ready"], 1)
                    for h in range(4):
                        c = slice(h * 256, (h + 1) * 256)
                        ins = act.activation(logf[:, c], E[0][:, c], ACT.Ln, scale=lcols[:, 12 + h:13 + h],
                                             bias=lcols[:, 8 + h:9 + h])
                    ins.then_inc(S["log_ready"], 1)

                def qh_silu():
                    copy_out(qTh[:], AUX1.turn("QH", L), 1024, S["qTh_ready"], ACT.Silu)

                def mm_out(name, dst, event, func=ACT.Copy):
                    pair, value = MM1.turn(name, L)
                    act.wait_ge(tile_done, L * NT1 + (LAST1[name] + RING + 1))
                    ins = act.activation(dst, mm[pair][:, :].rearrange("p (t n) -> p t n", t=TT), func)
                    release(ins, mm_free[pair], value, event)

                def level_exp(j):
                    act.wait_ge(S["D_ready"], L * 8 + j)
                    e = E[(j - 1) % 2]
                    act.activation(e, e, ACT.Exp).then_inc(S["E_ready"], 1)

                def kv_out():
                    pair, value = MM1.turn("kv", L)
                    act.wait_ge(S["qk_ready"], L + 1)
                    act.activation(v_sb[:], mm[pair][:, :].rearrange("p (t n) -> p t n", t=TT)[:, :, P:2 * P],
                                   ACT.Copy).then_inc(S["v_ready"], 1)

                def sink_exp(u, n_heads):
                    act.wait_ge(S["sinkexp_in"], L * 3 + (u + 1))
                    a = a_at(u)
                    act.activation(ast[:, 4, a:a + n_heads], ast[:, 3, a:a + n_heads], ACT.Exp
                                   ).then_inc(S["sinkexp_ready"], 1)

                def hgrn_norm():
                    pair, value = AUX1.turn("OH", L)
                    act.wait_ge(aux_ready[pair], value)
                    act.activation(E[0], aux[pair][:, :], ACT.Square).then_inc(S["osq_ready"], 1)
                    act.wait_ge(S["oss_ready"], L + 1)
                    act.activation(hst[:, 8:16], hst[:, 0:8], ACT.Sqrt, bias=one[:, 0:1], scale=1.0 / P
                                   ).then_inc(S["ostd_ready"], 1)

                def b_split():
                    pair, value = AUX1.turn("BT", L)
                    act.wait_ge(aux_ready[pair], value)
                    act.activation(bT_hi[:, :, :].rearrange("p a b -> p (a b)"), aux[pair][:, :], ACT.Copy,
                                   scale=lcols[:, 16:17]).then_inc(S["bT_hi_ready"], 1)

                def a_split():
                    pair, value = AUX1.turn("AT", L)
                    act.wait_ge(aux_ready[pair], value)
                    act.activation(aT_hi[:, :, :].rearrange("p a b -> p (a b)"), aux[pair][:, :], ACT.Copy
                                   ).then_inc(S["aT_hi_ready"], 1)

                steps = {
                    3: [sigmoids], 5: [qh_silu], 6: [lambda: (act.wait_ge(S["lmask_ready"], 1), mm_out("vh", vh[:], S["vh_ready"]))],
                    7: [lambda: level_exp(1)], 8: [lambda: level_exp(2)], 9: [lambda: level_exp(3)],
                    10: [kv_out, lambda: level_exp(4)],
                    11: [lambda: level_exp(5)],
                    12: [lambda: mm_out("z", z[:], S["z_ready"], ACT.Silu),
                         lambda: copy_out(qTp[:], AUX1.turn("QT", L), 1024, S["qT_ready"], scale=0.125),
                         lambda: copy_out(kT[:], AUX1.turn("KT", L), 256, S["kT_ready"]),
                         lambda: level_exp(6)],
                    13: [lambda: exps(0, L, 8), lambda: sink_exp(0, 8), lambda: level_exp(7)],
                    14: [lambda: mm_out("g", g[:], S["g_ready"], ACT.Silu), lambda: exps(1, L, 4), lambda: sink_exp(1, 4),
                         lambda: level_exp(8)],
                    15: [lambda: copy_out(pT[:], AUX1.turn("P0", L), 1024, S["pT_ready"]),
                         lambda: copy_out(sc128[:], AUX1.turn("L8", L), 512, S["sc128_ready"])],
                    16: [lambda: mm_out("ga0", ga[:, :, 0:W], S["gate_ready"], ACT.Sigmoid), lambda: exps(2, L, 4),
                         lambda: sink_exp(2, 4)],
                    17: [lambda: copy_out(pT[:], AUX1.turn("P1", L), 1024, S["pT_ready"]), hgrn_norm],
                    18: [lambda: mm_out("ga1", ga[:, :, W:D], S["gate_ready"], ACT.Sigmoid)],
                    19: [lambda: copy_out(pT[:], AUX1.turn("P2", L), 1024, S["pT_ready"])],
                    20: [lambda: mm_out("gb0", gb[:, :, 0:W], S["gate_ready"], ACT.Sigmoid), b_split],
                    21: [a_split],
                    22: [lambda: mm_out("gb1", gb[:, :, W:D], S["gate_ready"], ACT.Sigmoid)],
                    26: [lambda: split_T([AUX1.turn("M0", L), AUX1.turn("M1", L)], None, L * 2 + 1)],
                }
                for i in range(1, NT1 - 2):
                    layer_hi(i + 2)
                    for f in steps.get(i, ()):
                        f()
                for i in range(EARLY):
                    hi(i, 2048, L * NT1 + (NT1 + i), L * (32 * NT1 // RING) + 32 * (NT1 // RING + 1))
                act.sem_clear(S["act_chain"])

            chain[0] = 0

            def hi2(t):
                hi(t, 2048, t, 32 * (t // RING + 1))

            row_norm(2, lambda: act.wait_ge(x_ready, 3))
            row_norm(3, lambda: act.wait_ge(x_ready, 4))
            hi2(T2 + 2)
            split_T([AUX2.turn("N0"), AUX2.turn("N1")], lambda k: cols[:, COL_AT["attn_norm"] + k:COL_AT["attn_norm"] + k + 1], 4)
            act.wait_ge(in_small, 16 * 9)
            act.activation(wf_hi[:], wf[:], ACT.Copy).then_inc(S["wf_hi_ready"], 1)
            act.activation(wr_hi[:], wr[:], ACT.Copy).then_inc(S["wf_hi_ready"], 1)

            def mm_out(name, dst, event, func=ACT.Copy):
                pair, value = MM2.turn(name)
                act.wait_ge(tile_done, LAST2[name] + RING + 1)
                ins = act.activation(dst, mm[pair][:, :].rearrange("p (t n) -> p t n", t=TT), func)
                release(ins, mm_free[pair], value, event)

            def forget_exp():
                act.wait_ge(S["lf_in"], 1)
                link(act.activation(lf[:, 1], lf[:, 1], ACT.Exp, scale=-1.0))
                act.activation(lf[:, 1], lf[:, 1], ACT.Ln, bias=one[:, 1:2]).then_inc(S["lf_exp"], 1)

            def head_norm(i, name):
                pair, value = MM2.turn(name)
                act.wait_ge(tile_done, LAST2[name] + RING + 1)
                act.activation(E[0], mm[pair][:, :], ACT.Square).then_inc(S["qsq_ready"], 1)
                act.wait_ge(S["qss_ready"], i + 1)
                act.activation(st[:, 24:40], st[:, 8:24], ACT.Sqrt, bias=one[:, 0:1], scale=1.0 / 64
                               ).then_inc(S["qstd_ready"], 1)

            def T_out(dst, name, event, width=1024, **kw):
                copy_out(dst, AUX2.turn(name), width, event, **kw)

            def split_out(dst, name, width, event):
                pair, value = AUX2.turn(name)
                act.wait_ge(aux_ready[pair], value)
                act.activation(dst, aux[pair][:, 0:width], ACT.Copy).then_inc(event, 1)

            def y_split():
                act.wait_ge(S["y_ready"], 1)
                act.activation(bT_hi[:, :, :].rearrange("p a b -> p (a b)"), kTh[:], ACT.Copy).then_inc(S["bT_hi_ready"], 1)

            def cb_out():
                act.wait_ge(S["u_ready"], 1)
                mm_out("cb", z[:], S["cb_ready"])

            steps = {
                1: [forget_exp], 2: [lambda: head_norm(0, "q")], 4: [lambda: head_norm(1, "k"),
                                                                     lambda: (act.wait_ge(S["gain_ready"], 1),
                                                                              T_out(qTp[:], "QT", S["qT_ready"], scale=one[:, 2:3]))],
                6: [lambda: mm_out("v", vh[:], S["vh_ready"]),
                    lambda: T_out(kT2[:], "KT", S["kT_ready"], scale=cols[:, COL_AT["k_gain"]:COL_AT["k_gain"] + 1])],
                7: [lambda: exps(0, 2, 8)],
                8: [lambda: mm_out("cc", z[:], S["cc_ready"]), lambda: exps(1, 2, 4)],
                9: [lambda: T_out(pT[:], "P0", S["pT_ready"])], 10: [lambda: exps(2, 2, 4)],
                11: [lambda: T_out(pT[:], "P1", S["pT_ready"])],
                12: [cb_out],
                13: [lambda: T_out(pT[:], "P2", S["pT_ready"])],
                14: [lambda: mm_out("ga0", ga[:, :, 0:W], S["gate_ready"], ACT.Sigmoid)],
                16: [lambda: mm_out("ga1", ga[:, :, W:D], S["gate_ready"], ACT.Sigmoid), y_split],
                18: [lambda: mm_out("gb0", gb[:, :, 0:W], S["gate_ready"], ACT.Sigmoid),
                     lambda: split_out(aT_hi[:, :, :].rearrange("p a b -> p (a b)"), "AT", 1024, S["aT_hi_ready"])],
                20: [lambda: mm_out("gb1", gb[:, :, W:D], S["gate_ready"], ACT.Sigmoid)],
                24: [lambda: split_out(aT_hi[:, 2:4, :].rearrange("p a b -> p (a b)"), "PT", 512, S["aT_hi_ready"]),
                     lambda: split_T([AUX2.turn("M0"), AUX2.turn("M1")], None, 5)],
            }
            for i in range(1, NT2):
                if i + 2 < NT2:
                    hi2(T2 + i + 2)
                for f in steps.get(i, ()):
                    f()
            hi2(TM)
            hi2(TM + 1)
            row_norm(4, lambda: act.wait_ge(x_ready, 5))
            hi2(TM + 2)
            split_T([AUX2.turn("R0"), AUX2.turn("R1")], lambda k: cols[:, COL_AT["ffn_norm"] + k:COL_AT["ffn_norm"] + k + 1], 6)
            act.wait_ge(S["logit_ready"], 1)
            act.activation(moe[:, 3], moe[:, 2], ACT.Exp).then_inc(S["prob_ready"], 1)

            def silu(parity, turn):
                act.wait_ge(tile_done, turn)
                act.activation(sil[:, parity], aux[0][:, :].rearrange("p (t n) -> p t n", t=TT)[:, :, 0:256], ACT.Silu
                               ).then_inc(S["sil_ready"], 1)

            def eT_split(parity, turn):
                act.wait_ge(aux_ready[1], turn)
                dst = (bT_hi if parity else aT_hi)[:, 0:2, :].rearrange("p a b -> p (a b)")
                act.activation(dst, aux[1][:, 0:W], ACT.Copy).then_inc(S["eT_hi_ready"], 1)

            hi2(TM + 3)
            silu(0, TM + 1 + (RING + 1))
            hi2(TM + 4)
            eT_split(0, AUXM[1] + 1)
            hi2(TM + 5)
            silu(1, TM + 3 + (RING + 1))
            hi2(TM + 6)
            with act.Fori(0, (EXPERTS - 2) // 2) as it:
                for j in range(2):
                    n = TM + 5 + 3 * j
                    e = 2 + j
                    for i in (2, 3, 4):
                        hi(n + i, 2048, it * 6 + (n + i), it * 64 + 32 * ((n + i) // RING + 1))
                        if i == 2:
                            eT_split((e - 1) % 2, it * 2 + (AUXM[1] + e))
                        if i == 3:
                            silu(e % 2, it * 6 + (n + 1 + RING + 1))
            eT_split(1, AUXM[1] + EXPERTS)
            hi2(TP + 1)
            for c in range(2):
                act.wait_ge(tile_done, TP + RING + 1)
                act.activation(pl[:, :, c * W:(c + 1) * W], aux[c][:, :].rearrange("p (t n) -> p t n", t=TT), ACT.Copy
                               ).then_inc(aux_free[c], 1)
            row_norm(5, lambda: act.wait_ge(x_ready, 6))
            hi2(TP + 2)
            split_T([(0, AUXM[0] + 1), (1, AUXP[1] + 1)], lambda k: cols[:, COL_AT["ple_norm"] + k:COL_AT["ple_norm"] + k + 1], 7)
            hi2(TP + 3)
            hi2(TP + 4)
            for c in range(2):
                act.wait_ge(tile_done, TP + 2 * c + (RING + 3))
                act.activation(ga[:, :, c * W:(c + 1) * W], mm[c][:, :].rearrange("p (t n) -> p t n", t=TT), ACT.Sigmoid
                               ).then_inc(S["pg_ready"], 1)

        @block.vector
        def _(dve):
            chain = [0]

            def link(ins):
                chain[0] += 1
                ins.then_inc(S["dve_chain"], 1)
                dve.wait_ge(S["dve_chain"], chain[0])

            def release(ins, free, value, event=None):
                ins.then_inc(free, 1)
                dve.wait_ge(free, value + 1)
                if event is not None:
                    dve.sem_inc(event, 1)

            def tt_(out_, a, b, op):
                return dve.tensor_tensor(out_, a, b, op)

            def ts_(out_, a, s1, op0, s2=None, op1=None):
                if op1 is None:
                    return dve.tensor_scalar(out_, a, s1, None, op0)
                return dve.tensor_scalar(out_, a, s1, s2, op0, op1)

            link(dve.memset(one[:, 0:1], EPS))
            link(dve.memset(one[:, 1:2], 1.0))
            link(dve.memset(segment[:], 1.0))
            link(dve.memset(segment[:, :].rearrange("p (c n) -> p c n", n=64)[:, :, 0:1], 0.0))
            dve.wait_ge(in_x, 16)
            dve.sem_inc(x_ready, 1)
            dve.wait_ge(S["setup_pe"], 1)
            link(dve.tensor_copy(cols[:], mm[1][:, 0:N_COLS]))
            lb0 = cols[:, COL_AT["lb"]:COL_AT["lb"] + 4]
            lb1 = cols[:, COL_AT["lb"] + 4:COL_AT["lb"] + 8]
            link(tt_(hst[:, 16:20], lb0, lb1, ALU.max))
            tt_(hst[:, 8:12], lb0, hst[:, 16:20], ALU.subtract)
            link(tt_(hst[:, 12:16], lb1, hst[:, 16:20], ALU.subtract))
            dve.sem_inc(S["lb_in"], 1)
            dve.wait_ge(S["lb_exp"], 1)
            link(tt_(hst[:, 16:20], hst[:, 0:4], hst[:, 4:8], ALU.add))
            link(dve.reciprocal(hst[:, 20:24], hst[:, 16:20]))
            tt_(hst[:, 0:4], hst[:, 0:4], hst[:, 20:24], ALU.mult)
            link(tt_(hst[:, 4:8], hst[:, 4:8], hst[:, 20:24], ALU.mult))
            link(tt_(hst[:, 8:12], hst[:, 0:4], hst[:, 4:8], ALU.add))
            for layer in range(2):
                k = COL_AT["norm_w"] + layer * KT
                dve.tensor_copy(lcols_all[:, layer, 0:8], cols[:, k:k + KT])
                dve.tensor_copy(lcols_all[:, layer, 16:17], cols[:, COL_AT["hgrn"] + layer:COL_AT["hgrn"] + layer + 1])
                src = hst[:, 0:4] if layer == 0 else hst[:, 8:12]
                link(tt_(lcols_all[:, layer, 8:12], src, hst[:, 0:4], ALU.subtract))
                link(ts_(lcols_all[:, layer, 12:16], lcols_all[:, layer, 8:12], -1.0, ALU.mult, 1.0, ALU.add))
            dve.wait_ge(in_small, 16 * 9)
            link(ts_(one[:, 2:3], cols[:, COL_AT["q_gain"]:COL_AT["q_gain"] + 1], 0.125, ALU.mult))
            dve.sem_inc(S["gain_ready"], 1)
            dve.sem_inc(S["cols_ready"], 1)
            inv_freq = [float(np.float32(np.power(np.float32(500000.0), np.float32(-i * (2.0 / 16))))) for i in range(8)]
            link(dve.tensor_copy(st[:, 4:6], pos_i[:]))
            for i in range(8):
                ins = ts_(rope_t[:, 0, :, i], st[:, 4:6], inv_freq[i], ALU.mult)
            link(ins)
            link(ts_(rope_t[:, 1], rope_t[:, 0], 1.0 / (2 * np.pi), ALU.mult))
            link(ts_(rope_t[:, 1], rope_t[:, 1], 12582912.0, ALU.add))
            link(ts_(rope_t[:, 1], rope_t[:, 1], 12582912.0, ALU.subtract))
            part1 = 6.28125
            part2 = 2029.0 / 2 ** 20
            part3 = 2 * np.pi - part1 - part2
            for c in (part1, part2, part3):
                link(ts_(rope_t[:, 2], rope_t[:, 1], c, ALU.mult))
                link(tt_(rope_t[:, 0], rope_t[:, 0], rope_t[:, 2], ALU.subtract))
            link(ts_(rope_t[:, 4], rope_t[:, 0], np.pi / 2, ALU.add))
            link(ts_(rope_t[:, 3], rope_t[:, 4], float(np.pi), ALU.is_gt, 2 * np.pi, ALU.mult))
            link(tt_(rope_t[:, 4], rope_t[:, 4], rope_t[:, 3], ALU.subtract))
            link(dve.tensor_copy(rope_t[:, 5], rope_t[:, 0]))
            top = 3.1415925
            link(ts_(rope_t[:, 4:6], rope_t[:, 4:6], top, ALU.min, -top, ALU.max))
            dve.sem_inc(S["rope_in"], 1)

            def finish_norm(v, use, out3, gain=None):
                dve.wait_ge(std_ready, v + 1)
                link(dve.reciprocal(st[:, 6:8], st[:, 2:4]))
                for tt in range(TT):
                    ins = ts_(out3[:, tt, :], x[:, tt, :], st[:, 6 + tt:7 + tt], ALU.mult)
                return ins

            def rest_T(turns, colfn, use):
                for h, (pair, value) in enumerate(turns):
                    dve.wait_ge(aux_ready[pair], value)
                    for k in range(4):
                        kk = 4 * h + k
                        if k % 2 == 0:
                            dve.wait_ge(hT_hi_ready, use * KT + (kk + 2))
                        src = aux[pair][:, k * 256:(k + 1) * 256]
                        hi_ = hT_hi[:, kk, :].bitcast(F32)
                        if colfn is None:
                            ins = tt_(hT_lo[:, kk, :], src, hi_, ALU.subtract)
                        else:
                            ins = dve.scalar_tensor_tensor(out=hT_lo[:, kk, :], in0=src, scalar=colfn(kk), in1=hi_,
                                                           op0=ALU.mult, op1=ALU.subtract)
                        ins.then_inc(hT_lo_ready, 1)
                    dve.wait_ge(hT_lo_ready, use * KT + (4 * h + 4))
                    dve.sem_inc(aux_free[pair], 1)

            def mask_of(u, block2):
                if u == 0:
                    return amask[:, 1:2, :].broadcast_to([P, 8, P])
                m = amask[:, 2:4, :] if block2 else amask[:, 0:2, :]
                return m.rearrange("p a b -> p (a b)").unsqueeze(1).broadcast_to([P, 4, 256])

            def softmax_in(u, n, turn, sinks):
                nh = 8 if u == 0 else 4
                a = a_at(u)
                pair, value = turn
                dve.wait_ge(aux_ready[pair], value)
                if u == 2:
                    dve.wait_ge(S["pT_ready"], n * 3 + 1)
                dve.wait_ge(S["amask_ready"], 1)
                src = aux[pair][:, :].rearrange("p (h k) -> p h k", h=nh)
                dst = s_ring[:, u % 2, :].rearrange("p (h k) -> p h k", h=nh)
                ins = tt_(dst, src, mask_of(u, sinks is None), ALU.add)
                release(ins, aux_free[pair], value)
                link(dve.tensor_reduce(ast[:, 0, a:a + nh], dst, AX, ALU.max))
                if sinks is not None:
                    hs = sinks[:, 0:8] if u == 0 else sinks[:, 4 * (u - 1):4 * u]
                    link(tt_(ast[:, 0, a:a + nh], ast[:, 0, a:a + nh], hs, ALU.max))
                link(ts_(ast[:, 1, a:a + nh], ast[:, 0, a:a + nh], -1.0, ALU.mult))
                if sinks is not None:
                    link(tt_(ast[:, 3, a:a + nh], hs, ast[:, 1, a:a + nh], ALU.add))
                    dve.sem_inc(S["sinkexp_in"], 1)
                dve.sem_inc(S["S_ready"], 1)

            def softmax_out(u, n, turn, sinks, gate):
                nh = 8 if u == 0 else 4
                a = a_at(u)
                h0 = 0 if u == 0 else 4 * (u - 1)
                tt = 0 if u == 0 else 1
                dve.wait_ge(S["p_ready"], n * 3 + (u + 1))
                if sinks is not None:
                    dve.wait_ge(S["sinkexp_ready"], n * 3 + (u + 1))
                    link(tt_(ast[:, 2, a:a + nh], ast[:, 2, a:a + nh], ast[:, 4, a:a + nh], ALU.add))
                link(dve.reciprocal(ast[:, 0, a:a + nh], ast[:, 2, a:a + nh]))
                pair, value = turn
                dve.wait_ge(aux_ready[pair], value)
                dst = a_tok[:, tt, h0 * 64:(h0 + nh) * 64]
                ins = tt_(dst.rearrange("p (h d) -> p h d", h=nh),
                          aux[pair][:, 0:nh * 64].rearrange("p (h d) -> p h d", h=nh),
                          ast[:, 0, a:a + nh].unsqueeze(2).broadcast_to([P, nh, 64]), ALU.mult)
                release(ins, aux_free[pair], value)
                if gate is not None:
                    link(tt_(dst, dst, gate[:, tt, h0 * 64:(h0 + nh) * 64], ALU.mult))
                if u == 2:
                    dve.sem_inc(S["a_ready"], 1)

            def gated(turn, done, gate, c, first):
                pair, value = turn
                dve.wait_ge(tile_done, done)
                src = mm[pair][:, :].rearrange("p (t n) -> p t n", t=TT)
                cs = slice(c * W, (c + 1) * W)
                if first:
                    ins = tt_(xm3[:, :, cs], gate[:, :, cs], src, ALU.mult)
                    release(ins, mm_free[pair], value)
                else:
                    ins = tt_(gate[:, :, cs], gate[:, :, cs], src, ALU.mult)
                    release(ins, mm_free[pair], value)
                    link(tt_(xm3[:, :, cs], xm3[:, :, cs], gate[:, :, cs], ALU.add))

            def add_x(turn, done, c):
                pair, value = turn
                dve.wait_ge(tile_done, done)
                cs = slice(c * W, (c + 1) * W)
                ins = tt_(x[:, :, cs], x[:, :, cs], mm[pair][:, :].rearrange("p (t n) -> p t n", t=TT), ALU.add)
                release(ins, mm_free[pair], value)

            def make_level_masks():
                count = [0]

                def hold(ins):
                    count[0] += 1
                    ins.then_inc(S["mask_chain"], 1)
                    dve.wait_ge(S["mask_chain"], count[0])

                dve.wait_ge(S["iota_ready"], 2)
                same, later = [blk[0], blk[1]], blk[3]
                hold(tt_(same[0], iota_t, iota_s, ALU.is_equal))
                hold(dve.tensor_copy(lmask[:, 0, :], same[0]))
                hold(tt_(later, iota_t, iota_s, ALU.is_gt))
                for j in range(1, LEVELS + 1):
                    hold(dve.tensor_scalar(iota_t, iota_t, 1, None, ALU.logical_shift_right))
                    hold(dve.tensor_scalar(iota_s, iota_s, 1, None, ALU.logical_shift_right))
                    hold(tt_(same[j % 2], iota_t, iota_s, ALU.is_equal))
                    hold(tt_(blk[2], same[j % 2], same[1 - j % 2], ALU.subtract))
                    hold(tt_(lmask[:, j, :], blk[2], later, ALU.mult))
                dve.sem_inc(S["lmask_ready"], 1)

            link(dve.memset(acc[:], 0.0))
            dve.sem_clear(S["dve_chain"])
            with dve.Fori(0, 2) as L:
                chain[0] = 0
                link(dve.tensor_copy(lcols[:].unsqueeze(1), lcols_all[:, bass.ds(L, 1), :]))
                dve.sem_inc(S["layer_cols"], 1)
                sinks = lcols[:, LAYER_COLS - 8:LAYER_COLS]
                ins = finish_norm(L, L * 2, xm3)
                ins.then_inc(src_ready, 1)
                rest_T([AUX1.turn("N0", L), AUX1.turn("N1", L)], lambda k: lcols[:, k:k + 1], L * 2)

                def tok_out(name, dst, event):
                    pair, value = MM1.turn(name, L)
                    dve.wait_ge(tile_done, L * NT1 + (LAST1[name] + RING + 1))
                    ins = dve.tensor_copy(dst, mm[pair][:, :])
                    release(ins, mm_free[pair], value, event)

                def f_clamp():
                    pair, value = AUX1.turn("F", L)
                    dve.wait_ge(aux_ready[pair], value)
                    ins = ts_(fT, aux[pair][:, :], GATE_FLOOR, ALU.max)
                    release(ins, aux_free[pair], value, S["fT_ready"])

                def scan():
                    dve.wait_ge(S["sig_ready"], L + 1)
                    for h in range(4):
                        c = slice(h * 256, (h + 1) * 256)
                        ins = ts_(kTh[:, c], kTh[:, c], lcols[:, 12 + h:13 + h], ALU.mult)
                    ins.then_inc(S["kTh_ready"], 1)
                    dve.wait_ge(S["log_ready"], L + 1)
                    for h in range(4):
                        c = slice(h * 256, (h + 1) * 256)
                        ins = dve.tensor_tensor_scan(pre[:, c], segment[:], logf[:, c], 0.0, ALU.mult, ALU.add)
                    link(ins)

                def level_diffs(j):
                    m = 1 << (j - 1)
                    e = E[(j - 1) % 2]
                    if j < 8:
                        pv_ = pre[:, :].rearrange("p (n two m) -> p n two m", two=2, m=m)
                        ev = e.rearrange("p (n two m) -> p n two m", two=2, m=m)
                        nb = 1024 // (2 * m)
                        mid = pv_[:, :, 0, m - 1:m].broadcast_to([P, nb, m])
                        tt_(ev[:, :, 0, :], mid, pv_[:, :, 0, :], ALU.subtract)
                        if j < 7:
                            ins = tt_(ev[:, :, 1, :], pv_[:, :, 1, :], mid, ALU.subtract)
                        else:
                            ins = dve.tensor_copy(ev[:, :, 1, :], pv_[:, :, 1, :])
                    else:
                        pv_ = pre[:, :].rearrange("p (h c m) -> p h c m", h=4, c=4)
                        ev = e.rearrange("p (h c m) -> p h c m", h=4, c=4)

                        def ends(c):
                            return pv_[:, :, c, 63:64]
                        link(tt_(hst[:, 24:28].unsqueeze(2), ends(0), ends(1), ALU.add))
                        tt_(ev[:, :, 0, :], hst[:, 24:28].unsqueeze(2).broadcast_to([P, 4, 64]), pv_[:, :, 0, :], ALU.subtract)
                        tt_(ev[:, :, 1, :], ends(1).broadcast_to([P, 4, 64]), pv_[:, :, 1, :], ALU.subtract)
                        dve.tensor_copy(ev[:, :, 2, :], pv_[:, :, 2, :])
                        ins = tt_(ev[:, :, 3, :], ends(2).broadcast_to([P, 4, 64]), pv_[:, :, 3, :], ALU.add)
                    ins.then_inc(S["D_ready"], 1)

                def level_factors(j):
                    m = 1 << (j - 1)
                    e = E[(j - 1) % 2]
                    dve.wait_ge(S["E_ready"], L * 8 + j)
                    if j == 1:
                        dve.wait_ge(S["kTh_ready"], L + 1)
                        dve.wait_ge(S["qTh_ready"], L + 1)

                    def half(t, i):
                        return t.rearrange("p (n two m) -> p n two m", two=2, m=m)[:, :, i, :]
                    tt_(half(e, 0), half(e, 0), half(kTh[:, :], 0), ALU.mult)
                    tt_(half(e, 1), half(e, 1), half(qTh[:, :], 1), ALU.mult).then_inc(S["W_ready"], 1)

                def take_level(j):
                    pair, value = AUX1.turn(f"L{j}", L)
                    dve.wait_ge(aux_ready[pair], value)
                    dve.sem_inc(S["level_seen"], 1)
                    ins = dve.copy_predicated(acc[:, :].rearrange("p (i t) -> p i t", i=8),
                                              lmask[:, j:j + 1, :].broadcast_to([P, 8, P]),
                                              aux[pair][:, :].rearrange("p (i t) -> p i t", i=8))
                    release(ins, aux_free[pair], value, S["acc_ready"] if j == 7 else None)

                def levels(j, take=True):
                    level_diffs(j)
                    if take:
                        take_level(j - 1)
                    level_factors(j)

                def q_rope():
                    pair, value = MM1.turn("q", L)
                    dve.wait_ge(tile_done, L * NT1 + (LAST1["q"] + RING + 1))
                    for tt in range(TT):
                        for a in range(2):
                            ins = dve.tensor_copy(qk[:, tt, 0:8, :].rearrange("p (j g) d -> p g j d", g=2)[:, a],
                                                  mm[pair][:, tt * W + a * 256:tt * W + (a + 1) * 256].rearrange("p (j d) -> p j d", j=4))
                    ins.then_inc(mm_free[pair], 1)

                def kv_rope():
                    pair, value = MM1.turn("kv", L)
                    dve.wait_ge(tile_done, L * NT1 + (LAST1["kv"] + RING + 1))
                    link(dve.tensor_copy(qk[:, :, 8:10, :].rearrange("p t h d -> p t (h d)"),
                                         mm[pair][:, :].rearrange("p (t n) -> p t n", t=TT)[:, :, 0:P]))
                    dve.wait_ge(S["rope_sin"], 1)
                    x1, x2 = qk[:, :, :, 0:8], qk[:, :, :, 8:16]
                    cos, sin = (rope[:, i, :, :].unsqueeze(2).broadcast_to([P, TT, 10, 8]) for i in range(2))
                    tt_(rt[:, 0], x1, cos, ALU.mult)
                    tt_(rt[:, 1], x2, sin, ALU.mult)
                    tt_(rt[:, 2], x2, cos, ALU.mult)
                    link(tt_(rt[:, 3], x1, sin, ALU.mult))
                    tt_(x1, rt[:, 0], rt[:, 1], ALU.subtract)
                    tt_(x2, rt[:, 2], rt[:, 3], ALU.add).then_inc(S["qk_ready"], 1)
                    dve.wait_ge(S["v_ready"], L + 1)
                    dve.sem_inc(mm_free[pair], 1)

                def hgrn_norm():
                    pair, value = AUX1.turn("OH", L)
                    dve.wait_ge(S["osq_ready"], L + 1)
                    link(dve.tensor_reduce(hst[:, 0:8], E[0].rearrange("p (a b) -> p a b", a=8), AX, ALU.add))
                    dve.sem_inc(S["oss_ready"], 1)
                    dve.wait_ge(S["ostd_ready"], L + 1)
                    link(dve.reciprocal(hst[:, 16:24], hst[:, 8:16]))
                    dve.wait_ge(aux_ready[pair], value)
                    ins = tt_(b_tok[:, :].rearrange("p (a b) -> p a b", a=8), aux[pair][:, :].rearrange("p (a b) -> p a b", a=8),
                              hst[:, 16:24].unsqueeze(2).broadcast_to([P, 8, P]), ALU.mult)
                    release(ins, aux_free[pair], value)
                    dve.wait_ge(S["g_ready"], L + 1)
                    tt_(b_tok[:], b_tok[:], g[:, :, :].rearrange("p a b -> p (a b)"), ALU.mult).then_inc(S["b_ready"], 1)

                def b_rest():
                    pair, value = AUX1.turn("BT", L)
                    dve.wait_ge(aux_ready[pair], value)
                    dve.wait_ge(S["bT_hi_ready"], L + 1)
                    ins = dve.scalar_tensor_tensor(out=bT_lo[:, :, :].rearrange("p a b -> p (a b)"), in0=aux[pair][:, :],
                                                   scalar=lcols[:, 16:17],
                                                   in1=bT_hi[:, :, :].rearrange("p a b -> p (a b)").bitcast(F32),
                                                   op0=ALU.mult, op1=ALU.subtract)
                    release(ins, aux_free[pair], value, S["bT_lo_ready"])

                def a_rest():
                    pair, value = AUX1.turn("AT", L)
                    dve.wait_ge(aux_ready[pair], value)
                    dve.wait_ge(S["aT_hi_ready"], L + 1)
                    ins = tt_(aT_lo[:, :, :].rearrange("p a b -> p (a b)"), aux[pair][:, :],
                              aT_hi[:, :, :].rearrange("p a b -> p (a b)").bitcast(F32), ALU.subtract)
                    release(ins, aux_free[pair], value, S["aT_lo_ready"])

                def wait_z():
                    dve.wait_ge(S["z_ready"], L + 1)

                def unit_in(u):
                    softmax_in(u, L, AUX1.turn(f"S{u}", L), sinks)

                def unit_out(u):
                    softmax_out(u, L, AUX1.turn(f"V{u}", L), sinks, z)

                steps = {
                    2: [lambda: tok_out("fh", E[0], S["ftok_ready"])], 3: [f_clamp],
                    4: [lambda: tok_out("qh", E[1], S["qhtok_ready"]), scan],
                    7: [lambda: levels(1)],
                    8: [q_rope, lambda: levels(2)], 9: [lambda: levels(3)], 10: [kv_rope, lambda: levels(4)],
                    11: [lambda: levels(5)],
                    12: [wait_z, lambda: levels(6)],
                    13: [lambda: unit_in(0), lambda: levels(7)],
                    14: [lambda: unit_in(1), lambda: levels(8)],
                    15: [],
                    16: [lambda: unit_out(0), lambda: unit_in(2)], 17: [hgrn_norm],
                    18: [lambda: unit_out(1)],
                    20: [lambda: unit_out(2), b_rest], 21: [a_rest],
                    23: [lambda: (dve.wait_ge(S["gate_ready"], L * 4 + 4), gated(MM1.turn("a0", L), L * NT1 + (LAST1["a0"] + RING + 1), ga, 0, True))],
                    24: [lambda: gated(MM1.turn("a1", L), L * NT1 + (LAST1["a1"] + RING + 1), ga, 1, True)],
                    25: [lambda: gated(MM1.turn("b0", L), L * NT1 + (LAST1["b0"] + RING + 1), gb, 0, False)],
                    26: [lambda: gated(MM1.turn("b1", L), L * NT1 + (LAST1["b1"] + RING + 1), gb, 1, False), lambda: dve.sem_inc(src_ready, 1),
                         lambda: rest_T([AUX1.turn("M0", L), AUX1.turn("M1", L)], None, L * 2 + 1)],
                    28: [lambda: add_x(MM1.turn("o0", L), L * NT1 + (LAST1["o0"] + RING + 1), 0)], 30: [lambda: add_x(MM1.turn("o1", L), L * NT1 + (LAST1["o1"] + RING + 1), 1),
                                                                    lambda: dve.sem_inc(x_ready, 1)],
                }
                for i in range(1, NT1 + 1):
                    if i == 5:
                        with dve.If(L < 1):
                            make_level_masks()
                    for f in steps.get(i, ()):
                        f()
                dve.sem_clear(S["dve_chain"])

            chain[0] = 0
            dve.wait_ge(in_fw, 16)
            link(finish_norm(2, None, x))
            link(tt_(x[:, :, :], x[:, :, :], fw.unsqueeze(1).broadcast_to([P, TT, D]), ALU.mult))
            dve.sem_inc(x_ready, 1)
            finish_norm(3, 4, xm3).then_inc(src_ready, 1)
            rest_T([AUX2.turn("N0"), AUX2.turn("N1")], lambda k: cols[:, COL_AT["attn_norm"] + k:COL_AT["attn_norm"] + k + 1], 4)
            for part, (w, hi_, lo_) in enumerate(((wf, wf_hi, wf_lo), (wr, wr_hi, wr_lo))):
                dve.wait_ge(S["wf_hi_ready"], part + 1)
                tt_(lo_[:], w[:], hi_[:].bitcast(F32), ALU.subtract).then_inc(S["wf_lo_ready"], 1)

            def forget_gate():
                pair, value = AUX2.turn("FL")
                dve.wait_ge(aux_ready[pair], value)
                ins = tt_(lf[:, 0], aux[pair][:, :].rearrange("p (t n) -> p t n", t=TT)[:, :, 0:8],
                          bias[:, 0:8].unsqueeze(1).broadcast_to([P, TT, 8]), ALU.add)
                release(ins, aux_free[pair], value)
                link(ts_(lf[:, 2], lf[:, 0], -1.0, ALU.mult))
                tt_(lf[:, 1], lf[:, 0], lf[:, 2], ALU.max).then_inc(S["lf_in"], 1)
                link(dve.memset(lfw[:], 0.0))
                link(ts_(lf[:, 0], lf[:, 0], 0.0, ALU.min))
                dve.wait_ge(S["lf_exp"], 1)
                for c in (0, 64):
                    ins = tt_(lfw[:, :, c:c + 8], lf[:, 0], lf[:, 1], ALU.subtract)
                ins.then_inc(S["lf_ready"], 1)

            def take_cT():
                pair, value = AUX2.turn("CT")
                dve.wait_ge(aux_ready[pair], value)
                ins = dve.tensor_copy(cT[:], aux[pair][:, 0:256])
                release(ins, aux_free[pair], value, S["cT_ready"])

            def head_norm(i, name, dst):
                pair, value = MM2.turn(name)
                dve.wait_ge(S["qsq_ready"], i + 1)
                link(dve.tensor_reduce(st[:, 8:24], E[0].rearrange("p (a b) -> p a b", b=64), AX, ALU.add))
                dve.sem_inc(S["qss_ready"], 1)
                dve.wait_ge(S["qstd_ready"], i + 1)
                link(dve.reciprocal(st[:, 40:56], st[:, 24:40]))
                for tt in range(TT):
                    for a in range(2):
                        c = tt * W + a * 256
                        ins = tt_(dst[:, tt * W:(tt + 1) * W].rearrange("p (j g d) -> p g j d", g=2, d=64)[:, a],
                                  mm[pair][:, c:c + 256].rearrange("p (j d) -> p j d", d=64),
                                  st[:, 40 + 8 * tt + 4 * a:44 + 8 * tt + 4 * a].unsqueeze(2).broadcast_to([P, 4, 64]), ALU.mult)
                release(ins, mm_free[pair], value, S["q2_ready"])

            def make_u():
                pair, value = MM2.turn("cu")
                dve.wait_ge(S["cc_ready"], 1)
                dve.wait_ge(tile_done, LAST2["cu"] + RING + 1)
                ins = tt_(g[:], z[:], mm[pair][:, :].rearrange("p (t n) -> p t n", t=TT), ALU.mult)
                release(ins, mm_free[pair], value, S["u_ready"])

            def conv():
                dve.memset(uT[:, :, 0:2], 0.0)
                pair, value = AUX2.turn("UT")
                dve.wait_ge(aux_ready[pair], value)
                ins = dve.tensor_copy(uT[:, :, 2:258], aux[pair][:, :].rearrange("p (c t) -> p c t", c=4))
                release(ins, aux_free[pair], value, S["uT_ready"])
                y = kTh[:, :].rearrange("p (c t) -> p c t", c=4)
                for j in range(3):
                    for c in range(4):
                        k = COL_AT["conv"] + 4 * j + c
                        if j == 0:
                            ins = ts_(y[:, c], uT[:, c, 0:256], cols[:, k:k + 1], ALU.mult)
                        else:
                            ins = dve.scalar_tensor_tensor(out=y[:, c], in0=uT[:, c, j:j + 256], scalar=cols[:, k:k + 1],
                                                           in1=y[:, c], op0=ALU.mult, op1=ALU.add)
                    link(ins)

            def conv_gate():
                pair, value = AUX2.turn("CB")
                dve.wait_ge(aux_ready[pair], value)
                ins = tt_(kTh[:], kTh[:], aux[pair][:, :], ALU.mult)
                release(ins, aux_free[pair], value, S["y_ready"])
                dve.wait_ge(S["bT_hi_ready"], 3)
                tt_(bT_lo[:, :, :].rearrange("p a b -> p (a b)"), kTh[:],
                    bT_hi[:, :, :].rearrange("p a b -> p (a b)").bitcast(F32), ALU.subtract).then_inc(S["bT_lo_ready"], 1)

            def a_rest(lo_, hi_, name, width, n, event):
                pair, value = AUX2.turn(name)
                dve.wait_ge(aux_ready[pair], value)
                dve.wait_ge(S["aT_hi_ready"], n)
                ins = tt_(lo_.rearrange("p a b -> p (a b)"), aux[pair][:, 0:width],
                          hi_.rearrange("p a b -> p (a b)").bitcast(F32), ALU.subtract)
                release(ins, aux_free[pair], value, event)

            def unit_in(u):
                softmax_in(u, 2, AUX2.turn(f"S{u}"), None)

            def unit_out(u):
                softmax_out(u, 2, AUX2.turn(f"V{u}"), None, None)

            steps = {
                1: [forget_gate], 2: [lambda: head_norm(0, "q", a_tok[:, :, :].rearrange("p a b -> p (a b)"))],
                3: [take_cT], 4: [lambda: head_norm(1, "k", k2[:, :])],
                7: [lambda: unit_in(0)], 8: [lambda: unit_in(1)],
                10: [make_u, lambda: unit_out(0), lambda: unit_in(2)],
                12: [lambda: unit_out(1)], 14: [lambda: unit_out(2)], 15: [conv], 16: [conv_gate],
                18: [lambda: a_rest(aT_lo[:, :, :], aT_hi[:, :, :], "AT", 1024, 3, S["aT_lo_ready"])],
                21: [lambda: (dve.wait_ge(S["gate_ready"], 12), gated(MM2.turn("b0"), LAST2["b0"] + RING + 1, gb, 0, True))],
                22: [lambda: gated(MM2.turn("b1"), LAST2["b1"] + RING + 1, gb, 1, True)],
                23: [lambda: gated(MM2.turn("a0"), LAST2["a0"] + RING + 1, ga, 0, False)],
                24: [lambda: gated(MM2.turn("a1"), LAST2["a1"] + RING + 1, ga, 1, False), lambda: dve.sem_inc(src_ready, 1),
                     lambda: a_rest(aT_lo[:, 2:4, :], aT_hi[:, 2:4, :], "PT", 512, 4, S["pT_lo_ready"]),
                     lambda: rest_T([AUX2.turn("M0"), AUX2.turn("M1")], None, 5)],
                26: [lambda: add_x(MM2.turn("o0"), LAST2["o0"] + RING + 1, 0)],
                28: [lambda: add_x(MM2.turn("o1"), LAST2["o1"] + RING + 1, 1), lambda: dve.sem_inc(x_ready, 1)],
            }
            for i in range(1, NT2 + 1):
                for f in steps.get(i, ()):
                    f()

            finish_norm(4, 6, xm3).then_inc(src_ready, 1)
            rest_T([AUX2.turn("R0"), AUX2.turn("R1")], lambda k: cols[:, COL_AT["ffn_norm"] + k:COL_AT["ffn_norm"] + k + 1], 6)
            pair, value = AUX2.turn("RL")
            dve.wait_ge(aux_ready[pair], value)
            logits = moe[:, 0]
            ins = tt_(logits, aux[pair][:, :].rearrange("p (t n) -> p t n", t=TT)[:, :, 0:20],
                      bias[:, 8:28].unsqueeze(1).broadcast_to([P, TT, 20]), ALU.add)
            release(ins, aux_free[pair], value)
            order = moe[:, 1, :, 0:4]
            for j in range(4):
                link(dve.memset(order[:, :, j:j + 1], 4.0 - j))

            def top1(values, mx, onehot, scratch):
                link(dve.tensor_reduce(mx, values, AX, ALU.max))
                link(tt_(scratch, values, mx.unsqueeze(2).broadcast_to([P, TT, 4]), ALU.is_equal))
                link(tt_(scratch, scratch, order, ALU.mult))
                link(dve.tensor_reduce(mx2, scratch, AX, ALU.max))
                link(tt_(onehot, scratch, mx2.unsqueeze(2).broadcast_to([P, TT, 4]), ALU.is_equal))

            gl = logits[:, :, 0:4]
            el = logits[:, :, 4:20]
            gmax = moe[:, 4, :, 0]
            mx2 = moe[:, 4, :, 1]
            emax = moe[:, 4, :, 2]
            ghot = moe[:, 5, :, 0:4]
            scr = moe[:, 5, :, 4:8]
            top1(gl, gmax, ghot, scr)
            link(tt_(moe[:, 6, :, 0:16].rearrange("p t (g e) -> p t g e", g=4)[:, 0],
                     el[:, 0].rearrange("p (g e) -> p g e", g=4), ghot[:, 0].unsqueeze(2).broadcast_to([P, 4, 4]), ALU.mult))
            link(tt_(moe[:, 6, :, 0:16].rearrange("p t (g e) -> p t g e", g=4)[:, 1],
                     el[:, 1].rearrange("p (g e) -> p g e", g=4), ghot[:, 1].unsqueeze(2).broadcast_to([P, 4, 4]), ALU.mult))
            ein = moe[:, 7, :, 0:4]
            link(tt_(ein, moe[:, 6, :, 0:4], moe[:, 6, :, 4:8], ALU.add))
            link(tt_(ein, ein, moe[:, 6, :, 8:12], ALU.add))
            link(tt_(ein, ein, moe[:, 6, :, 12:16], ALU.add))
            hot1, hot2, left = moe[:, 7, :, 4:8], moe[:, 7, :, 8:12], moe[:, 7, :, 12:16]
            top1(ein, emax, hot1, scr)
            m2 = moe[:, 4, :, 3]
            link(ts_(left, hot1, -3e38, ALU.mult))
            link(tt_(left, left, ein, ALU.add))
            top1(left, m2, hot2, scr)
            link(dve.memset(moe[:, 2], 0.0))
            link(tt_(moe[:, 2, :, 0:4], gl, gmax.unsqueeze(2).broadcast_to([P, TT, 4]), ALU.subtract))
            link(tt_(moe[:, 2, :, 4:8], ein, emax.unsqueeze(2).broadcast_to([P, TT, 4]), ALU.subtract))
            dve.sem_inc(S["logit_ready"], 1)
            dve.wait_ge(S["prob_ready"], 1)
            gexp, eexp = moe[:, 3, :, 0:4], moe[:, 3, :, 4:8]
            sums = moe[:, 8, :, 0:2]
            link(dve.tensor_reduce(moe[:, 8, :, 0], gexp, AX, ALU.add))
            link(dve.tensor_reduce(moe[:, 8, :, 1], eexp, AX, ALU.add))
            link(dve.reciprocal(moe[:, 8, :, 2:4], sums))
            link(tt_(moe[:, 9, :, 0:4], gexp, ghot, ALU.mult))
            link(dve.tensor_reduce(moe[:, 8, :, 4], moe[:, 9, :, 0:4], AX, ALU.add))
            link(tt_(moe[:, 8, :, 4:5], moe[:, 8, :, 4:5], moe[:, 8, :, 2:3], ALU.mult))
            link(tt_(moe[:, 9, :, 0:4], eexp, moe[:, 8, :, 3:4].broadcast_to([P, TT, 4]), ALU.mult))
            link(tt_(hot1, hot1, hot2, ALU.add))
            link(tt_(moe[:, 9, :, 0:4], moe[:, 9, :, 0:4], hot1, ALU.mult))
            link(dve.tensor_reduce(moe[:, 8, :, 5], moe[:, 9, :, 0:4], AX, ALU.add))
            link(dve.reciprocal(moe[:, 8, :, 6:7], moe[:, 8, :, 5:6]))
            link(tt_(moe[:, 9, :, 0:4], moe[:, 9, :, 0:4], moe[:, 8, :, 6:7].broadcast_to([P, TT, 4]), ALU.mult))
            link(tt_(moe[:, 9, :, 0:4], moe[:, 9, :, 0:4], moe[:, 8, :, 4:5].broadcast_to([P, TT, 4]), ALU.mult))
            for tt in range(TT):
                link(tt_(combine[:, tt, :].rearrange("p (g e) -> p g e", g=4), ghot[:, tt].unsqueeze(2).broadcast_to([P, 4, 4]),
                         moe[:, 9, tt, 0:4].unsqueeze(1).broadcast_to([P, 4, 4]), ALU.mult))

            def hidden(parity, weight, done):
                dve.wait_ge(S["sil_ready"], done)
                for tt in range(TT):
                    ins = dve.scalar_tensor_tensor(out=hid[:, parity, tt, :], in0=aux[0][:, tt * W + 256:(tt + 1) * W],
                                                   scalar=weight(tt), in1=sil[:, parity, tt, :], op0=ALU.mult, op1=ALU.mult)
                ins.then_inc(aux_free[0], 1)

            def eT_rest(parity, turn, done):
                dve.wait_ge(aux_ready[1], turn)
                dve.wait_ge(S["eT_hi_ready"], done)
                lo_, hi_ = (bT_lo, bT_hi) if parity else (aT_lo, aT_hi)
                ins = tt_(lo_[:, 0:2, :].rearrange("p a b -> p (a b)"), aux[1][:, 0:W],
                          hi_[:, 0:2, :].rearrange("p a b -> p (a b)").bitcast(F32), ALU.subtract)
                ins.then_inc(aux_free[1], 1)

            hidden(0, lambda tt: combine[:, tt, 0:1], 1)
            eT_rest(0, AUXM[1] + 1, 1)
            hidden(1, lambda tt: combine[:, tt, 1:2], 2)
            dve.sem_clear(S["dve_chain"])
            with dve.Fori(0, (EXPERTS - 2) // 2) as it:
                chain[0] = 0
                dve.wait_ge(aux_free[0], it * 2 + (AUXM[0] + 3))
                link(dve.tensor_copy(cnow[:], combine[:, :, bass.ds(it * 2 + 2, 2)]))
                for j in range(2):
                    e = 2 + j
                    eT_rest((e - 1) % 2, it * 2 + (AUXM[1] + e), it * 2 + e)
                    hidden(e % 2, lambda tt: cnow[:, tt, j:j + 1], it * 2 + (e + 1))
                dve.sem_clear(S["dve_chain"])
            chain[0] = 0
            eT_rest(1, AUXM[1] + EXPERTS, EXPERTS)
            for tt in range(TT):
                dve.wait_ge(tile_done, TP + RING)
                ins = tt_(x[:, tt, :], x[:, tt, :], mm[tt][:, :], ALU.add)
                release(ins, mm_free[tt], MMM[tt] + 1)
            dve.sem_inc(x_ready, 1)

            finish_norm(5, 7, xm3).then_inc(src_ready, 1)
            rest_T([(0, AUXM[0] + 1), (1, AUXP[1] + 1)], lambda k: cols[:, COL_AT["ple_norm"] + k:COL_AT["ple_norm"] + k + 1], 7)
            for c in range(2):
                dve.wait_ge(S["pg_ready"], c + 1)
                cs = slice(c * W, (c + 1) * W)
                link(tt_(ga[:, :, cs], ga[:, :, cs], pl[:, :, cs], ALU.mult))
                tt_(x[:, :, cs], x[:, :, cs], ga[:, :, cs], ALU.add).then_inc(S["final_ready"], 1)


def a_at(u):
    return (0, 8, 12)[u]


def kernel(**inputs):
    import concourse.bacc as _bacc
    from concourse.bass_utils import run_bass_kernel_spmd as _run

    nc = _bacc.Bacc("TRN2", target_bir_lowering=False, num_devices=1)
    arrays, A = {}, {}
    for name, value in inputs.items():
        a = np.ascontiguousarray(value)
        arrays[f"in_{name}"] = a
        ap = nc.dram_tensor(f"in_{name}", a.shape, mybir.dt.from_np(a.dtype), kind="ExternalInput").ap()
        if name in ("x", "positions") or name.endswith("_2"):
            ap = ap[0]
        A[name] = ap[0] if name == "p_2" else ap
    out = nc.dram_tensor("out", (1, TT * P, D), F32, kind="ExternalOutput").ap()
    build(nc, A, out[0])
    r = _run(nc, [arrays], core_ids=[0])
    return r.results[0]["out"]
```

```python
from contextlib import ExitStack

import numpy as np
import concourse.bass as bass
from concourse import mybir

F32 = mybir.dt.float32
F32R = mybir.dt.float32r
I32 = mybir.dt.int32
U8 = mybir.dt.uint8
ALU = mybir.AluOpType
ACT = mybir.ActivationFunctionType
AX = mybir.AxisListType.X

P = 128
TT = 2
D = 1024
HEAD = 64
KT = D // P
W = 512
RING = 3
EPS = 1e-6
MASKED = -1e30
LEVELS = 7
GATE_FLOOR = -43.0

B1_COLS = dict(fh=1792, qh=1280, vh=2304, q=0, kv=512, z=768, g=2816, ga0=3328, ga1=3840, gb0=4352, gb1=4864)


def group_tiles(matrix, col, width, row_tiles):
    return [(matrix, k, 4, col, width) for k in range(0, row_tiles, 4)]


B1_TILES = []
for _name, _col in B1_COLS.items():
    B1_TILES += group_tiles("w_in", _col, 256 if _name == "kv" else W, KT)
for _m in ("w_up_attn", "w_up_hgrn"):
    B1_TILES += group_tiles(_m, 0, W, 4) + group_tiles(_m, W, W, 4)
B1_TILES += group_tiles("w_out", 0, W, KT) + group_tiles("w_out", W, W, KT)
NT1 = len(B1_TILES)
assert NT1 % RING == 0

B2_COLS = dict(q=0, k=512, v=1024, cc=2056, cu=2568, cb=1544, ga0=3080, ga1=3592, gb0=4104, gb1=4616)
B2_TILES = []
for _name, _col in B2_COLS.items():
    B2_TILES += group_tiles("w_in_2", _col, W, KT)
for _m in ("w_out_conv_2", "w_out_att_2"):
    B2_TILES += group_tiles(_m, 0, W, 4) + group_tiles(_m, W, W, 4)
B2_TILES += group_tiles("w_o_2", 0, W, KT) + group_tiles("w_o_2", W, W, KT)
NT2 = len(B2_TILES)
T2 = 2 * NT1
TM = T2 + NT2
EXPERTS = 16
NTM = 3 * EXPERTS
TP = TM + NTM

JOBS1 = ["N1", "RB", "L0", "L1", "L2", "L3", "L4", "QT", "KT", "S0", "L5", "S1", "P0", "L6", "V0", "S2", "P1", "L7",
         "V1", "L8", "P2", "OH", "V2", "BT", "AT", "O0", "N0"]
JOBS2 = ["N1", "FL", "RB", "CT", "QT", "KT", "S0", "S1", "P0", "V0", "S2", "P1", "V1", "P2", "V2", "AT", "PT",
         "R0", "R1"]
GROUPS1 = list(B1_COLS) + ["a0", "a1", "b0", "b1", "o0", "o1"]
MM_GROUPS1 = [n for n in GROUPS1 if n != "o0"]
GROUPS2 = list(B2_COLS) + ["b0", "b1", "a0", "a1", "o0", "o1"]


class Turns:

    def __init__(self, names, base, first):
        self.names = names
        self.base = base
        self.first = first
        n = len(names)
        self.per = [(n + (p == first)) // 2 for p in range(2)]

    def turn(self, name, layer=0):
        i = self.names.index(name)
        pair = (self.first + i) % 2
        return pair, layer * self.per[pair] + self.base[pair] + i // 2 + 1


def last_tiles(names, tiles, first):
    at, out = first, {}
    for name in names:
        at += 1 if name[0] in "ab" and name[1:] in ("0", "1") else 2
        out[name] = at - 1
    assert at == first + len(tiles)
    return out


AUX1 = Turns(JOBS1, [0, 1], 1)
AUX2 = Turns(JOBS2, [AUX1.base[p] + 2 * AUX1.per[p] for p in range(2)], 1)
MM1 = Turns(MM_GROUPS1, [0, 0], 0)
MM2 = Turns(GROUPS2, [2 * n for n in MM1.per], 0)
LAST1 = last_tiles(GROUPS1, B1_TILES, 0)
LAST2 = last_tiles(GROUPS2, B2_TILES, T2)
RL = (1, AUX2.turn("R1")[1] + 1)
AUXM = [AUX2.base[0] + AUX2.per[0], RL[1]]
MMM = [MM2.base[p] + MM2.per[p] + (p == 0) for p in range(2)]
AUXP = [AUXM[0] + EXPERTS, AUXM[1] + EXPERTS]

COLS = ["norm_w", "attn_norm", "final_norm", "lb", "hgrn", "ffn_norm", "ple_norm", "conv", "q_gain", "k_gain"]
COL_COUNT = dict(norm_w=2 * KT, attn_norm=KT, final_norm=KT, lb=2 * 4, hgrn=2, ffn_norm=KT,
                 ple_norm=KT, conv=3 * 4, q_gain=1, k_gain=1)
COL_AT, _n = {}, 0
for _c in COLS:
    COL_AT[_c] = _n
    _n += COL_COUNT[_c]
N_COLS = _n
LAYER_COLS = 4 + 4 + 1 + 8


def build(nc, A, out):
    ctx = ExitStack()
    with ctx:
        def sb(name, shape, dt=F32):
            return ctx.enter_context(nc.sbuf_tensor("sb_" + name, shape, dt))

        def sem(name):
            return ctx.enter_context(nc.semaphore(name))

        raw = sb("raw", [P, RING, 2048])
        w_hi = sb("w_hi", [P, RING, 2048], F32R)
        w_lo = sb("w_lo", [P, RING, 2048], F32R)
        x = sb("x", [P, TT, D])
        xm = sb("xm", [P, TT * D])
        hT_hi = sb("hT_hi", [P, KT, TT * P], F32R)
        hT_lo = sb("hT_lo", [P, KT, TT * P], F32R)
        aT_hi = sb("aT_hi", [P, 4, TT * P], F32R)
        aT_lo = sb("aT_lo", [P, 4, TT * P], F32R)
        bT_hi = sb("bT_hi", [P, 4, TT * P], F32R)
        bT_lo = sb("bT_lo", [P, 4, TT * P], F32R)
        ga = sb("ga", [P, KT, TT * P])
        gb = sb("gb", [P, KT, TT * P])
        z = sb("z", [P, TT, W])
        g = sb("g", [P, TT, W])
        qk = sb("qk", [P, TT, 10, 64])
        a_tok = sb("a_tok", [P, TT, W])
        v_sb = sb("v_sb", [P, TT, P])
        vh = sb("vh", [P, TT, W])
        qTh = sb("qTh", [P, 1024])
        kTh = sb("kTh", [P, 1024])
        pre = sb("pre", [P, 1024])
        acc = sb("acc", [P, 1024])
        sc128 = sb("sc128", [P, 512])
        qTp = sb("qTp", [P, 1024])
        kT = sb("kT", [P, 256])
        s_ring = sb("s_ring", [P, 2, 1024])
        pT = sb("pT", [P, 1024])
        ident = sb("ident", [P, P])
        amask = sb("amask", [P, 4, P])
        lmask = sb("lmask", [P, LEVELS + 1, P], U8)
        segment = sb("segment", [P, 256])
        cols = sb("cols", [P, N_COLS])
        colrows = s_ring[0:N_COLS, 0, 0:P]
        lcols_all = sb("lcols_all", [P, 2, LAYER_COLS])
        lcols = sb("lcols", [P, LAYER_COLS])
        gains_all = sb("gains_all", [P, 3, KT])
        gain = sb("gain", [P, KT])
        r = sb("r", [P, TT])
        rB = sb("rB", [P, TT * P])
        ones = sb("ones", [P, P])
        rope = sb("rope", [P, 2, TT, 8])
        rope_t = sb("rope_t", [P, 6, TT, 8])
        pos_i = sb("pos_i", [P, TT], I32)
        st = sb("st", [P, 64])
        hst = sb("hst", [P, 32])
        ast = sb("ast", [P, 5, 16])
        rt = sb("rt", [P, 4, TT, 10, 8])
        wf = sb("wf", [P, KT, 8])
        wr = sb("wr", [P, KT, 20])
        wf_hi = sb("wf_hi", [P, KT, 8], F32R)
        wf_lo = sb("wf_lo", [P, KT, 8], F32R)
        wr_hi = sb("wr_hi", [P, KT, 20], F32R)
        wr_lo = sb("wr_lo", [P, KT, 20], F32R)
        bias = sb("bias", [P, 28])
        lf = sb("lf", [P, 3, TT, 8])
        cT = sb("cT", [P, 256])
        combine = sb("combine", [P, TT, EXPERTS])
        cnow = sb("cnow", [P, TT, 2])
        one = sb("one", [P, 4])

        E = [xm[:, 0:1024], xm[:, 1024:2048]]
        logf = s_ring[:, 0, :]
        fT = s_ring[:, 1, :]
        b_tok = qTh
        moe = pT[:, 0:12 * TT * 20].rearrange("p (a t n) -> p a t n", a=12, t=TT)
        ga_flat, gb_flat = (t[:, :, :].rearrange("p k t -> p (k t)") for t in (ga, gb))
        iota_t, iota_s = (ga_flat[:, i * P:(i + 1) * P].bitcast(I32) for i in range(2))
        blk = [ga_flat[:, i * P:(i + 1) * P].bitcast(I32) for i in range(2, 6)]
        fw = gb_flat[:, 0:D]
        diag = rt[:, 0:2].rearrange("p a t h e -> p (a t h e)")[:, 0:TT * P].rearrange("p (t n) -> p t n", t=TT)
        selneg = acc[:, :]
        tri = sc128[:, 0:256]
        uT = gb_flat[:, 0:4 * 258].rearrange("p (c t) -> p c t", c=4)
        kT2 = pre
        k2 = kTh
        lfw = qk[:, 0, 0:4, :].rearrange("p h d -> p (h d)").rearrange("p (t n) -> p t n", t=TT)
        p_tok = g[:, :, 0:256]
        pl, pg = (t.rearrange("p (t d) -> p t d", t=TT) for t in (gb_flat, ga_flat))
        sil = z[:, :, :].rearrange("p t (e n) -> p e t n", e=2)
        hid = g[:, :, :].rearrange("p t (e n) -> p e t n", e=2)

        mm = [ctx.enter_context(nc.psum_tensor(f"mm{i}", [P, 1024], F32)) for i in range(2)]
        aux = [ctx.enter_context(nc.psum_tensor(f"aux{i}", [P, 1024], F32)) for i in range(2)]

        raw_loaded = [sem(f"raw_loaded{i}") for i in range(RING)]
        hi_split, lo_split, tile_done = sem("hi_split"), sem("lo_split"), sem("tile_done")
        mm_free = [sem(f"mm_free{i}") for i in range(2)]
        aux_ready = [sem(f"aux_ready{i}") for i in range(2)]
        aux_free = [sem(f"aux_free{i}") for i in range(2)]
        in_norm_w, in_rows, in_more_rows, in_pos, in_sinks, in_small, in_fw, in_p = (
            sem(n) for n in ("in_norm_w", "in_rows", "in_more_rows", "in_pos", "in_sinks", "in_small", "in_fw", "in_p"))
        in_x = [sem(f"in_x{h}") for h in range(2)]
        x_ready, std_ready = sem("x_ready"), sem("std_ready")
        hT_hi_ready, hT_lo_ready = sem("hT_hi_ready"), sem("hT_lo_ready")
        names = ("ident_ready", "iota_ready", "amask_ready", "cols_ready", "setup_pe", "lb_in", "lb_exp",
                 "rope_in", "rope_sin", "layer_cols", "gain_now", "r_ready", "diag_ready", "qh_scaled",
                 "fT_ready", "sig_ready", "log_ready", "kTh_ready", "qTh_ready",
                 "vh_ready", "D_ready", "E_ready", "W_ready", "acc_ready", "sc128_ready",
                 "qk_ready", "v_ready", "qT_ready", "kT_ready", "S_ready", "p_ready", "sinkexp_in",
                 "sinkexp_ready", "pT_ready", "z_ready", "g_ready", "gate_in", "gate_ready", "osq_ready", "oss_ready",
                 "ostd_ready", "b_ready", "bT_hi_ready", "bT_lo_ready", "a_ready", "aT_hi_ready", "aT_lo_ready",
                 "wf_hi_ready", "wf_lo_ready", "lf_in", "lf_exp", "lf_ready", "cT_ready", "qsq_ready", "qss_ready",
                 "qstd_ready", "q2_ready", "y_ready", "x1_ready", "half_done", 
                 "pT_lo_ready", "logit_ready", "prob_ready", "sil_ready", "eT_hi_ready",
                 "pg_ready", "final_ready", "out_done", "selneg_ready", "tri_ready", "setup_chain", "level_seen", "load_begun",
                 "dve_chain", "act_chain", "pool_chain")
        S = {n: sem(n) for n in names}

        block = ctx.enter_context(nc.Block())

        def tile_width(tile):
            return tile[2] * tile[4]

        def slot(t):
            return t % RING

        rows = [("norm_w", A["norm_w"].rearrange("l (k c) -> (l k) c", c=P)),
                ("lb", A["lb_logits"].rearrange("l (k c) -> (l k) c", c=P)),
                ("hgrn", A["hgrn_norm_w"]),
                ("attn_norm", A["attn_norm_g_2"].rearrange("(k c) -> k c", c=P)),
                ("final_norm", A["final_norm_w"].rearrange("(k c) -> k c", c=P)),
                ("ffn_norm", A["ffn_norm_g_2"].rearrange("(k c) -> k c", c=P)),
                ("ple_norm", A["ple_norm_g_2"].rearrange("(k c) -> k c", c=P)),
                ("conv", A["conv_w_2"].rearrange("j (k c) -> (j k) c", c=P)),
                ("q_gain", A["q_norm_g_2"].unsqueeze(0)), ("k_gain", A["k_norm_g_2"].unsqueeze(0))]

        def load_rows(engine, some, loaded):
            for name, src in some:
                a = COL_AT[name]
                dst = colrows[a:a + COL_COUNT[name], :]
                if src.shape[1] < P:
                    dst = dst.rearrange("r (two c) -> r two c", two=2)
                    src = src.unsqueeze(1).broadcast_to([1, 2, HEAD])
                engine.dma_start(dst, src).then_inc(loaded, 16)

        def load_x(engine, h):
            c = slice(h * W, (h + 1) * W)
            engine.dma_start(x[:, :, c], A["x"].rearrange("(t p) d -> p t d", p=P)[:, :, c]).then_inc(in_x[h], 16)

        def by_feature(t, c):
            return t[:, 4 * c:4 * c + 4, :].rearrange("p k t -> p (k t)")

        @block.sync
        def _(sp):
            def load(t, halves, sofar):
                sp.wait_ge(lo_split, sofar + 1)
                sp.sem_inc(S["load_begun"], 1)
                for dst, src in halves:
                    sp.dma_start(dst, src).then_inc(raw_loaded[slot(t)], 32 // len(halves))

            def halves(t, tile, layer=None):
                matrix, k0, nk, col, width = tile
                w = A[matrix] if layer is None else A[matrix][layer]
                src = w[k0 * P:(k0 + nk) * P, col:col + width].rearrange("(k p) n -> p k n", p=P)
                dst = raw[:, slot(t), 0:nk * width].rearrange("p (k n) -> p k n", n=width)
                return [(dst[:, 0:nk // 2], src[:, 0:nk // 2]), (dst[:, nk // 2:nk], src[:, nk // 2:nk])]

            def expert_halves(t, e, part):
                if part == "down":
                    src = A["w_down_2"][e].rearrange("(k p) n -> p k n", p=P)
                    dst = raw[:, slot(t), :].rearrange("p (k n) -> p k n", n=D)
                    return [(dst[:, k], src[:, k]) for k in range(2)]
                dst = raw[:, slot(t), :].rearrange("p (k n) -> p k n", n=W)
                return [(dst[:, :, 256 * i:256 * i + 256],
                         A[m][e][part * W:(part + 1) * W, :].rearrange("(k p) n -> p k n", p=P))
                        for i, m in enumerate(("w_gate_2", "w_up_2"))]

            load_x(sp, 0)
            with sp.Fori(0, 2) as layer:
                for i in range(NT1):
                    load(i, halves(i, B1_TILES[i], layer), layer * NT1 + i)
            for a, n, src in ((0, 8, A["b_f_2"]), (8, 4, A["b_rg_2"]), (12, 16, A["b_re_2"])):
                sp.dma_start(bias[:, a:a + n], src.partition_broadcast(P)).then_inc(in_small, 16)
            sp.dma_start(wf[:], A["w_in_2"][:, 1536:1544].rearrange("(k p) n -> p k n", p=P)).then_inc(in_small, 16)
            sp.dma_start(wr[:, :, 0:4], A["w_rg_2"].rearrange("(k p) n -> p k n", p=P)).then_inc(in_small, 16)
            sp.dma_start(wr[:, :, 4:20], A["w_re_2"].rearrange("(k p) n -> p k n", p=P)).then_inc(in_small, 16)
            for i in range(NT2):
                load(T2 + i, halves(T2 + i, B2_TILES[i]), T2 + i)
                if i == 0:
                    sp.wait_ge(hT_lo_ready, 4 * KT)
                    sp.dma_start(fw, A["final_norm_w"].partition_broadcast(P)).then_inc(in_fw, 16)
                if i == 1:
                    sp.wait_ge(S["b_ready"], 2)
                    sp.dma_start(p_tok, A["p_2"].rearrange("(t p) n -> p t n", p=P)).then_inc(in_p, 16)
            for i, (e, part) in enumerate(((0, 0), (0, 1), (1, 0), (1, 1), (0, "down"))):
                load(TM + i, expert_halves(TM + i, e, part), TM + i)
            with sp.Fori(0, (EXPERTS - 2) // 2) as it:
                for j in range(2):
                    for i, (de, part) in enumerate(((2, 0), (2, 1), (1, "down"))):
                        n = 5 + 3 * j + i
                        load(TM + n, expert_halves(TM + n, it * 2 + (j + de), part), it * 6 + (TM + n))
            load(TP - 1, expert_halves(TP - 1, EXPERTS - 1, "down"), TP - 1)
            src = A["w_ple_2"].rearrange("(k p) n -> p k n", p=P)
            dst = raw[:, slot(TP), :].rearrange("p (k n) -> p k n", n=D)
            load(TP, [(dst[:, k], src[:, k]) for k in range(2)], TP)
            for i, tile in enumerate(group_tiles("w_pg_2", 0, W, KT) + group_tiles("w_pg_2", W, W, KT)):
                load(TP + 1 + i, halves(TP + 1 + i, tile), TP + 1 + i)
            for c in range(2):
                for tt in range(TT):
                    sp.wait_ge(S["final_ready"], 2 * c + tt + 1)
                    sp.dma_start(out[tt * P:(tt + 1) * P, c * W:(c + 1) * W], x[:, tt, c * W:(c + 1) * W]
                                 ).then_inc(S["out_done"], 16)
            sp.wait_ge(S["out_done"], 64)

        @block.gpsimd
        def _(pool):
            pool.sem_inc(lo_split, RING)
            pool.memset(ident[:], 0.0).then_inc(S["pool_chain"], 1)
            pool.wait_ge(S["pool_chain"], 1)
            pool.affine_select(out=ident[:], in_=ident[:], compare_op=ALU.not_equal, fill=1.0, base=0,
                               pattern=[[-1, P]], channel_multiplier=1).then_inc(S["ident_ready"], 1)
            load_rows(pool, rows[4:], in_more_rows)
            pool.dma_start(lcols_all[:, :, LAYER_COLS - 8:], A["attn_sinks"].partition_broadcast(P)).then_inc(in_sinks, 16)
            pool.iota(iota_t, pattern=[[1, P]], base=0, channel_multiplier=0).then_inc(S["iota_ready"], 1)
            pool.iota(iota_s, pattern=[[0, P]], base=0, channel_multiplier=1).then_inc(S["iota_ready"], 1)
            for b in range(4):
                i = pool.memset(amask[:, b, :], 0.0)
            i.then_inc(S["pool_chain"], 1)
            pool.wait_ge(S["pool_chain"], 2)
            pool.affine_select(out=amask[:, 0, :], in_=amask[:, 0, :], compare_op=ALU.is_gt, fill=MASKED, base=0,
                               pattern=[[1, P]], channel_multiplier=-1)
            for b in (1, 3):
                i = pool.affine_select(out=amask[:, b, :], in_=amask[:, b, :], compare_op=ALU.is_ge, fill=MASKED,
                                       base=0, pattern=[[-1, P]], channel_multiplier=1)
            i.then_inc(S["amask_ready"], 1)


            def lo(t, width, sofar, loads):
                pool.wait_ge(raw_loaded[slot(t)], loads)
                pool.wait_ge(hi_split, sofar + (RING + 1))
                pool.tensor_tensor(w_lo[:, slot(t), 0:width], raw[:, slot(t), 0:width],
                                   w_hi[:, slot(t), 0:width].bitcast(F32), ALU.subtract).then_inc(lo_split, 1)

            with pool.Fori(0, 2) as layer:
                for i in range(NT1):
                    lo(i, tile_width(B1_TILES[i]), layer * NT1 + i, layer * (32 * NT1 // RING) + 32 * (i // RING + 1))
            for t in range(T2, T2 + NT2):
                lo(t, 2048, t, 32 * (t // RING + 1))
                if t == T2:
                    pool.wait_ge(S["b_ready"], 2)
                    pool.memset(selneg, 0.0).then_inc(S["pool_chain"], 1)
                    pool.memset(tri, 1.0).then_inc(S["pool_chain"], 1)
                    pool.wait_ge(S["pool_chain"], 4)
                    sel3 = selneg.rearrange("h (g c) -> h g c", g=8)
                    pool.affine_select(out=sel3, in_=sel3, compare_op=ALU.not_equal, fill=-1.0, base=0,
                                       pattern=[[-1, 8], [0, P]], channel_multiplier=1).then_inc(S["pool_chain"], 1)
                    pool.wait_ge(S["pool_chain"], 5)
                    pool.affine_select(out=sel3, in_=sel3, compare_op=ALU.not_equal, fill=-1.0, base=-64,
                                       pattern=[[-1, 8], [0, P]], channel_multiplier=1).then_inc(S["selneg_ready"], 1)
                    pool.affine_select(out=tri[:, 0:P], in_=tri[:, 0:P], compare_op=ALU.is_ge, fill=0.0, base=0,
                                       pattern=[[1, P]], channel_multiplier=-1).then_inc(S["tri_ready"], 1)
            for t in range(TM, TM + 5):
                lo(t, 2048, t, 32 * (t // RING + 1))
            with pool.Fori(0, (EXPERTS - 2) // 2) as it:
                for n in range(TM + 5, TM + 11):
                    lo(n, 2048, it * 6 + n, it * 64 + 32 * (n // RING + 1))
            for t in range(TP - 1, TP + 5):
                lo(t, 2048, t, 32 * (t // RING + 1))

        @block.tensor
        def _(pe):
            pe.sem_inc(tile_done, RING)
            for p in range(2):
                pe.sem_inc(mm_free[p], 1)
                pe.sem_inc(aux_free[p], 1)

            def products(dst, lhs, k, tt, rhs, start, stop):
                a_hi = lhs[0][:, k, tt * P:(tt + 1) * P]
                a_lo = lhs[1][:, k, tt * P:(tt + 1) * P]
                pe.matmul(dst, a_hi, rhs[0], start=start, stop=False, skip_group_check=True)
                pe.matmul(dst, a_hi, rhs[1], start=False, stop=False, skip_group_check=True)
                return pe.matmul(dst, a_lo, rhs[0], start=False, stop=stop, skip_group_check=True)

            def tile_parts(t, n, width=2048):
                return [w[:, slot(t), 0:width].rearrange("p (k n) -> p k n", n=n) for w in (w_hi, w_lo)]

            def use_tile(t, sofar, body, n, width=2048):
                pe.wait_ge(lo_split, sofar + (RING + 1))
                body(tile_parts(t, n, width)).then_inc(tile_done, 1)

            def products_T(dst, w, k, c, acts, start, stop):
                cs = slice(c * P, (c + 1) * P)
                pe.matmul(dst, w[0][:, k, cs], acts[0][:, k, :], start=start, stop=False, skip_group_check=True)
                pe.matmul(dst, w[0][:, k, cs], acts[1][:, k, :], start=False, stop=False, skip_group_check=True)
                return pe.matmul(dst, w[1][:, k, cs], acts[0][:, k, :], start=False, stop=stop, skip_group_check=True)

            def group_T(tiles, first, sofar, acts, turn, acts_wait=None, between=None, mid=None):
                pair, value = turn
                pe.wait_ge(mm_free[pair], value)
                for j in range(len(tiles)):
                    def body(parts):
                        for k in range(4):
                            if mid is not None and j == 0 and k == 2:
                                mid()
                            if acts_wait is not None:
                                acts_wait(j * 4 + k)
                            for c in range(4):
                                last = products_T(mm[pair][:, c * 256:(c + 1) * 256], parts, k, c,
                                                  [a[:, j * 4:j * 4 + 4] for a in acts],
                                                  j == 0 and k == 0 and c % 2 == 0, j == len(tiles) - 1 and k == 3)
                        return last
                    use_tile(first + j, sofar + j, body, W)
                    if between is not None:
                        between(j)

            def group(tiles, first, sofar, lhs, turn, lhs_wait=None, between=None, mid=None, in_aux=False):
                pair, value = turn
                banks, free = (aux, aux_free) if in_aux else (mm, mm_free)
                n_tiles = len(tiles)
                for j, tile in enumerate(tiles):
                    nk, n = tile[2], tile[4]
                    if j == 0:
                        pe.wait_ge(free[pair], value)

                    def body(parts):
                        for k in range(nk):
                            if mid is not None and j == 0 and k == 2:
                                mid()
                            if lhs_wait is not None:
                                lhs_wait(j * 4 + k)
                            for tt in range(TT):
                                last = products(banks[pair][:, tt * W:tt * W + n], lhs, j * 4 + k, tt,
                                                [q[:, k, :] for q in parts], j == 0 and k == 0,
                                                j == n_tiles - 1 and k == nk - 1)
                        return last
                    use_tile(first + j, sofar + j, body, n, nk * n)
                    if between is not None:
                        between(j)

            def begin(turn):
                pair, value = turn
                pe.wait_ge(aux_free[pair], value)
                return aux[pair]

            def end(turn, last):
                last.then_inc(aux_ready[turn[0]], 1)

            def transposes(turn, blocks):
                ps = begin(turn)
                for i, b in enumerate(blocks):
                    last = pe.transpose(ps[:, i * P:(i + 1) * P], b, ident[:])
                end(turn, last)

            def x_transposes(turn, h, halves):
                if halves is not None:
                    pe.wait_ge(x_ready, halves)
                transposes(turn, [x[:, tt, k * P:(k + 1) * P] for k in range(4 * h, 4 * h + 4) for tt in range(TT)])

            def spread_r(turn, n):
                pe.wait_ge(S["diag_ready"], n)
                ps = begin(turn)
                for tt in range(TT):
                    last = pe.matmul(ps[:, tt * P:(tt + 1) * P], ones[:], diag[:, tt, :], start=True, stop=True)
                end(turn, last)

            hT, aT, bT = (hT_hi, hT_lo), (aT_hi, aT_lo), (bT_hi, bT_lo)

            def hT_part(use):
                def wait(k):
                    pe.wait_ge(hT_lo_ready, use * KT + (k + 1))
                return wait

            def score_unit(turn, u, qpart, kpart, bias2):
                ps = begin(turn)
                heads = range(8) if u == 0 else range(4 * (u - 1), 4 * u)
                keys = P if u == 0 else 2 * P
                for i, h in enumerate(heads):
                    dst = ps[:, i * keys:(i + 1) * keys]
                    qtt = 0 if u == 0 else 1
                    last = pe.matmul(dst, qpart(h, qtt), kpart(h, keys), start=True, stop=not bias2)
                    if bias2:
                        r = slice(64 * (h // 4), 64 * (h // 4) + 64)
                        last = pe.matmul(dst, selneg[r, h * P:(h + 1) * P], cT[r, 0:keys], start=False, stop=True)
                end(turn, last)

            def p_transposes(turn, u, n):
                pe.wait_ge(S["p_ready"], n * 3 + (u + 1))
                transposes(turn, [s_ring[:, u % 2, i * P:(i + 1) * P] for i in range(8)])

            def pv(turn, u, n, vpart):
                pe.wait_ge(S["pT_ready"], n * 3 + (u + 1))
                ps = begin(turn)
                if u == 0:
                    for h in range(8):
                        last = pe.matmul(ps[:, h * 64:h * 64 + 64], pT[:, h * P:(h + 1) * P], vpart(h, 0),
                                         start=True, stop=True)
                else:
                    for i in range(4):
                        for kt in range(2):
                            last = pe.matmul(ps[:, i * 64:i * 64 + 64], pT[:, (2 * i + kt) * P:(2 * i + kt + 1) * P],
                                             vpart(4 * (u - 1) + i, kt), start=kt == 0, stop=kt == 1)
                end(turn, last)

            pe.wait_ge(S["ident_ready"], 1)
            pe.wait_ge(in_norm_w, 16)
            pe.transpose(mm[1][:, 0:2 * KT], colrows[0:2 * KT, :], ident[0:2 * KT, 0:2 * KT]).then_inc(S["setup_pe"], 1)
            pe.wait_ge(in_x[0], 16)
            x_transposes((1, 1), 0, None)
            pe.wait_ge(in_rows, 16 * 3)
            pe.wait_ge(in_more_rows, 16 * 6)
            pe.transpose(mm[1][:, W:W + N_COLS], colrows, ident[0:N_COLS, 0:N_COLS]).then_inc(S["setup_pe"], 1)

            with pe.Fori(0, 2) as L:
                def job(name):
                    return AUX1.turn(name, L)

                def level(j):
                    name = f"L{j}"
                    if j == 0:
                        pe.wait_ge(S["kTh_ready"], L + 1)
                        pe.wait_ge(S["qTh_ready"], L + 1)
                    else:
                        pe.wait_ge(S["W_ready"], L * 8 + j)
                    ps = begin(job(name))
                    e = E[(j - 1) % 2]
                    if j == 8:
                        for h in range(4):
                            last = pe.matmul(ps[:, h * P:(h + 1) * P], e[:, h * 256:h * 256 + P],
                                             e[:, h * 256 + P:h * 256 + 256], start=True, stop=True)
                    else:
                        a, b = (kTh, qTh) if j == 0 else (e, e)
                        for i in range(8):
                            last = pe.matmul(ps[:, i * P:(i + 1) * P], a[:, i * P:(i + 1) * P], b[:, i * P:(i + 1) * P],
                                             start=True, stop=True)
                    end(job(name), last)

                def hgrn_out():
                    pe.wait_ge(S["acc_ready"], L + 1)
                    pe.wait_ge(S["sc128_ready"], L + 1)
                    pe.wait_ge(S["vh_ready"], L + 1)
                    ps = begin(job("OH"))
                    for h in range(4):
                        v0, v1 = (vh[:, tt, h * P:(h + 1) * P] for tt in range(2))
                        pe.matmul(ps[:, h * P:(h + 1) * P], acc[:, 2 * h * P:(2 * h + 1) * P], v0, start=True, stop=True)
                        dst = ps[:, W + h * P:W + (h + 1) * P]
                        pe.matmul(dst, acc[:, (2 * h + 1) * P:(2 * h + 2) * P], v1, start=True, stop=False)
                        last = pe.matmul(dst, sc128[:, h * P:(h + 1) * P], v0, start=False, stop=True)
                    end(job("OH"), last)

                def q_transposes():
                    pe.wait_ge(S["qk_ready"], L + 1)
                    transposes(job("QT"), [qk[:, tt, 2 * j:2 * j + 2, :].rearrange("p a b -> p (a b)")
                                           for j in range(4) for tt in range(TT)])

                def k_transposes():
                    transposes(job("KT"), [qk[:, tt, 8:10, :].rearrange("p a b -> p (a b)") for tt in range(TT)])

                def scores(u):
                    if u == 0:
                        pe.wait_ge(S["qT_ready"], L + 1)
                        pe.wait_ge(S["kT_ready"], L + 1)
                    score_unit(job(f"S{u}"), u,
                               lambda h, tt: qTp[64 * (h // 4):64 * (h // 4) + 64, (h % 4) * 256 + tt * P:(h % 4) * 256 + (tt + 1) * P],
                               lambda h, keys: kT[64 * (h // 4):64 * (h // 4) + 64, 0:keys], False)

                def pvs(u):
                    if u == 0:
                        pe.wait_ge(S["v_ready"], L + 1)
                    pv(job(f"V{u}"), u, L, lambda h, kt: v_sb[:, kt, 64 * (h // 4):64 * (h // 4) + 64])

                def b_transposes():
                    pe.wait_ge(S["b_ready"], L + 1)
                    transposes(job("BT"), [b_tok[:, tt * W + c * P:tt * W + (c + 1) * P] for c in range(4) for tt in range(TT)])

                def a_transposes():
                    pe.wait_ge(S["a_ready"], L + 1)
                    transposes(job("AT"), [a_tok[:, tt, c * P:(c + 1) * P] for c in range(4) for tt in range(TT)])

                after = {1: [lambda: spread_r(job("RB"), L + 1)], 4: [lambda: level(0)], 5: [lambda: level(1)], 6: [lambda: level(2)], 7: [lambda: level(3)],
                         9: [lambda: level(4)], 10: [q_transposes, k_transposes],
                         11: [lambda: scores(0), lambda: level(5)], 12: [lambda: scores(1)],
                         13: [lambda: p_transposes(job("P0"), 0, L), lambda: level(6)],
                         14: [lambda: pvs(0), lambda: scores(2)],
                         15: [lambda: p_transposes(job("P1"), 1, L), lambda: level(7)],
                         16: [lambda: pvs(1), lambda: level(8)],
                         17: [lambda: p_transposes(job("P2"), 2, L), hgrn_out],
                         18: [lambda: pvs(2)], 19: [b_transposes], 20: [a_transposes],
                         28: [lambda: x_transposes(job("N0"), 0, L * 2 + 3)]}

                def between_from(first):
                    def between(j):
                        for f in after.get(first + j, ()):
                            f()
                    return between

                t = 0
                for i, name in enumerate(GROUPS1[:11]):
                    form = group_T if name in ("fh", "qh", "ga0", "ga1", "gb0", "gb1") else group
                    form(B1_TILES[t:t + 2], t, L * NT1 + t, hT, MM1.turn(name, L),
                         hT_part(L * 2) if i == 0 else None, between_from(t),
                         (lambda: x_transposes(job("N1"), 1, L * 2 + 2)) if i == 0 else None)
                    if i == 0:
                        pe.wait_ge(S["cols_ready"], 1)
                    t += 2
                for i, name in enumerate(("a0", "a1", "b0", "b1")):
                    if i == 0:
                        pe.wait_ge(S["aT_lo_ready"], L + 1)
                    if i == 2:
                        pe.wait_ge(S["bT_lo_ready"], L + 1)
                    group_T(B1_TILES[t:t + 1], t, L * NT1 + t, aT if i < 2 else bT, MM1.turn(name, L))
                    t += 1
                for i, name in enumerate(("o0", "o1")):
                    group(B1_TILES[t:t + 2], t, L * NT1 + t, hT, AUX1.turn("O0", L) if i == 0 else MM1.turn(name, L),
                          hT_part(L * 2 + 1) if i == 0 else None, between_from(t), in_aux=i == 0)
                    if i == 0:
                        pe.sem_inc(aux_ready[AUX1.turn("O0")[0]], 1)
                    t += 2

            def job(name):
                return AUX2.turn(name)

            def small(turn, parts, n, wait=None):
                ps = begin(turn)
                for tt in range(TT):
                    for k in range(KT):
                        last = products(ps[:, tt * W:tt * W + n], hT, k, tt, [q[:, k, :] for q in parts], k == 0, k == KT - 1)
                end(turn, last)

            def forget_logits():
                pe.wait_ge(S["wf_lo_ready"], 1)
                small(job("FL"), (wf_hi, wf_lo), 8)

            def forget_sums():
                pe.wait_ge(S["lf_ready"], 1)
                pe.wait_ge(S["tri_ready"], 1)
                ps = begin(job("CT"))
                pe.matmul(ps[:, 0:256], lfw[:, 0, :], tri, start=True, stop=False, skip_group_check=True)
                last = pe.matmul(ps[:, P:256], lfw[:, 1, :], tri[:, 0:P], start=False, stop=True, skip_group_check=True)
                end(job("CT"), last)

            def q2_transposes():
                pe.wait_ge(S["q2_ready"], 1)
                transposes(job("QT"), [a_tok[:, tt, c * P:(c + 1) * P] for c in range(4) for tt in range(TT)])

            def k2_transposes():
                pe.wait_ge(S["q2_ready"], 2)
                transposes(job("KT"), [k2[:, tt * W + c * P:tt * W + (c + 1) * P] for c in range(4) for tt in range(TT)])

            def scores2(u):
                if u == 0:
                    pe.wait_ge(S["qT_ready"], 3)
                    pe.wait_ge(S["kT_ready"], 3)
                    pe.wait_ge(S["cT_ready"], 1)
                    pe.wait_ge(S["selneg_ready"], 1)
                score_unit(job(f"S{u}"), u,
                           lambda h, tt: qTp[64 * (h // 4):64 * (h // 4) + 64, (h % 4) * 256 + tt * P:(h % 4) * 256 + (tt + 1) * P],
                           lambda h, keys: kT2[64 * (h // 4):64 * (h // 4) + 64, (h % 4) * 256:(h % 4) * 256 + keys], True)

            def pvs2(u):
                if u == 0:
                    pe.wait_ge(S["vh_ready"], 3)
                pv(job(f"V{u}"), u, 2, lambda h, kt: vh[:, kt, h * 64:h * 64 + 64])

            def a2_transposes():
                pe.wait_ge(S["a_ready"], 3)
                transposes(job("AT"), [a_tok[:, tt, c * P:(c + 1) * P] for c in range(4) for tt in range(TT)])

            def p2_transposes():
                pe.wait_ge(in_p, 16)
                transposes(job("PT"), [p_tok[:, tt, c * P:(c + 1) * P] for c in range(2) for tt in range(TT)])

            after = {1: [forget_logits], 3: [lambda: spread_r(job("RB"), 3)], 4: [forget_sums, q2_transposes],
                     5: [k2_transposes],
                     6: [lambda: scores2(0)], 7: [lambda: scores2(1)], 8: [lambda: p_transposes(job("P0"), 0, 2)],
                     9: [lambda: pvs2(0), lambda: scores2(2)], 10: [lambda: p_transposes(job("P1"), 1, 2)],
                     11: [lambda: pvs2(1)], 12: [lambda: p_transposes(job("P2"), 2, 2)],
                     13: [lambda: pvs2(2)], 15: [a2_transposes],
                     23: [p2_transposes], 26: [lambda: x_transposes(job("R0"), 0, 7)]}

            def between_from(first):
                def between(j):
                    for f in after.get(first + j, ()):
                        f()
                return between

            t = 0
            for i, name in enumerate(GROUPS2[:10]):
                form = group if name in ("q", "k", "v") else group_T
                form(B2_TILES[t:t + 2], T2 + t, T2 + t, hT, MM2.turn(name), hT_part(4) if i == 0 else None,
                     between_from(t), (lambda: x_transposes(job("N1"), 1, 6)) if i == 0 else None)
                t += 2
            for i, name in enumerate(("b0", "b1", "a0", "a1")):
                if i == 0:
                    pe.wait_ge(S["bT_lo_ready"], 3)
                if i == 2:
                    pe.wait_ge(S["aT_lo_ready"], 3)
                group_T(B2_TILES[t:t + 1], T2 + t, T2 + t, bT if i < 2 else aT, MM2.turn(name), between=between_from(t))
                t += 1
            for i, name in enumerate(("o0", "o1")):
                group(B2_TILES[t:t + 2], T2 + t, T2 + t, hT, MM2.turn(name), hT_part(5) if i == 0 else None,
                      between_from(t))
                t += 2

            def router_logits():
                pe.wait_ge(S["wf_lo_ready"], 2)
                small(RL, (wr_hi, wr_lo), 20)

            def gate_up(t, sofar, part, turn, hT_wait=None, mid=None, mid_k=2, dst=aux[0]):
                if turn is not None:
                    pe.wait_ge(aux_free[0], turn)

                def body(parts):
                    for k in range(4):
                        if hT_wait is not None:
                            hT_wait(4 * part + k)
                        if mid is not None and k == mid_k:
                            mid()
                        for tt in range(TT):
                            last = products(dst[:, tt * W:(tt + 1) * W], hT, 4 * part + k, tt,
                                            [q[:, k, :] for q in parts], part == 0 and k == 0, part == 1 and k == 3)
                    return last
                use_tile(t, sofar, body, W)

            def expert_transposes(parity, turn, hidden_turn):
                pe.wait_ge(aux_free[0], hidden_turn + 1)
                pe.wait_ge(aux_free[1], turn)
                for i, (c, tt) in enumerate((c, tt) for c in range(2) for tt in range(TT)):
                    last = pe.transpose(aux[1][:, i * P:(i + 1) * P], hid[:, parity, tt, c * P:(c + 1) * P], ident[:])
                last.then_inc(aux_ready[1], 1)

            def down(t, sofar, parity, turn, first=False, final=False):
                pe.wait_ge(aux_free[1], turn + 1)
                lhs = bT if parity else aT

                def body(parts):
                    if first:
                        for tt in (1, 0):
                            pe.wait_ge(mm_free[tt], MMM[tt] + 1)
                            for c in range(2):
                                for k in range(2):
                                    last = products(mm[tt][:, c * W:(c + 1) * W], lhs, k, tt,
                                                    [q[:, k, c * W:(c + 1) * W] for q in parts], k == 0, False)
                        return last
                    for c in range(2):
                        for k in range(2):
                            for tt in range(TT):
                                last = products(mm[tt][:, c * W:(c + 1) * W], lhs, k, tt,
                                                [q[:, k, c * W:(c + 1) * W] for q in parts],
                                                False, final and k == 1)
                        if final and c == 0:
                            last.then_inc(S["half_done"], 1)
                    return last
                use_tile(t, sofar, body, D)

            gate_up(TM, TM, 0, AUXM[0] + 1, hT_part(6), lambda: x_transposes(job("R1"), 1, 8))
            gate_up(TM + 1, TM + 1, 1, None, hT_part(6), router_logits, 1)
            pe.wait_ge(mm_free[0], MMM[0])
            gate_up(TM + 2, TM + 2, 0, None, dst=mm[0])
            gate_up(TM + 3, TM + 3, 1, None, mid=lambda: expert_transposes(0, AUXM[1] + 1, AUXM[0] + 1), mid_k=1, dst=mm[0])
            down(TM + 4, TM + 4, 0, AUXM[1] + 1, first=True)
            with pe.Fori(0, (EXPERTS - 2) // 2) as it:
                for j in range(2):
                    n = TM + 5 + 3 * j
                    e = 2 + j
                    gate_up(n, it * 6 + n, 0, it * 2 + (AUXM[0] + e + 1))
                    expert_transposes((e - 1) % 2, it * 2 + (AUXM[1] + e), it * 2 + (AUXM[0] + e))
                    gate_up(n + 1, it * 6 + (n + 1), 1, None)
                    down(n + 2, it * 6 + (n + 2), (e - 1) % 2, it * 2 + (AUXM[1] + e))
            expert_transposes(1, AUXM[1] + EXPERTS, AUXM[0] + EXPERTS)
            down(TP - 1, TP - 1, 1, AUXM[1] + EXPERTS, final=True)

            pe.wait_ge(S["pT_lo_ready"], 1)

            def ple(parts):
                for c in range(2):
                    if c == 0:
                        dst = begin((0, AUXP[0] + 1))
                    else:
                        x_transposes((1, AUXP[1] + 1), 0, 9)
                        pe.wait_ge(mm_free[0], MMM[0] + 2)
                        dst = mm[0]
                    for k in range(2):
                        for tt in range(TT):
                            last = products(dst[:, tt * W:(tt + 1) * W], aT, 2 + k, tt,
                                            [q[:, k, c * W:(c + 1) * W] for q in parts], k == 0, k == 1)
                    if c == 0:
                        end((0, AUXP[0] + 1), last)
                return last
            use_tile(TP, TP, ple, D)
            x_transposes((0, AUXP[0] + 2), 1, 10)
            for c in range(2):
                group(group_tiles("w_pg_2", c * W, W, KT), TP + 1 + 2 * c, TP + 1 + 2 * c, hT,
                      (1, MMM[1] + 2) if c == 0 else (0, MMM[0] + 3), hT_part(7) if c == 0 else None)

        @block.scalar
        def _(act):
            act.sem_inc(hi_split, RING)
            load_rows(act, rows[:1], in_norm_w)
            load_rows(act, rows[1:4], in_rows)
            act.dma_start(pos_i[:].unsqueeze(2), A["positions"].rearrange("(t p one) -> p t one", p=P, one=1),
                          allow_slow_non_contiguous=True).then_inc(in_pos, 16)
            load_x(act, 1)
            chain = [0]

            def link(ins):
                chain[0] += 1
                ins.then_inc(S["act_chain"], 1)
                act.wait_ge(S["act_chain"], chain[0])

            def release(ins, free, value, event):
                ins.then_inc(free, 1)
                act.wait_ge(free, value + 1)
                act.sem_inc(event, 1)

            def hi(t, width, sofar, loads):
                act.wait_ge(raw_loaded[slot(t)], loads)
                act.wait_ge(tile_done, sofar + 1)
                act.activation(w_hi[:, slot(t), 0:width], raw[:, slot(t), 0:width], ACT.Copy).then_inc(hi_split, 1)

            def squares(h, halves):
                if halves is not None:
                    act.wait_ge(x_ready, halves)
                for tt in range(TT):
                    ins = act.activation(E[0][:, tt * W:(tt + 1) * W], x[:, tt, h * W:(h + 1) * W], ACT.Square,
                                         accum_out=st[:, 2 * h + tt:2 * h + tt + 1])
                link(ins)
                if h == 0:
                    link(act.activation(st[:, 4:6], st[:, 0:2], ACT.Identity, bias=one[:, 0:1], scale=1.0 / D))

            def root():
                for tt in range(TT):
                    ins = act.activation(st[:, 6 + tt:7 + tt], st[:, 2 + tt:3 + tt], ACT.Sqrt, bias=st[:, 4 + tt:5 + tt],
                                         scale=1.0 / D)
                ins.then_inc(std_ready, 1)

            def split_T(turn, h, gains, use):
                pair, value = turn
                act.wait_ge(aux_ready[pair], value)
                for k in range(4):
                    act.activation(hT_hi[:, 4 * h + k, :], aux[pair][:, k * 256:(k + 1) * 256], ACT.Copy,
                                   scale=gains[:, 4 * h + k:4 * h + k + 1]).then_inc(hT_hi_ready, 1)

            def exps(u, n, n_heads):
                act.wait_ge(S["S_ready"], n * 3 + (u + 1))
                w = 1024 // n_heads
                for i in range(n_heads):
                    src = s_ring[:, u % 2, i * w:(i + 1) * w]
                    ins = act.activation(src, src, ACT.Exp, bias=ast[:, 1, a_at(u) + i:a_at(u) + i + 1],
                                         accum_out=ast[:, 2, a_at(u) + i:a_at(u) + i + 1])
                ins.then_inc(S["p_ready"], 1)

            def copy_out(dst, turn, width, event, func=ACT.Copy, **kw):
                pair, value = turn
                act.wait_ge(aux_ready[pair], value)
                ins = act.activation(dst, aux[pair][:, 0:width], func, **kw)
                release(ins, aux_free[pair], value, event)

            def gains_of(name):
                return cols[:, COL_AT[name]:COL_AT[name] + KT]

            hi(0, 2048, 0, 32)
            act.wait_ge(S["gain_now"], 1)
            split_T((1, 1), 0, gain, 0)
            hi(1, 2048, 1, 32)
            act.wait_ge(in_x[0], 16)
            squares(0, None)
            act.wait_ge(S["lb_in"], 1)
            act.activation(hst[:, 0:8], hst[:, 8:16], ACT.Exp).then_inc(S["lb_exp"], 1)
            act.sem_clear(S["act_chain"])

            with act.Fori(0, 2) as L:
                def per(i):
                    return L * (32 * NT1 // RING) + 32 * (i // RING + 1)

                def layer_hi(i):
                    width = tile_width(B1_TILES[i]) if i < NT1 else 2048
                    hi(i, width, L * NT1 + i, per(i))

                chain[0] = 0
                layer_hi(2)
                squares(1, L * 2 + 2)
                split_T(AUX1.turn("N1", L), 1, gain, L * 2)
                root()

                def sigmoids():
                    act.wait_ge(S["layer_cols"], L + 1)
                    act.wait_ge(S["fT_ready"], L + 1)
                    link(act.activation(E[0], fT, ACT.Sigmoid))
                    act.activation(kTh[:], fT, ACT.Sigmoid, scale=-1.0).then_inc(S["sig_ready"], 1)
                    for h in range(4):
                        c = slice(h * 256, (h + 1) * 256)
                        ins = act.activation(logf[:, c], E[0][:, c], ACT.Ln, scale=lcols[:, 4 + h:5 + h],
                                             bias=lcols[:, h:h + 1])
                    ins.then_inc(S["log_ready"], 1)

                def mm_out(name, dst, event, func=ACT.Copy):
                    pair, value = MM1.turn(name, L)
                    act.wait_ge(S["r_ready"], L + 1)
                    act.wait_ge(tile_done, L * NT1 + (LAST1[name] + RING + 1))
                    for tt in range(TT):
                        ins = act.activation(dst[:, tt, :], mm[pair][:, tt * W:(tt + 1) * W], func, scale=r[:, tt:tt + 1])
                    release(ins, mm_free[pair], value, event)

                def qh_silu():
                    act.wait_ge(S["qh_scaled"], L + 1)
                    act.activation(qTh[:], qTh[:], ACT.Silu).then_inc(S["qTh_ready"], 1)

                def gate(n, half):
                    act.wait_ge(S["gate_in"], L * 4 + n)
                    act.activation(half, half, ACT.Sigmoid).then_inc(S["gate_ready"], 1)

                def level_exp(j):
                    act.wait_ge(S["D_ready"], L * 8 + j)
                    e = E[(j - 1) % 2]
                    act.activation(e, e, ACT.Exp).then_inc(S["E_ready"], 1)

                def kv_out():
                    pair, value = MM1.turn("kv", L)
                    act.wait_ge(S["qk_ready"], L + 1)
                    for tt in range(TT):
                        ins = act.activation(v_sb[:, tt, :], mm[pair][:, tt * W + P:tt * W + 2 * P], ACT.Copy,
                                             scale=r[:, tt:tt + 1])
                    ins.then_inc(S["v_ready"], 1)

                def sink_exp(u, n_heads):
                    act.wait_ge(S["sinkexp_in"], L * 3 + (u + 1))
                    a = a_at(u)
                    act.activation(ast[:, 4, a:a + n_heads], ast[:, 3, a:a + n_heads], ACT.Exp
                                   ).then_inc(S["sinkexp_ready"], 1)

                def hgrn_norm():
                    pair, value = AUX1.turn("OH", L)
                    act.wait_ge(aux_ready[pair], value)
                    act.activation(E[0], aux[pair][:, :], ACT.Square).then_inc(S["osq_ready"], 1)
                    act.wait_ge(S["oss_ready"], L + 1)
                    act.activation(hst[:, 8:16], hst[:, 0:8], ACT.Sqrt, bias=one[:, 0:1], scale=1.0 / P
                                   ).then_inc(S["ostd_ready"], 1)

                def b_split():
                    pair, value = AUX1.turn("BT", L)
                    act.wait_ge(aux_ready[pair], value)
                    act.activation(bT_hi[:, :, :].rearrange("p a b -> p (a b)"), aux[pair][:, :], ACT.Copy,
                                   scale=lcols[:, 8:9]).then_inc(S["bT_hi_ready"], 1)

                def a_split():
                    pair, value = AUX1.turn("AT", L)
                    act.wait_ge(aux_ready[pair], value)
                    act.activation(aT_hi[:, :, :].rearrange("p a b -> p (a b)"), aux[pair][:, :], ACT.Copy
                                   ).then_inc(S["aT_hi_ready"], 1)

                def T_out(dst, name, width, event, **kw):
                    copy_out(dst, AUX1.turn(name, L), width, event, **kw)

                steps = {
                    2: [sigmoids], 4: [qh_silu],
                    5: [lambda: level_exp(1)],
                    6: [lambda: mm_out("vh", vh, S["vh_ready"]),
                        lambda: level_exp(2)],
                    7: [lambda: level_exp(3)], 8: [lambda: level_exp(4)],
                    10: [kv_out, lambda: level_exp(5)],
                    11: [lambda: T_out(qTp[:], "QT", 1024, S["qT_ready"], scale=0.125),
                         lambda: T_out(kT[:], "KT", 256, S["kT_ready"])],
                    12: [lambda: mm_out("z", z, S["z_ready"], ACT.Silu), lambda: level_exp(6)],
                    13: [lambda: exps(0, L, 8), lambda: sink_exp(0, 8), lambda: exps(1, L, 4), lambda: sink_exp(1, 4)],
                    14: [lambda: T_out(pT[:], "P0", 1024, S["pT_ready"]), lambda: level_exp(7),
                         lambda: mm_out("g", g, S["g_ready"], ACT.Silu)],
                    15: [lambda: level_exp(8), lambda: exps(2, L, 4), lambda: sink_exp(2, 4)],
                    16: [lambda: T_out(pT[:], "P1", 1024, S["pT_ready"]),
                         lambda: gate(1, by_feature(ga, 0))],
                    17: [lambda: T_out(sc128[:], "L8", 512, S["sc128_ready"])],
                    18: [lambda: T_out(pT[:], "P2", 1024, S["pT_ready"]), hgrn_norm,
                         lambda: gate(2, by_feature(ga, 1))],
                    20: [b_split, lambda: gate(3, by_feature(gb, 0))],
                    21: [a_split],
                    22: [lambda: gate(4, by_feature(gb, 1))],
                    29: [lambda: act.wait_ge(S["gain_now"], L + 2), lambda: split_T(AUX1.turn("N0", L), 0, gain, L * 2 + 2),
                         lambda: squares(0, L * 2 + 3)],
                }
                for i in range(1, NT1):
                    layer_hi(i + 2)
                    if i == 9:
                        with act.If(L < 1):
                            act.wait_ge(S["rope_in"], 1)
                            act.activation(rope[:, :, :, :].rearrange("p a b c -> p (a b c)"),
                                           rope_t[:, 4:6, :, :].rearrange("p a b c -> p (a b c)"), ACT.Sin
                                           ).then_inc(S["rope_sin"], 1)
                    for f in steps.get(i, ()):
                        f()
                act.sem_clear(S["act_chain"])

            chain[0] = 0

            def hi2(t):
                hi(t, 2048, t, 32 * (t // RING + 1))

            hi2(T2 + 2)
            squares(1, 6)
            split_T(AUX2.turn("N1"), 1, gain, 4)
            root()
            act.wait_ge(in_small, 16 * 6)
            act.activation(wf_hi[:], wf[:], ACT.Copy).then_inc(S["wf_hi_ready"], 1)
            act.activation(wr_hi[:], wr[:], ACT.Copy).then_inc(S["wf_hi_ready"], 1)

            def second_root():
                act.wait_ge(S["x1_ready"], 1)
                for tt in range(TT):
                    ins = act.activation(E[tt], x[:, tt, :], ACT.Square, accum_out=st[:, tt:tt + 1])
                link(ins)
                act.activation(st[:, 6:8], st[:, 0:2], ACT.Sqrt, bias=one[:, 0:1], scale=1.0 / D).then_inc(std_ready, 1)

            def v_out():
                pair, value = MM2.turn("v")
                act.wait_ge(tile_done, LAST2["v"] + RING + 1)
                for tt in range(TT):
                    ins = act.activation(vh[:, tt, :], mm[pair][:, tt * W:(tt + 1) * W], ACT.Copy, scale=r[:, tt:tt + 1])
                release(ins, mm_free[pair], value, S["vh_ready"])

            def gate(n, half):
                act.wait_ge(S["gate_in"], 8 + n)
                act.activation(half, half, ACT.Sigmoid).then_inc(S["gate_ready"], 1)

            def forget_exp():
                act.wait_ge(S["lf_in"], 1)
                link(act.activation(lf[:, 1], lf[:, 1], ACT.Exp, scale=-1.0))
                act.activation(lf[:, 1], lf[:, 1], ACT.Ln, bias=one[:, 1:2]).then_inc(S["lf_exp"], 1)

            def head_norm(i, name):
                pair, value = MM2.turn(name)
                act.wait_ge(tile_done, LAST2[name] + RING + 1)
                act.wait_ge(S["r_ready"], 4)
                for tt in range(TT):
                    ins = act.activation(E[0][:, tt * W:(tt + 1) * W], mm[pair][:, tt * W:(tt + 1) * W], ACT.Square,
                                         scale=r[:, tt:tt + 1])
                ins.then_inc(S["qsq_ready"], 1)
                act.wait_ge(S["qss_ready"], i + 1)
                act.activation(st[:, 24:40], st[:, 8:24], ACT.Sqrt, bias=one[:, 0:1], scale=1.0 / 64
                               ).then_inc(S["qstd_ready"], 1)

            def T_out(dst, name, event, width=1024, **kw):
                copy_out(dst, AUX2.turn(name), width, event, **kw)

            def split_out(dst, name, width, event):
                pair, value = AUX2.turn(name)
                act.wait_ge(aux_ready[pair], value)
                act.activation(dst, aux[pair][:, 0:width], ACT.Copy).then_inc(event, 1)

            def y_split():
                act.wait_ge(S["y_ready"], 1)
                act.activation(bT_hi[:, :, :].rearrange("p a b -> p (a b)"), kTh[:], ACT.Copy).then_inc(S["bT_hi_ready"], 1)

            steps = {
                1: [second_root], 2: [lambda: head_norm(0, "q")], 3: [forget_exp],
                4: [lambda: head_norm(1, "k")],
                5: [lambda: T_out(qTp[:], "QT", S["qT_ready"], scale=one[:, 2:3])],
                6: [v_out,
                    lambda: T_out(kT2[:], "KT", S["kT_ready"], scale=cols[:, COL_AT["k_gain"]:COL_AT["k_gain"] + 1])],
                7: [lambda: exps(0, 2, 8)],
                8: [lambda: exps(1, 2, 4)],
                9: [lambda: T_out(pT[:], "P0", S["pT_ready"])], 10: [lambda: exps(2, 2, 4)],
                11: [lambda: T_out(pT[:], "P1", S["pT_ready"])],
                13: [lambda: T_out(pT[:], "P2", S["pT_ready"]), y_split],
                14: [lambda: gate(1, by_feature(ga, 0))],
                16: [lambda: gate(2, by_feature(ga, 1)),
                     lambda: split_out(aT_hi[:, :, :].rearrange("p a b -> p (a b)"), "AT", 1024, S["aT_hi_ready"])],
                18: [lambda: gate(3, by_feature(gb, 0))],
                20: [lambda: gate(4, by_feature(gb, 1))],
                24: [lambda: split_out(aT_hi[:, 2:4, :].rearrange("p a b -> p (a b)"), "PT", 512, S["aT_hi_ready"])],
                27: [lambda: split_T(AUX2.turn("R0"), 0, gains_of("ffn_norm"), 6), lambda: squares(0, 7)],
            }
            for i in range(1, NT2):
                hi2(T2 + i + 2)
                for f in steps.get(i, ()):
                    f()
            hi2(TM + 2)
            squares(1, 8)
            split_T(AUX2.turn("R1"), 1, gains_of("ffn_norm"), 6)
            root()
            hi2(TM + 3)
            act.wait_ge(S["r_ready"], 5)

            def silu(parity, turn, src=aux[0]):
                act.wait_ge(tile_done, turn)
                for tt in range(TT):
                    ins = act.activation(sil[:, parity, tt, :], src[:, tt * W:tt * W + 256], ACT.Silu, scale=r[:, tt:tt + 1])
                ins.then_inc(S["sil_ready"], 1)

            def eT_split(parity, turn):
                act.wait_ge(aux_ready[1], turn)
                dst = (bT_hi if parity else aT_hi)[:, 0:2, :].rearrange("p a b -> p (a b)")
                act.activation(dst, aux[1][:, 0:W], ACT.Copy).then_inc(S["eT_hi_ready"], 1)

            act.wait_ge(S["logit_ready"], 1)
            act.activation(moe[:, 3], moe[:, 2], ACT.Exp).then_inc(S["prob_ready"], 1)
            silu(0, TM + 1 + (RING + 1))
            hi2(TM + 4)
            eT_split(0, AUXM[1] + 1)
            hi2(TM + 5)
            silu(1, TM + 3 + (RING + 1), mm[0])
            hi2(TM + 6)
            with act.Fori(0, (EXPERTS - 2) // 2) as it:
                for j in range(2):
                    n = TM + 5 + 3 * j
                    e = 2 + j
                    for i in (2, 3, 4):
                        hi(n + i, 2048, it * 6 + (n + i), it * 64 + 32 * ((n + i) // RING + 1))
                        if i == 2:
                            eT_split((e - 1) % 2, it * 2 + (AUXM[1] + e))
                        if i == 3:
                            silu(e % 2, it * 6 + (n + 1 + RING + 1))
            eT_split(1, AUXM[1] + EXPERTS)
            hi2(TP + 1)
            squares(0, 9)
            hi2(TP + 2)

            def ple_out(c, src, free):
                act.activation(pl[:, :, c * W:(c + 1) * W], src[:, :].rearrange("p (t n) -> p t n", t=TT), ACT.Copy
                               ).then_inc(free, 1)

            act.wait_ge(aux_ready[0], AUXM[0] + 1)
            ple_out(0, aux[0], aux_free[0])
            split_T((1, AUXP[1] + 1), 0, gains_of("ple_norm"), 7)
            squares(1, 10)
            act.wait_ge(tile_done, TP + RING + 1)
            ple_out(1, mm[0], mm_free[0])
            split_T((0, AUXM[0] + 2), 1, gains_of("ple_norm"), 7)
            hi2(TP + 3)
            root()
            hi2(TP + 4)
            act.wait_ge(S["r_ready"], 6)
            for c in range(2):
                act.wait_ge(tile_done, TP + 2 * c + (RING + 3))
                for tt in range(TT):
                    act.activation(pg[:, tt, c * W:(c + 1) * W], mm[1 - c][:, tt * W:(tt + 1) * W], ACT.Sigmoid,
                                   scale=r[:, tt:tt + 1]).then_inc(S["pg_ready"], 1)

        @block.vector
        def _(dve):
            chain = [0]

            def link(ins):
                chain[0] += 1
                ins.then_inc(S["dve_chain"], 1)
                dve.wait_ge(S["dve_chain"], chain[0])

            def release(ins, free, value, event=None):
                ins.then_inc(free, 1)
                dve.wait_ge(free, value + 1)
                if event is not None:
                    dve.sem_inc(event, 1)

            def tt_(out_, a, b, op):
                return dve.tensor_tensor(out_, a, b, op)

            def ts_(out_, a, s1, op0, s2=None, op1=None):
                if op1 is None:
                    return dve.tensor_scalar(out_, a, s1, None, op0)
                return dve.tensor_scalar(out_, a, s1, s2, op0, op1)

            def gains_of(name):
                return cols[:, COL_AT[name]:COL_AT[name] + KT]

            setup_count = [0]

            def hold(ins):
                setup_count[0] += 1
                ins.then_inc(S["setup_chain"], 1)
                dve.wait_ge(S["setup_chain"], setup_count[0])

            def rope_angles():
                inv_freq = [float(np.float32(np.power(np.float32(500000.0), np.float32(-i * (2.0 / 16))))) for i in range(8)]
                dve.wait_ge(in_pos, 16)
                hold(dve.tensor_copy(st[:, 56:58], pos_i[:]))
                for i in range(8):
                    ins = ts_(rope_t[:, 0, :, i], st[:, 56:58], inv_freq[i], ALU.mult)
                hold(ins)
                hold(ts_(rope_t[:, 1], rope_t[:, 0], 1.0 / (2 * np.pi), ALU.mult))
                hold(ts_(rope_t[:, 1], rope_t[:, 1], 12582912.0, ALU.add))
                hold(ts_(rope_t[:, 1], rope_t[:, 1], 12582912.0, ALU.subtract))
                part1 = 6.28125
                part2 = 2029.0 / 2 ** 20
                part3 = 2 * np.pi - part1 - part2
                for c in (part1, part2, part3):
                    hold(ts_(rope_t[:, 2], rope_t[:, 1], c, ALU.mult))
                    hold(tt_(rope_t[:, 0], rope_t[:, 0], rope_t[:, 2], ALU.subtract))
                hold(ts_(rope_t[:, 4], rope_t[:, 0], np.pi / 2, ALU.add))
                hold(ts_(rope_t[:, 3], rope_t[:, 4], float(np.pi), ALU.is_gt, 2 * np.pi, ALU.mult))
                hold(tt_(rope_t[:, 4], rope_t[:, 4], rope_t[:, 3], ALU.subtract))
                hold(dve.tensor_copy(rope_t[:, 5], rope_t[:, 0]))
                top = 3.1415925
                hold(ts_(rope_t[:, 4:6], rope_t[:, 4:6], top, ALU.min, -top, ALU.max))
                dve.sem_inc(S["rope_in"], 1)

            def level_masks(levels_):
                same, later = [blk[0], blk[1]], blk[3]
                for j in levels_:
                    if j == 0:
                        dve.wait_ge(S["iota_ready"], 2)
                        hold(tt_(same[0], iota_t, iota_s, ALU.is_equal))
                        hold(dve.tensor_copy(lmask[:, 0, :], same[0]))
                        hold(tt_(later, iota_t, iota_s, ALU.is_gt))
                        continue
                    dve.tensor_scalar(iota_t, iota_t, 1, None, ALU.logical_shift_right)
                    hold(dve.tensor_scalar(iota_s, iota_s, 1, None, ALU.logical_shift_right))
                    hold(tt_(same[j % 2], iota_t, iota_s, ALU.is_equal))
                    hold(tt_(blk[2], same[j % 2], same[1 - j % 2], ALU.subtract))
                    hold(tt_(lmask[:, j, :], blk[2], later, ALU.mult))

            link(dve.memset(one[:, 0:1], EPS))
            link(dve.memset(one[:, 1:2], 1.0))
            link(dve.memset(ones[:], 1.0))
            link(dve.memset(segment[:], 1.0))
            link(dve.memset(segment[:, :].rearrange("p (c n) -> p c n", n=64)[:, :, 0:1], 0.0))
            link(dve.memset(acc[:], 0.0))
            dve.wait_ge(S["setup_pe"], 1)
            link(dve.tensor_copy(gain[:], mm[1][:, 0:KT]))
            dve.sem_inc(S["gain_now"], 1)
            def compute_r(v):
                dve.wait_ge(std_ready, v + 1)
                link(dve.reciprocal(r[:], st[:, 6:8]))
                dve.sem_inc(S["r_ready"], 1)

            def make_diag():
                for tt in range(TT):
                    ins = ts_(diag[:, tt, :], ident[:], r[:, tt:tt + 1], ALU.mult)
                ins.then_inc(S["diag_ready"], 1)

            def take_rB(turn):
                pair, value = turn
                dve.wait_ge(aux_ready[pair], value)
                ins = dve.tensor_copy(rB[:], aux[pair][:, 0:TT * P])
                release(ins, aux_free[pair], value)

            def by_4(t):
                return t.rearrange("p (c t) -> p c t", c=4)

            rB4 = rB[:, :].unsqueeze(1).broadcast_to([P, 4, TT * P])

            def scaled(dst, turn, done, event):
                pair, value = turn
                dve.wait_ge(tile_done, done)
                ins = tt_(by_4(dst), by_4(mm[pair][:, :]), rB4, ALU.mult)
                release(ins, mm_free[pair], value, event)

            def rest_T(turn, h, gains, use):
                pair, value = turn
                dve.wait_ge(aux_ready[pair], value)
                for k in range(4):
                    kk = 4 * h + k
                    if k % 2 == 0:
                        dve.wait_ge(hT_hi_ready, use * KT + (kk + 2))
                    dve.scalar_tensor_tensor(out=hT_lo[:, kk, :], in0=aux[pair][:, k * 256:(k + 1) * 256],
                                             scalar=gains[:, kk:kk + 1], in1=hT_hi[:, kk, :].bitcast(F32),
                                             op0=ALU.mult, op1=ALU.subtract).then_inc(hT_lo_ready, 1)
                dve.wait_ge(hT_lo_ready, use * KT + (4 * h + 4))
                dve.sem_inc(aux_free[pair], 1)

            def mask_of(u, block2):
                if u == 0:
                    return amask[:, 1:2, :].broadcast_to([P, 8, P])
                m = amask[:, 2:4, :] if block2 else amask[:, 0:2, :]
                return m.rearrange("p a b -> p (a b)").unsqueeze(1).broadcast_to([P, 4, 256])

            def softmax_in(u, n, turn, sinks):
                nh = 8 if u == 0 else 4
                a = a_at(u)
                pair, value = turn
                dve.wait_ge(aux_ready[pair], value)
                if u == 2:
                    dve.wait_ge(S["pT_ready"], n * 3 + 1)
                dve.wait_ge(S["amask_ready"], 1)
                src = aux[pair][:, :].rearrange("p (h k) -> p h k", h=nh)
                dst = s_ring[:, u % 2, :].rearrange("p (h k) -> p h k", h=nh)
                ins = tt_(dst, src, mask_of(u, sinks is None), ALU.add)
                release(ins, aux_free[pair], value)
                link(dve.tensor_reduce(ast[:, 0, a:a + nh], dst, AX, ALU.max))
                if sinks is not None:
                    hs = sinks[:, 0:8] if u == 0 else sinks[:, 4 * (u - 1):4 * u]
                    link(tt_(ast[:, 0, a:a + nh], ast[:, 0, a:a + nh], hs, ALU.max))
                link(ts_(ast[:, 1, a:a + nh], ast[:, 0, a:a + nh], -1.0, ALU.mult))
                if sinks is not None:
                    link(tt_(ast[:, 3, a:a + nh], hs, ast[:, 1, a:a + nh], ALU.add))
                    dve.sem_inc(S["sinkexp_in"], 1)
                dve.sem_inc(S["S_ready"], 1)

            def softmax_out(u, n, turn, sinks, gate):
                nh = 8 if u == 0 else 4
                a = a_at(u)
                h0 = 0 if u == 0 else 4 * (u - 1)
                tt = 0 if u == 0 else 1
                dve.wait_ge(S["p_ready"], n * 3 + (u + 1))
                if sinks is not None:
                    dve.wait_ge(S["sinkexp_ready"], n * 3 + (u + 1))
                    link(tt_(ast[:, 2, a:a + nh], ast[:, 2, a:a + nh], ast[:, 4, a:a + nh], ALU.add))
                link(dve.reciprocal(ast[:, 0, a:a + nh], ast[:, 2, a:a + nh]))
                pair, value = turn
                dve.wait_ge(aux_ready[pair], value)
                dst = a_tok[:, tt, h0 * 64:(h0 + nh) * 64]
                ins = tt_(dst.rearrange("p (h d) -> p h d", h=nh),
                          aux[pair][:, 0:nh * 64].rearrange("p (h d) -> p h d", h=nh),
                          ast[:, 0, a:a + nh].unsqueeze(2).broadcast_to([P, nh, 64]), ALU.mult)
                release(ins, aux_free[pair], value)
                if gate is not None:
                    link(tt_(dst, dst, gate[:, tt, h0 * 64:(h0 + nh) * 64], ALU.mult))
                if u == 2:
                    dve.sem_inc(S["a_ready"], 1)

            def merge(turn, done, gate, c, other=None, use=None):
                pair, value = turn
                dve.wait_ge(tile_done, done)
                mine = by_feature(gate, c)
                ins = tt_(mine, mine, mm[pair][:, :], ALU.mult)
                release(ins, mm_free[pair], value)
                if other is not None:
                    link(tt_(mine, mine, by_feature(other, c), ALU.add))
                    dve.tensor_copy(by_feature(hT_hi, c), mine).then_inc(hT_hi_ready, 4)
                    dve.wait_ge(hT_hi_ready, use * KT + (4 * c + 4))
                    tt_(by_feature(hT_lo, c), mine, by_feature(hT_hi, c).bitcast(F32), ALU.subtract).then_inc(hT_lo_ready, 4)

            def add_x(turn, done, c, banks=mm, free=mm_free):
                pair, value = turn
                dve.wait_ge(tile_done, done)
                cs = slice(c * W, (c + 1) * W)
                ins = tt_(x[:, :, cs], x[:, :, cs], banks[pair][:, :].rearrange("p (t n) -> p t n", t=TT), ALU.add)
                release(ins, free[pair], value)

            rest_T((1, 1), 0, gain, 0)
            for h in range(2):
                dve.wait_ge(in_x[h], 16)
                dve.sem_inc(x_ready, 1)
            dve.wait_ge(S["setup_pe"], 2)
            link(dve.tensor_copy(cols[:], mm[1][:, W:W + N_COLS]))
            dve.sem_inc(S["cols_ready"], 1)
            a = COL_AT["norm_w"]
            for layer in range(2):
                dve.tensor_copy(gains_all[:, layer, :], cols[:, a + layer * KT:a + (layer + 1) * KT])
            tt_(gains_all[:, 2, :], cols[:, COL_AT["final_norm"]:COL_AT["final_norm"] + KT],
                cols[:, COL_AT["attn_norm"]:COL_AT["attn_norm"] + KT], ALU.mult)
            link(ts_(one[:, 2:3], cols[:, COL_AT["q_gain"]:COL_AT["q_gain"] + 1], 0.125, ALU.mult))
            lb0 = cols[:, COL_AT["lb"]:COL_AT["lb"] + 4]
            lb1 = cols[:, COL_AT["lb"] + 4:COL_AT["lb"] + 8]
            link(tt_(hst[:, 16:20], lb0, lb1, ALU.max))
            tt_(hst[:, 8:12], lb0, hst[:, 16:20], ALU.subtract)
            link(tt_(hst[:, 12:16], lb1, hst[:, 16:20], ALU.subtract))
            dve.sem_inc(S["lb_in"], 1)
            dve.wait_ge(S["lb_exp"], 1)
            link(tt_(hst[:, 16:20], hst[:, 0:4], hst[:, 4:8], ALU.add))
            link(dve.reciprocal(hst[:, 20:24], hst[:, 16:20]))
            tt_(hst[:, 0:4], hst[:, 0:4], hst[:, 20:24], ALU.mult)
            link(tt_(hst[:, 4:8], hst[:, 4:8], hst[:, 20:24], ALU.mult))
            link(tt_(hst[:, 8:12], hst[:, 0:4], hst[:, 4:8], ALU.add))
            for layer in range(2):
                dve.tensor_copy(lcols_all[:, layer, 8:9], cols[:, COL_AT["hgrn"] + layer:COL_AT["hgrn"] + layer + 1])
                src = hst[:, 0:4] if layer == 0 else hst[:, 8:12]
                link(tt_(lcols_all[:, layer, 0:4], src, hst[:, 0:4], ALU.subtract))
                link(ts_(lcols_all[:, layer, 4:8], lcols_all[:, layer, 0:4], -1.0, ALU.mult, 1.0, ALU.add))
            dve.wait_ge(in_sinks, 16)

            dve.sem_clear(S["dve_chain"])
            with dve.Fori(0, 2) as L:
                chain[0] = 0
                rest_T(AUX1.turn("N1", L), 1, gain, L * 2)
                compute_r(L)
                make_diag()
                link(dve.tensor_copy(lcols[:].unsqueeze(1), lcols_all[:, bass.ds(L, 1), :]))
                dve.sem_inc(S["layer_cols"], 1)
                sinks = lcols[:, LAYER_COLS - 8:LAYER_COLS]

                def by_feature_out(name, dst, event=None):
                    scaled(dst, MM1.turn(name, L), L * NT1 + (LAST1[name] + RING + 1), event)

                def f_clamp():
                    take_rB(AUX1.turn("RB", L))
                    by_feature_out("fh", fT)
                    link(ts_(fT, fT, GATE_FLOOR, ALU.max))
                    dve.sem_inc(S["fT_ready"], 1)

                def scan():
                    dve.wait_ge(S["sig_ready"], L + 1)
                    for h in range(4):
                        c = slice(h * 256, (h + 1) * 256)
                        ins = ts_(kTh[:, c], kTh[:, c], lcols[:, 4 + h:5 + h], ALU.mult)
                    ins.then_inc(S["kTh_ready"], 1)
                    dve.wait_ge(S["log_ready"], L + 1)
                    for h in range(4):
                        c = slice(h * 256, (h + 1) * 256)
                        ins = dve.tensor_tensor_scan(pre[:, c], segment[:], logf[:, c], 0.0, ALU.mult, ALU.add)
                    link(ins)

                def level_diffs(j):
                    m = 1 << (j - 1)
                    e = E[(j - 1) % 2]
                    if j < 8:
                        pv_ = pre[:, :].rearrange("p (n two m) -> p n two m", two=2, m=m)
                        ev = e.rearrange("p (n two m) -> p n two m", two=2, m=m)
                        nb = 1024 // (2 * m)
                        mid = pv_[:, :, 0, m - 1:m].broadcast_to([P, nb, m])
                        tt_(ev[:, :, 0, :], mid, pv_[:, :, 0, :], ALU.subtract)
                        if j < 7:
                            ins = tt_(ev[:, :, 1, :], pv_[:, :, 1, :], mid, ALU.subtract)
                        else:
                            ins = dve.tensor_copy(ev[:, :, 1, :], pv_[:, :, 1, :])
                    else:
                        pv_ = pre[:, :].rearrange("p (h c m) -> p h c m", h=4, c=4)
                        ev = e.rearrange("p (h c m) -> p h c m", h=4, c=4)

                        def ends(c):
                            return pv_[:, :, c, 63:64]
                        link(tt_(hst[:, 24:28].unsqueeze(2), ends(0), ends(1), ALU.add))
                        tt_(ev[:, :, 0, :], hst[:, 24:28].unsqueeze(2).broadcast_to([P, 4, 64]), pv_[:, :, 0, :], ALU.subtract)
                        tt_(ev[:, :, 1, :], ends(1).broadcast_to([P, 4, 64]), pv_[:, :, 1, :], ALU.subtract)
                        dve.tensor_copy(ev[:, :, 2, :], pv_[:, :, 2, :])
                        ins = tt_(ev[:, :, 3, :], ends(2).broadcast_to([P, 4, 64]), pv_[:, :, 3, :], ALU.add)
                    ins.then_inc(S["D_ready"], 1)

                def level_factors(j):
                    m = 1 << (j - 1)
                    e = E[(j - 1) % 2]
                    dve.wait_ge(S["E_ready"], L * 8 + j)
                    if j == 1:
                        dve.wait_ge(S["kTh_ready"], L + 1)
                        dve.wait_ge(S["qTh_ready"], L + 1)

                    def half(t, i):
                        return t.rearrange("p (n two m) -> p n two m", two=2, m=m)[:, :, i, :]
                    tt_(half(e, 0), half(e, 0), half(kTh[:, :], 0), ALU.mult)
                    tt_(half(e, 1), half(e, 1), half(qTh[:, :], 1), ALU.mult).then_inc(S["W_ready"], 1)

                def take_level(j):
                    pair, value = AUX1.turn(f"L{j}", L)
                    dve.wait_ge(aux_ready[pair], value)
                    dve.sem_inc(S["level_seen"], 1)
                    ins = dve.copy_predicated(acc[:, :].rearrange("p (i t) -> p i t", i=8),
                                              lmask[:, j:j + 1, :].broadcast_to([P, 8, P]),
                                              aux[pair][:, :].rearrange("p (i t) -> p i t", i=8))
                    release(ins, aux_free[pair], value, S["acc_ready"] if j == 7 else None)

                def levels(j):
                    level_diffs(j)
                    take_level(j - 1)
                    level_factors(j)

                def q_rope():
                    pair, value = MM1.turn("q", L)
                    dve.wait_ge(tile_done, L * NT1 + (LAST1["q"] + RING + 1))
                    for tt in range(TT):
                        for a in range(2):
                            ins = ts_(qk[:, tt, 0:8, :].rearrange("p (j g) d -> p g j d", g=2)[:, a],
                                      mm[pair][:, tt * W + a * 256:tt * W + (a + 1) * 256].rearrange("p (j d) -> p j d", j=4),
                                      r[:, tt:tt + 1], ALU.mult)
                    ins.then_inc(mm_free[pair], 1)

                def kv_rope():
                    pair, value = MM1.turn("kv", L)
                    dve.wait_ge(tile_done, L * NT1 + (LAST1["kv"] + RING + 1))
                    for tt in range(TT):
                        ins = ts_(qk[:, tt, 8:10, :].rearrange("p h d -> p (h d)"), mm[pair][:, tt * W:tt * W + P],
                                  r[:, tt:tt + 1], ALU.mult)
                    link(ins)
                    dve.wait_ge(S["rope_sin"], 1)
                    x1, x2 = qk[:, :, :, 0:8], qk[:, :, :, 8:16]
                    cos, sin = (rope[:, i, :, :].unsqueeze(2).broadcast_to([P, TT, 10, 8]) for i in range(2))
                    tt_(rt[:, 0], x1, cos, ALU.mult)
                    tt_(rt[:, 1], x2, sin, ALU.mult)
                    tt_(rt[:, 2], x2, cos, ALU.mult)
                    link(tt_(rt[:, 3], x1, sin, ALU.mult))
                    tt_(x1, rt[:, 0], rt[:, 1], ALU.subtract)
                    tt_(x2, rt[:, 2], rt[:, 3], ALU.add).then_inc(S["qk_ready"], 1)
                    dve.wait_ge(S["v_ready"], L + 1)
                    dve.sem_inc(mm_free[pair], 1)

                def hgrn_norm():
                    pair, value = AUX1.turn("OH", L)
                    dve.wait_ge(S["osq_ready"], L + 1)
                    link(dve.tensor_reduce(hst[:, 0:8], E[0].rearrange("p (a b) -> p a b", a=8), AX, ALU.add))
                    dve.sem_inc(S["oss_ready"], 1)
                    dve.wait_ge(S["ostd_ready"], L + 1)
                    link(dve.reciprocal(hst[:, 16:24], hst[:, 8:16]))
                    dve.wait_ge(aux_ready[pair], value)
                    ins = tt_(b_tok[:, :].rearrange("p (a b) -> p a b", a=8), aux[pair][:, :].rearrange("p (a b) -> p a b", a=8),
                              hst[:, 16:24].unsqueeze(2).broadcast_to([P, 8, P]), ALU.mult)
                    release(ins, aux_free[pair], value)
                    dve.wait_ge(S["g_ready"], L + 1)
                    tt_(b_tok[:], b_tok[:], g[:, :, :].rearrange("p a b -> p (a b)"), ALU.mult).then_inc(S["b_ready"], 1)

                def b_rest():
                    pair, value = AUX1.turn("BT", L)
                    dve.wait_ge(aux_ready[pair], value)
                    dve.wait_ge(S["bT_hi_ready"], L + 1)
                    ins = dve.scalar_tensor_tensor(out=bT_lo[:, :, :].rearrange("p a b -> p (a b)"), in0=aux[pair][:, :],
                                                   scalar=lcols[:, 8:9],
                                                   in1=bT_hi[:, :, :].rearrange("p a b -> p (a b)").bitcast(F32),
                                                   op0=ALU.mult, op1=ALU.subtract)
                    release(ins, aux_free[pair], value, S["bT_lo_ready"])

                def a_rest():
                    pair, value = AUX1.turn("AT", L)
                    dve.wait_ge(aux_ready[pair], value)
                    dve.wait_ge(S["aT_hi_ready"], L + 1)
                    ins = tt_(aT_lo[:, :, :].rearrange("p a b -> p (a b)"), aux[pair][:, :],
                              aT_hi[:, :, :].rearrange("p a b -> p (a b)").bitcast(F32), ALU.subtract)
                    release(ins, aux_free[pair], value, S["aT_lo_ready"])

                def wait_z():
                    dve.wait_ge(S["z_ready"], L + 1)

                def unit_in(u):
                    softmax_in(u, L, AUX1.turn(f"S{u}", L), sinks)

                def unit_out(u):
                    softmax_out(u, L, AUX1.turn(f"V{u}", L), sinks, z)

                def next_gain():
                    link(dve.tensor_copy(gain[:].unsqueeze(1), gains_all[:, bass.ds(L + 1, 1), :]))
                    dve.sem_inc(S["gain_now"], 1)

                def merged(name, gate, c, other=None):
                    merge(MM1.turn(name, L), L * NT1 + (LAST1[name] + RING + 1), gate, c, other, L * 2 + 1)

                steps = {
                    2: [f_clamp], 3: [scan], 4: [lambda: by_feature_out("qh", qTh[:], S["qh_scaled"])],
                    5: [lambda: levels(1)], 6: [lambda: levels(2)], 7: [lambda: levels(3)],
                    8: [q_rope, lambda: levels(4)], 10: [kv_rope, lambda: levels(5)],
                    12: [lambda: unit_in(0), lambda: levels(6)], 13: [wait_z, lambda: unit_in(1)],
                    14: [lambda: levels(7)],
                    15: [lambda: level_diffs(8), lambda: unit_out(0), lambda: unit_in(2)],
                    16: [lambda: take_level(7), lambda: level_factors(8),
                         lambda: by_feature_out("ga0", by_feature(ga, 0), S["gate_in"])],
                    17: [lambda: unit_out(1)],
                    18: [hgrn_norm, lambda: by_feature_out("ga1", by_feature(ga, 1), S["gate_in"])],
                    19: [lambda: unit_out(2)],
                    20: [b_rest, lambda: by_feature_out("gb0", by_feature(gb, 0), S["gate_in"])],
                    21: [a_rest], 22: [lambda: by_feature_out("gb1", by_feature(gb, 1), S["gate_in"])],
                    23: [lambda: dve.wait_ge(S["gate_ready"], L * 4 + 4), lambda: merged("a0", ga, 0)],
                    24: [lambda: merged("a1", ga, 1)],
                    25: [lambda: merged("b0", gb, 0, ga)], 26: [lambda: merged("b1", gb, 1, ga)],
                    28: [lambda: add_x(AUX1.turn("O0", L), L * NT1 + (LAST1["o0"] + RING + 1), 0, aux, aux_free),
                         lambda: dve.sem_inc(x_ready, 1), next_gain],
                    29: [lambda: rest_T(AUX1.turn("N0", L), 0, gain, L * 2 + 2)],
                    30: [lambda: add_x(MM1.turn("o1", L), L * NT1 + (LAST1["o1"] + RING + 1), 1),
                         lambda: dve.sem_inc(x_ready, 1)],
                }
                masks_at = {2: (0, 1), 4: (2, 3), 5: (4,), 6: (5,), 7: (6,), 8: (7,)}
                for i in range(1, NT1 + 1):
                    for f in steps.get(i, ()):
                        f()
                    if i == 1:
                        with dve.If(L < 1):
                            rope_angles()
                    if i in masks_at:
                        with dve.If(L < 1):
                            level_masks(masks_at[i])
                dve.sem_clear(S["dve_chain"])

            chain[0] = 0
            rest_T(AUX2.turn("N1"), 1, gain, 4)
            compute_r(2)
            dve.wait_ge(in_fw, 16)
            for tt in range(TT):
                ins = dve.scalar_tensor_tensor(out=x[:, tt, :], in0=x[:, tt, :], scalar=r[:, tt:tt + 1], in1=fw,
                                               op0=ALU.mult, op1=ALU.mult)
            link(ins)
            dve.sem_inc(S["x1_ready"], 1)
            for part, (w, hi_, lo_) in enumerate(((wf, wf_hi, wf_lo), (wr, wr_hi, wr_lo))):
                dve.wait_ge(S["wf_hi_ready"], part + 1)
                tt_(lo_[:], w[:], hi_[:].bitcast(F32), ALU.subtract).then_inc(S["wf_lo_ready"], 1)

            def second_r():
                dve.wait_ge(std_ready, 4)
                link(dve.reciprocal(st[:, 58:60], st[:, 6:8]))
                link(tt_(r[:], r[:], st[:, 58:60], ALU.mult))
                dve.sem_inc(S["r_ready"], 1)
                make_diag()

            def by_feature_out(name, dst, event=None):
                scaled(dst, MM2.turn(name), LAST2[name] + RING + 1, event)

            def forget_gate():
                pair, value = AUX2.turn("FL")
                dve.wait_ge(aux_ready[pair], value)
                dve.wait_ge(in_small, 16 * 6)
                for tt in range(TT):
                    ins = dve.scalar_tensor_tensor(out=lf[:, 0, tt, :], in0=aux[pair][:, tt * W:tt * W + 8],
                                                   scalar=r[:, tt:tt + 1], in1=bias[:, 0:8], op0=ALU.mult, op1=ALU.add)
                release(ins, aux_free[pair], value)
                link(ts_(lf[:, 2], lf[:, 0], -1.0, ALU.mult))
                tt_(lf[:, 1], lf[:, 0], lf[:, 2], ALU.max).then_inc(S["lf_in"], 1)
                link(dve.memset(lfw, 0.0))
                link(ts_(lf[:, 0], lf[:, 0], 0.0, ALU.min))
                dve.wait_ge(S["lf_exp"], 1)
                for c in (0, 64):
                    ins = tt_(lfw[:, :, c:c + 8], lf[:, 0], lf[:, 1], ALU.subtract)
                ins.then_inc(S["lf_ready"], 1)

            def take_cT():
                pair, value = AUX2.turn("CT")
                dve.wait_ge(aux_ready[pair], value)
                ins = dve.tensor_copy(cT[:], aux[pair][:, 0:256])
                release(ins, aux_free[pair], value, S["cT_ready"])

            def head_norm(i, name, dst):
                pair, value = MM2.turn(name)
                dve.wait_ge(S["qsq_ready"], i + 1)
                link(dve.tensor_reduce(st[:, 8:24], E[0].rearrange("p (a b) -> p a b", b=64), AX, ALU.add))
                dve.sem_inc(S["qss_ready"], 1)
                dve.wait_ge(S["qstd_ready"], i + 1)
                link(dve.reciprocal(st[:, 40:56], st[:, 24:40]))
                for tt in range(TT):
                    c = slice(40 + 8 * tt, 48 + 8 * tt)
                    ins = ts_(st[:, c], st[:, c], r[:, tt:tt + 1], ALU.mult)
                link(ins)
                for tt in range(TT):
                    for a in range(2):
                        c = tt * W + a * 256
                        ins = tt_(dst[:, tt * W:(tt + 1) * W].rearrange("p (j g d) -> p g j d", g=2, d=64)[:, a],
                                  mm[pair][:, c:c + 256].rearrange("p (j d) -> p j d", d=64),
                                  st[:, 40 + 8 * tt + 4 * a:44 + 8 * tt + 4 * a].unsqueeze(2).broadcast_to([P, 4, 64]), ALU.mult)
                release(ins, mm_free[pair], value, S["q2_ready"])

            def make_u():
                pair, value = MM2.turn("cu")
                dve.memset(uT[:, :, 0:2], 0.0)
                dve.wait_ge(tile_done, LAST2["cu"] + RING + 1)
                u = uT[:, :, 2:258]
                ins = tt_(u, by_4(E[1]), by_4(mm[pair][:, :]), ALU.mult)
                release(ins, mm_free[pair], value)
                link(tt_(u, u, rB4, ALU.mult))

            def conv():
                y = kTh[:, :].rearrange("p (c t) -> p c t", c=4)
                for j in range(3):
                    for c in range(4):
                        k = COL_AT["conv"] + 4 * j + c
                        if j == 0:
                            ins = ts_(y[:, c], uT[:, c, 0:256], cols[:, k:k + 1], ALU.mult)
                        else:
                            ins = dve.scalar_tensor_tensor(out=y[:, c], in0=uT[:, c, j:j + 256], scalar=cols[:, k:k + 1],
                                                           in1=y[:, c], op0=ALU.mult, op1=ALU.add)
                    link(ins)

            def conv_gate():
                pair, value = MM2.turn("cb")
                dve.wait_ge(tile_done, LAST2["cb"] + RING + 1)
                ins = tt_(kTh[:], kTh[:], mm[pair][:, :], ALU.mult)
                release(ins, mm_free[pair], value)
                link(tt_(by_4(kTh[:, :]), by_4(kTh[:, :]), rB4, ALU.mult))
                dve.sem_inc(S["y_ready"], 1)
                dve.wait_ge(S["bT_hi_ready"], 3)
                tt_(bT_lo[:, :, :].rearrange("p a b -> p (a b)"), kTh[:],
                    bT_hi[:, :, :].rearrange("p a b -> p (a b)").bitcast(F32), ALU.subtract).then_inc(S["bT_lo_ready"], 1)

            def a_rest(lo_, hi_, name, width, n, event):
                pair, value = AUX2.turn(name)
                dve.wait_ge(aux_ready[pair], value)
                dve.wait_ge(S["aT_hi_ready"], n)
                ins = tt_(lo_.rearrange("p a b -> p (a b)"), aux[pair][:, 0:width],
                          hi_.rearrange("p a b -> p (a b)").bitcast(F32), ALU.subtract)
                release(ins, aux_free[pair], value, event)

            def unit_in(u):
                softmax_in(u, 2, AUX2.turn(f"S{u}"), None)

            def unit_out(u):
                softmax_out(u, 2, AUX2.turn(f"V{u}"), None, None)

            def merged(name, gate, c, other=None):
                merge(MM2.turn(name), LAST2[name] + RING + 1, gate, c, other, 5)

            steps = {
                1: [second_r], 2: [lambda: head_norm(0, "q", a_tok[:, :, :].rearrange("p a b -> p (a b)"))], 3: [forget_gate],
                4: [lambda: take_rB(AUX2.turn("RB")), lambda: head_norm(1, "k", k2[:, :])], 5: [take_cT],
                7: [lambda: unit_in(0)], 8: [lambda: unit_in(1), lambda: by_feature_out("cc", E[1])],
                10: [lambda: unit_out(0), lambda: unit_in(2), make_u],
                11: [conv], 12: [lambda: unit_out(1)], 13: [conv_gate],
                14: [lambda: unit_out(2), lambda: by_feature_out("ga0", by_feature(ga, 0), S["gate_in"])],
                16: [lambda: by_feature_out("ga1", by_feature(ga, 1), S["gate_in"]),
                     lambda: a_rest(aT_lo[:, :, :], aT_hi[:, :, :], "AT", 1024, 3, S["aT_lo_ready"])],
                18: [lambda: by_feature_out("gb0", by_feature(gb, 0), S["gate_in"])],
                20: [lambda: by_feature_out("gb1", by_feature(gb, 1), S["gate_in"])],
                21: [lambda: dve.wait_ge(S["gate_ready"], 12), lambda: merged("b0", gb, 0)],
                22: [lambda: merged("b1", gb, 1)], 23: [lambda: merged("a0", ga, 0, gb)],
                24: [lambda: merged("a1", ga, 1, gb),
                     lambda: a_rest(aT_lo[:, 2:4, :], aT_hi[:, 2:4, :], "PT", 512, 4, S["pT_lo_ready"])],
                26: [lambda: add_x(MM2.turn("o0"), LAST2["o0"] + RING + 1, 0), lambda: dve.sem_inc(x_ready, 1)],
                27: [lambda: rest_T(AUX2.turn("R0"), 0, gains_of("ffn_norm"), 6)],
                28: [lambda: add_x(MM2.turn("o1"), LAST2["o1"] + RING + 1, 1), lambda: dve.sem_inc(x_ready, 1)],
            }
            for i in range(1, NT2 + 1):
                for f in steps.get(i, ()):
                    f()

            rest_T(AUX2.turn("R1"), 1, gains_of("ffn_norm"), 6)
            order = moe[:, 1, :, 0:4]
            for j in range(4):
                link(dve.memset(order[:, :, j:j + 1], 4.0 - j))
            compute_r(4)
            pair, value = RL
            dve.wait_ge(aux_ready[pair], value)
            logits = moe[:, 0]
            for tt in range(TT):
                ins = dve.scalar_tensor_tensor(out=logits[:, tt, :], in0=aux[pair][:, tt * W:tt * W + 20],
                                               scalar=r[:, tt:tt + 1], in1=bias[:, 8:28], op0=ALU.mult, op1=ALU.add)
            release(ins, aux_free[pair], value)

            def top1(values, mx, onehot, scratch):
                link(dve.tensor_reduce(mx, values, AX, ALU.max))
                link(tt_(scratch, values, mx.unsqueeze(2).broadcast_to([P, TT, 4]), ALU.is_equal))
                link(tt_(scratch, scratch, order, ALU.mult))
                link(dve.tensor_reduce(mx2, scratch, AX, ALU.max))
                link(tt_(onehot, scratch, mx2.unsqueeze(2).broadcast_to([P, TT, 4]), ALU.is_equal))

            gl = logits[:, :, 0:4]
            el = logits[:, :, 4:20]
            gmax = moe[:, 4, :, 0]
            mx2 = moe[:, 4, :, 1]
            emax = moe[:, 4, :, 2]
            ghot = moe[:, 5, :, 0:4]
            scr = moe[:, 5, :, 4:8]
            top1(gl, gmax, ghot, scr)
            link(tt_(moe[:, 6, :, 0:16].rearrange("p t (g e) -> p t g e", g=4)[:, 0],
                     el[:, 0].rearrange("p (g e) -> p g e", g=4), ghot[:, 0].unsqueeze(2).broadcast_to([P, 4, 4]), ALU.mult))
            link(tt_(moe[:, 6, :, 0:16].rearrange("p t (g e) -> p t g e", g=4)[:, 1],
                     el[:, 1].rearrange("p (g e) -> p g e", g=4), ghot[:, 1].unsqueeze(2).broadcast_to([P, 4, 4]), ALU.mult))
            ein = moe[:, 7, :, 0:4]
            link(tt_(ein, moe[:, 6, :, 0:4], moe[:, 6, :, 4:8], ALU.add))
            link(tt_(ein, ein, moe[:, 6, :, 8:12], ALU.add))
            link(tt_(ein, ein, moe[:, 6, :, 12:16], ALU.add))
            hot1, hot2, left = moe[:, 7, :, 4:8], moe[:, 7, :, 8:12], moe[:, 7, :, 12:16]
            top1(ein, emax, hot1, scr)
            m2 = moe[:, 4, :, 3]
            link(ts_(left, hot1, -3e38, ALU.mult))
            link(tt_(left, left, ein, ALU.add))
            top1(left, m2, hot2, scr)
            link(dve.memset(moe[:, 2], 0.0))
            link(tt_(moe[:, 2, :, 0:4], gl, gmax.unsqueeze(2).broadcast_to([P, TT, 4]), ALU.subtract))
            link(tt_(moe[:, 2, :, 4:8], ein, emax.unsqueeze(2).broadcast_to([P, TT, 4]), ALU.subtract))
            dve.sem_inc(S["logit_ready"], 1)
            dve.wait_ge(S["prob_ready"], 1)
            gexp, eexp = moe[:, 3, :, 0:4], moe[:, 3, :, 4:8]
            sums = moe[:, 8, :, 0:2]
            link(dve.tensor_reduce(moe[:, 8, :, 0], gexp, AX, ALU.add))
            link(dve.tensor_reduce(moe[:, 8, :, 1], eexp, AX, ALU.add))
            link(dve.reciprocal(moe[:, 8, :, 2:4], sums))
            link(tt_(moe[:, 9, :, 0:4], gexp, ghot, ALU.mult))
            link(dve.tensor_reduce(moe[:, 8, :, 4], moe[:, 9, :, 0:4], AX, ALU.add))
            link(tt_(moe[:, 8, :, 4:5], moe[:, 8, :, 4:5], moe[:, 8, :, 2:3], ALU.mult))
            link(tt_(moe[:, 9, :, 0:4], eexp, moe[:, 8, :, 3:4].broadcast_to([P, TT, 4]), ALU.mult))
            link(tt_(hot1, hot1, hot2, ALU.add))
            link(tt_(moe[:, 9, :, 0:4], moe[:, 9, :, 0:4], hot1, ALU.mult))
            link(dve.tensor_reduce(moe[:, 8, :, 5], moe[:, 9, :, 0:4], AX, ALU.add))
            link(dve.reciprocal(moe[:, 8, :, 6:7], moe[:, 8, :, 5:6]))
            link(tt_(moe[:, 9, :, 0:4], moe[:, 9, :, 0:4], moe[:, 8, :, 6:7].broadcast_to([P, TT, 4]), ALU.mult))
            link(tt_(moe[:, 9, :, 0:4], moe[:, 9, :, 0:4], moe[:, 8, :, 4:5].broadcast_to([P, TT, 4]), ALU.mult))
            for tt in range(TT):
                link(tt_(combine[:, tt, :].rearrange("p (g e) -> p g e", g=4), ghot[:, tt].unsqueeze(2).broadcast_to([P, 4, 4]),
                         moe[:, 9, tt, 0:4].unsqueeze(1).broadcast_to([P, 4, 4]), ALU.mult))
                link(ts_(combine[:, tt, :], combine[:, tt, :], r[:, tt:tt + 1], ALU.mult))

            def hidden(parity, weight, done, src=aux[0]):
                dve.wait_ge(S["sil_ready"], done)
                for tt in range(TT):
                    ins = dve.scalar_tensor_tensor(out=hid[:, parity, tt, :], in0=src[:, tt * W + 256:(tt + 1) * W],
                                                   scalar=weight(tt), in1=sil[:, parity, tt, :], op0=ALU.mult, op1=ALU.mult)
                ins.then_inc(aux_free[0], 1)

            def eT_rest(parity, turn, done):
                dve.wait_ge(aux_ready[1], turn)
                dve.wait_ge(S["eT_hi_ready"], done)
                lo_, hi_ = (bT_lo, bT_hi) if parity else (aT_lo, aT_hi)
                ins = tt_(lo_[:, 0:2, :].rearrange("p a b -> p (a b)"), aux[1][:, 0:W],
                          hi_[:, 0:2, :].rearrange("p a b -> p (a b)").bitcast(F32), ALU.subtract)
                ins.then_inc(aux_free[1], 1)

            hidden(0, lambda tt: combine[:, tt, 0:1], 1)
            eT_rest(0, AUXM[1] + 1, 1)
            hidden(1, lambda tt: combine[:, tt, 1:2], 2, mm[0])
            dve.wait_ge(aux_free[0], AUXM[0] + 3)
            dve.sem_inc(mm_free[0], 1)
            dve.sem_clear(S["dve_chain"])
            with dve.Fori(0, (EXPERTS - 2) // 2) as it:
                chain[0] = 0
                dve.wait_ge(aux_free[0], it * 2 + (AUXM[0] + 3))
                link(dve.tensor_copy(cnow[:], combine[:, :, bass.ds(it * 2 + 2, 2)]))
                for j in range(2):
                    e = 2 + j
                    eT_rest((e - 1) % 2, it * 2 + (AUXM[1] + e), it * 2 + e)
                    hidden(e % 2, lambda tt: cnow[:, tt, j:j + 1], it * 2 + (e + 1))
                dve.sem_clear(S["dve_chain"])
            chain[0] = 0
            eT_rest(1, AUXM[1] + EXPERTS, EXPERTS)
            for h in range(2):
                if h == 0:
                    dve.wait_ge(S["half_done"], 1)
                else:
                    dve.wait_ge(tile_done, TP + RING)
                c = slice(h * W, (h + 1) * W)
                for tt in range(TT):
                    ins = tt_(x[:, tt, c], x[:, tt, c], mm[tt][:, c], ALU.add)
                    if h == 0:
                        link(ins)
                    else:
                        release(ins, mm_free[tt], MMM[tt] + 1)
                dve.sem_inc(x_ready, 1)

            rest_T((1, AUXP[1] + 1), 0, gains_of("ple_norm"), 7)
            rest_T((0, AUXM[0] + 2), 1, gains_of("ple_norm"), 7)
            compute_r(5)
            for c in range(2):
                for tt in range(TT):
                    dve.wait_ge(S["pg_ready"], 2 * c + tt + 1)
                    cs = slice(c * W, (c + 1) * W)
                    link(tt_(pg[:, tt, cs], pg[:, tt, cs], pl[:, tt, cs], ALU.mult))
                    tt_(x[:, tt, cs], x[:, tt, cs], pg[:, tt, cs], ALU.add).then_inc(S["final_ready"], 1)


def a_at(u):
    return (0, 8, 12)[u]


def kernel(**inputs):
    import concourse.bacc as _bacc
    from concourse.bass_utils import run_bass_kernel_spmd as _run

    nc = _bacc.Bacc("TRN2", target_bir_lowering=False, num_devices=1)
    arrays, A = {}, {}
    for name, value in inputs.items():
        a = np.ascontiguousarray(value)
        arrays[f"in_{name}"] = a
        ap = nc.dram_tensor(f"in_{name}", a.shape, mybir.dt.from_np(a.dtype), kind="ExternalInput").ap()
        if name in ("x", "positions") or name.endswith("_2"):
            ap = ap[0]
        A[name] = ap[0] if name == "p_2" else ap
    out = nc.dram_tensor("out", (1, TT * P, D), F32, kind="ExternalOutput").ap()
    build(nc, A, out[0])
    r = _run(nc, [arrays], core_ids=[0])
    return r.results[0]["out"]
```
